# Optimizing a Trainium2 kernel written in Bass

```python
import math
import jax
import jax.numpy as jnp
from jax import lax
import numpy as np

D_MODEL = 1024
BATCH = 1
SEQ = 512
DEPTH = 2

GRID_W = 64
CTX_LEN = 256
POOL_W = 256
POOL_WINDOWS = (2, 4, 8, 16)
POOL_GROUP = POOL_W // len(POOL_WINDOWS)
CONV_W = 256
CONV_K = 31
DIFF_W = 256
DIFF_HEADS = 4
DIFF_DH = DIFF_W // (2 * DIFF_HEADS)
NA_W = 256
NA_HEADS = 4
NA_DH = NA_W // NA_HEADS
NA_ROWS = 8
NA_COLS = 16
D_MIX = POOL_W + CONV_W + DIFF_W + NA_W
D_FF = 2816
N_MOD = 9
ROPE_BASE = 10000.0
EPS = 1e-6
LN_EPS = 1e-5
Q_BLOCK = 128
NEG_INF = -1e30
OFF_POOL = 0
OFF_CONV = OFF_POOL + POOL_W
OFF_DIFF = OFF_CONV + 2 * CONV_W
OFF_NA = OFF_DIFF + 3 * DIFF_W
D_IN = OFF_NA + 3 * NA_W

kernel_name = "hybrid_parallel_mixer_dit_block"

def rmsnorm(x, g):
    xf = x.astype(jnp.float32)
    y = xf * lax.rsqrt(jnp.mean(xf * xf, axis=-1, keepdims=True) + EPS)
    return (y * g.astype(jnp.float32)).astype(x.dtype)

def layernorm(x, g, b):
    xf = x.astype(jnp.float32)
    mu = jnp.mean(xf, axis=-1, keepdims=True)
    var = jnp.mean(jnp.square(xf - mu), axis=-1, keepdims=True)
    y = (xf - mu) * lax.rsqrt(var + LN_EPS)
    return (y * g.astype(jnp.float32) + b.astype(jnp.float32)).astype(x.dtype)

def modulate_in(x, g, shift, scale):
    return rmsnorm(x, g) * (1 + scale) + shift

def swiglu(y, w_in, w_out):
    a, gt = jnp.split(y @ w_in, 2, axis=-1)
    return (jax.nn.silu(a) * gt) @ w_out

def axial_rope(x, n):
    dh = x.shape[-1]
    half = dh // 2
    nf = half // 2
    inv = jnp.power(ROPE_BASE, -jnp.arange(nf, dtype=jnp.float32) / nf)
    t = jnp.arange(n)
    out = []
    for pos, seg in ((t // GRID_W, x[..., :half]), (t % GRID_W, x[..., half:])):
        ang = pos.astype(jnp.float32)[:, None] * inv[None, :]
        cos = jnp.cos(ang).astype(x.dtype)
        sin = jnp.sin(ang).astype(x.dtype)
        s1, s2 = seg[..., :nf], seg[..., nf:]
        out += [s1 * cos - s2 * sin, s2 * cos + s1 * sin]
    return jnp.concatenate(out, axis=-1)

def pool_mixer(u, pool_w, pool_scale):
    n = u.shape[1]
    uf = u.astype(jnp.float32)
    cs = jnp.concatenate([jnp.zeros_like(uf[:, :1]), jnp.cumsum(uf, axis=1)], axis=1)
    t = jnp.arange(n)
    outs = []
    for gi, w in enumerate(POOL_WINDOWS):
        sl = slice(gi * POOL_GROUP, (gi + 1) * POOL_GROUP)
        lo = jnp.clip(t - w // 2, 0, n)
        hi = jnp.clip(t + w - w // 2, 0, n)
        csg = cs[..., sl]
        mean = (csg[:, hi] - csg[:, lo]) / (hi - lo).astype(jnp.float32)[None, :, None]
        d = (mean - uf[..., sl]).astype(u.dtype)
        outs.append(d @ pool_w[gi])
    return jnp.concatenate(outs, axis=-1) * pool_scale

def conv_module(u, dw, dw_b, ln_g, ln_b, pw, pw_b):
    a, g = jnp.split(u, 2, axis=-1)
    h = a * jax.nn.sigmoid(g)
    h = lax.conv_general_dilated(h, dw[:, None, :].astype(h.dtype), window_strides=(1,),
                                 padding=[(CONV_K // 2, CONV_K // 2)],
                                 dimension_numbers=('NWC', 'WIO', 'NWC'),
                                 feature_group_count=CONV_W) + dw_b
    h = jax.nn.silu(layernorm(h, ln_g, ln_b))
    return h @ pw + pw_b

def diff_attend(q, k, v, lam):
    b, h2, nq, _ = q.shape
    s = jnp.einsum('bhqd,bhkd->bhqk', q, k).astype(jnp.float32)
    p = jax.nn.softmax(s, axis=-1).reshape(b, h2 // 2, 2, nq, k.shape[2])
    w = p[:, :, 0] - lam * p[:, :, 1]
    return jnp.einsum('bhqk,bhkd->bhqd', w.astype(v.dtype), v)

def diff_mixer(zl, zc, lam_params, subln_g, li, need_ctx):
    b, n, _ = zl.shape
    lam_init = 0.8 - 0.6 * math.exp(-0.3 * li)
    lp = lam_params.astype(jnp.float32)
    lam = jnp.exp(jnp.sum(lp[0] * lp[1])) - jnp.exp(jnp.sum(lp[2] * lp[3])) + lam_init
    scale = DIFF_DH ** -0.5

    def split(z):
        m = z.shape[1]
        q = z[..., :DIFF_W].reshape(b, m, 2 * DIFF_HEADS, DIFF_DH).transpose(0, 2, 1, 3)
        k = z[..., DIFF_W:2 * DIFF_W].reshape(b, m, 2 * DIFF_HEADS, DIFF_DH).transpose(0, 2, 1, 3)
        v = z[..., 2 * DIFF_W:].reshape(b, m, DIFF_HEADS, 2 * DIFF_DH).transpose(0, 2, 1, 3)
        return q, k, v

    ql, kl, vl = split(zl)
    qc, kc, vc = split(zc)
    ql = axial_rope(ql, n) * scale
    kl = axial_rope(kl, n)
    k_all = jnp.concatenate([kl, kc], axis=2)
    v_all = jnp.concatenate([vl, vc], axis=2)
    nb = n // Q_BLOCK
    qb = ql.reshape(b, 2 * DIFF_HEADS, nb, Q_BLOCK, DIFF_DH).transpose(2, 0, 1, 3, 4)
    ob = lax.map(lambda qi: diff_attend(qi, k_all, v_all, lam), qb)
    ol = ob.transpose(1, 2, 0, 3, 4).reshape(b, DIFF_HEADS, n, 2 * DIFF_DH)

    def post(o):
        o = rmsnorm(o, subln_g) * (1 - lam_init)
        return o.transpose(0, 2, 1, 3).reshape(b, o.shape[2], DIFF_W)

    out_l = post(ol)
    out_c = post(diff_attend(qc * scale, kc, vc, lam)) if need_ctx else None
    return out_l, out_c

def na_mixer(zl, zc, rpb, need_ctx):
    b, n, _ = zl.shape
    rows = n // GRID_W
    kr = min(NA_ROWS, rows)
    scale = NA_DH ** -0.5

    def split(z):
        m = z.shape[1]
        q, k, v = (z[..., i * NA_W:(i + 1) * NA_W].reshape(b, m, NA_HEADS, NA_DH).transpose(0, 2, 1, 3)
                   for i in range(3))
        return q * scale, k, v

    ql, kl, vl = split(zl)
    qc, kc, vc = split(zc)
    grid = lambda t: t.reshape(b, NA_HEADS, rows, GRID_W, NA_DH)
    r = jnp.arange(rows)
    r_idx = jnp.clip(r - kr // 2, 0, rows - kr)[:, None] + jnp.arange(kr)[None, :]
    kb = grid(kl)[:, :, r_idx]
    vb = grid(vl)[:, :, r_idx]
    col = jnp.arange(GRID_W)
    c0 = jnp.clip(col - NA_COLS // 2, 0, GRID_W - NA_COLS)
    c_valid = (col[None, :] >= c0[:, None]) & (col[None, :] < c0[:, None] + NA_COLS)
    dr = r_idx - r[:, None] + (NA_ROWS - 1)
    dc = jnp.clip(col[None, :] - col[:, None], 1 - NA_COLS, NA_COLS - 1) + (NA_COLS - 1)
    bias = rpb[:, dr[:, None, :, None], dc[None, :, None, :]].astype(jnp.float32)
    qg = grid(ql)
    s_loc = jnp.einsum('bhrqd,bhrjkd->bhrqjk', qg, kb).astype(jnp.float32) + bias[None]
    s_loc = jnp.where(c_valid[:, None, :], s_loc, NEG_INF)
    s_ctx = jnp.einsum('bhrqd,bhcd->bhrqc', qg, kc).astype(jnp.float32)
    n_loc = kr * GRID_W
    s = jnp.concatenate([s_loc.reshape(b, NA_HEADS, rows, GRID_W, n_loc), s_ctx], axis=-1)
    p = jax.nn.softmax(s, axis=-1)
    p_loc = p[..., :n_loc].reshape(b, NA_HEADS, rows, GRID_W, kr, GRID_W).astype(vl.dtype)
    p_ctx = p[..., n_loc:].astype(vl.dtype)
    o = jnp.einsum('bhrqjk,bhrjkd->bhrqd', p_loc, vb) + jnp.einsum('bhrqc,bhcd->bhrqd', p_ctx, vc)
    merge = lambda t: t.transpose(0, 2, 1, 3).reshape(b, t.shape[2], NA_W)
    out_l = merge(o.reshape(b, NA_HEADS, n, NA_DH))
    out_c = None
    if need_ctx:
        pc = jax.nn.softmax(jnp.einsum('bhqd,bhkd->bhqk', qc, kc).astype(jnp.float32), axis=-1)
        out_c = merge(jnp.einsum('bhqk,bhkd->bhqd', pc.astype(vc.dtype), vc))
    return out_l, out_c

def token_mixer(yl, yc, lp, li, need_ctx):
    zl = yl @ lp['w_in']
    zc = yc @ lp['w_in']
    conv_args = (lp['conv_dw'], lp['conv_dw_b'], lp['conv_ln_g'], lp['conv_ln_b'], lp['conv_pw'], lp['conv_pw_b'])
    pool_l = pool_mixer(zl[..., OFF_POOL:OFF_CONV], lp['pool_w'], lp['pool_scale'])
    conv_l = conv_module(zl[..., OFF_CONV:OFF_DIFF], *conv_args)
    diff_l, diff_c = diff_mixer(zl[..., OFF_DIFF:OFF_NA], zc[..., OFF_DIFF:OFF_NA],
                                lp['diff_lambda'], lp['diff_subln_g'], li, need_ctx)
    na_l, na_c = na_mixer(zl[..., OFF_NA:], zc[..., OFF_NA:], lp['na_rpb'], need_ctx)
    out_l = jnp.concatenate([pool_l, conv_l, diff_l, na_l], axis=-1) @ lp['w_out']
    out_c = None
    if need_ctx:
        pool_c = pool_mixer(zc[..., OFF_POOL:OFF_CONV], lp['pool_w'], lp['pool_scale'])
        conv_c = conv_module(zc[..., OFF_CONV:OFF_DIFF], *conv_args)
        out_c = jnp.concatenate([pool_c, conv_c, diff_c, na_c], axis=-1) @ lp['w_out']
    return out_l, out_c

def trunk_layer(xl, xc, c, c_ctx, lp, li, need_ctx):
    b = c.shape[0]
    ml_all = (jax.nn.silu(c) @ lp['w_mod'] + lp['b_mod']).reshape(b, 1, N_MOD, D_MODEL)
    ml = [ml_all[:, :, i] for i in range(N_MOD)]
    mc = (jax.nn.silu(c_ctx) @ lp['w_mod'] + lp['b_mod']).reshape(N_MOD, D_MODEL)
    g = lp['g_norm']
    f_in, f_out = lp['ffn_in'], lp['ffn_out']
    xl = xl + 0.5 * ml[2] * swiglu(modulate_in(xl, g[0], ml[0], ml[1]), f_in[0], f_out[0])
    xc = xc + 0.5 * mc[2] * swiglu(modulate_in(xc, g[0], mc[0], mc[1]), f_in[0], f_out[0])
    ol, oc = token_mixer(modulate_in(xl, g[1], ml[3], ml[4]), modulate_in(xc, g[1], mc[3], mc[4]), lp, li, need_ctx)
    xl = xl + ml[5] * ol
    xl = xl + 0.5 * ml[8] * swiglu(modulate_in(xl, g[2], ml[6], ml[7]), f_in[1], f_out[1])
    if need_ctx:
        xc = xc + mc[5] * oc
        xc = xc + 0.5 * mc[8] * swiglu(modulate_in(xc, g[2], mc[6], mc[7]), f_in[1], f_out[1])
    return xl, xc

def setup_inputs(seed: int = 0) -> dict:
    key = jax.random.key(seed)
    ks = jax.random.split(key, 23)
    nrm = lambda k, shape, s: jax.random.normal(k, shape, jnp.float32) * s
    L, D = DEPTH, D_MODEL
    return {
        'x': nrm(ks[0], (BATCH, SEQ, D), 1.0),
        'c': nrm(ks[1], (BATCH, D), 1.0),
        'ctx': nrm(ks[2], (BATCH, CTX_LEN, D), 1.0),
        'c_ctx': nrm(ks[3], (D,), 1.0),
        'w_mod': nrm(ks[4], (L, D, N_MOD * D), 0.5 * D ** -0.5),
        'b_mod': nrm(ks[5], (L, N_MOD * D), 0.02),
        'g_norm': 1.0 + nrm(ks[6], (L, 3, D), 0.1),
        'ffn_in': nrm(ks[7], (L, 2, D, 2 * D_FF), D ** -0.5),
        'ffn_out': nrm(ks[8], (L, 2, D_FF, D), D_FF ** -0.5),
        'w_in': nrm(ks[9], (L, D, D_IN), D ** -0.5),
        'w_out': nrm(ks[10], (L, D_MIX, D), D_MIX ** -0.5),
        'pool_w': nrm(ks[11], (L, len(POOL_WINDOWS), POOL_GROUP, POOL_GROUP), POOL_GROUP ** -0.5),
        'pool_scale': 1.0 + nrm(ks[12], (L, POOL_W), 0.1),
        'conv_dw': nrm(ks[13], (L, CONV_K, CONV_W), CONV_K ** -0.5),
        'conv_dw_b': nrm(ks[14], (L, CONV_W), 0.02),
        'conv_ln_g': 1.0 + nrm(ks[15], (L, CONV_W), 0.1),
        'conv_ln_b': nrm(ks[16], (L, CONV_W), 0.02),
        'conv_pw': nrm(ks[17], (L, CONV_W, CONV_W), CONV_W ** -0.5),
        'conv_pw_b': nrm(ks[18], (L, CONV_W), 0.02),
        'diff_lambda': nrm(ks[19], (L, 4, DIFF_DH), 0.1),
        'diff_subln_g': 1.0 + nrm(ks[20], (L, 2 * DIFF_DH), 0.1),
        'na_rpb': nrm(ks[21], (L, NA_HEADS, 2 * NA_ROWS - 1, 2 * NA_COLS - 1), 0.1),
        'g_final': 1.0 + nrm(ks[22], (D,), 0.1),
    }

def reference(x, c, ctx, c_ctx, w_mod, b_mod, g_norm, ffn_in, ffn_out, w_in, w_out, pool_w, pool_scale,
              conv_dw, conv_dw_b, conv_ln_g, conv_ln_b, conv_pw, conv_pw_b, diff_lambda, diff_subln_g,
              na_rpb, g_final):
    xl, xc = x, ctx
    for li in range(DEPTH):
        lp = {
            'w_mod': w_mod[li], 'b_mod': b_mod[li], 'g_norm': g_norm[li],
            'ffn_in': ffn_in[li], 'ffn_out': ffn_out[li], 'w_in': w_in[li], 'w_out': w_out[li],
            'pool_w': pool_w[li], 'pool_scale': pool_scale[li],
            'conv_dw': conv_dw[li], 'conv_dw_b': conv_dw_b[li], 'conv_ln_g': conv_ln_g[li],
            'conv_ln_b': conv_ln_b[li], 'conv_pw': conv_pw[li], 'conv_pw_b': conv_pw_b[li],
            'diff_lambda': diff_lambda[li], 'diff_subln_g': diff_subln_g[li], 'na_rpb': na_rpb[li],
        }
        xl, xc = trunk_layer(xl, xc, c, c_ctx, lp, li, li < DEPTH - 1)
    return rmsnorm(xl, g_final)


_drawn_inputs = setup_inputs


def setup_inputs(seed=0):
    import zlib

    import numpy as np

    out = dict(_drawn_inputs(seed))
    spreads = {}
    factors = {'pool_scale': 2.944,
     'conv_dw_b': 8.0,
     'conv_ln_g': 3.703,
     'conv_ln_b': 23.158,
     'conv_pw_b': 8.0,
     'diff_lambda': 5.851,
     'diff_subln_g': 3.66,
     'na_rpb': 45.157}
    for name, (base, spread) in spreads.items():
        noise = np.random.default_rng([zlib.crc32(name.encode()), seed]).standard_normal(out[name].shape)
        drawn = base * np.exp(spread * noise) if base else spread * noise
        out[name] = jnp.asarray(drawn.astype(out[name].dtype))
    for name, factor in factors.items():
        out[name] = (out[name] * factor).astype(out[name].dtype)
    return out
```

```python
import math

import numpy as np

import concourse.bass as bass
from concourse import mybir

F32 = mybir.dt.float32
F32R = mybir.dt.float32r
ALU = mybir.AluOpType
ACT = mybir.ActivationFunctionType
AX_X = mybir.AxisListType.X

P = 128
D = 1024
LAYERS = 2
LAT = 512
CTX = 256
TOK = LAT + CTX
DC = D // P
F = 2816
FC = F // P
FG = FC // 2
N_MOD = 9
GRID_W = 64
GRID_H = LAT // GRID_W
NA_COLS = 16
RPB_R = 15
RPB_C = 31
CONV_K = 31
HALO = CONV_K // 2
W = 256
WC = W // P
HEADS = 4
DH = 64
DIFF_DH = 32
EPS = 1e-6
LN_EPS = 1e-5
POOL_WINDOWS = (2, 4, 8, 16)
RPB_PAD = 64

CONV_A, CONV_G, POOL_U, DIFF_Q, DIFF_K, DIFF_V, NA_Q, NA_K, NA_V = range(0, 18, 2)
Z_UNITS = 18
Z_COLUMNS = [W, 2 * W, 0, 3 * W, 4 * W, 5 * W, 6 * W, 7 * W, 8 * W]

MOD_COLS = 256
MOD_BLOCKS = N_MOD * D // MOD_COLS
MOD_ALL = LAYERS * MOD_BLOCKS
MOD_STEPS = 2 * DC
MOD_FIRST = 2 * D // MOD_COLS

CONV_LEN = HALO + LAT + HALO + CTX + HALO
CONV_OUT = LAT + HALO + CTX
CONV_LAT = slice(0, LAT)
CONV_CTX = slice(LAT + HALO, CONV_OUT)
PPAD = 8
POOL_LEN = PPAD + LAT + PPAD + CTX + PPAD
POOL_LAT0 = PPAD
POOL_CTX0 = PPAD + LAT + PPAD


class Phase:

    def __init__(self, name, layer, half, group, pairs, kc, tokens, first):
        self.name, self.layer, self.half, self.group = name, layer, half, group
        self.pairs, self.kc, self.tokens, self.first = pairs, kc, tokens, first
        self.next_kc = 0


def plan_phases():
    out, unit = [], 0

    def add(name, layer, half, group, pairs, kc, tokens):
        nonlocal unit
        p = Phase(name, layer, half, group, pairs, kc, tokens, unit)
        if out:
            out[-1].next_kc = kc
        out.append(p)
        unit += 2 * pairs

    for layer in range(LAYERS):
        last = layer == LAYERS - 1
        for half in range(2):
            tokens = LAT if last and half == 1 else TOK
            for group in range(2):
                add("up", layer, half, group, FG, DC, tokens)
                add("down", layer, half, group, DC // 2, FG, tokens)
            if half == 0:
                add("mix_in", layer, half, 0, Z_UNITS // 2, DC, TOK)
                add("mix_out", layer, half, 0, DC // 2, DC, LAT if last else TOK)
    return out


PHASES = plan_phases()


def plan_mod_blocks():
    out, block = [], MOD_FIRST
    for p in PHASES:
        n = min(p.pairs, MOD_ALL - block) if p.name in ("up", "down") else 0
        out.append((block, n))
        block += n
    return out


MOD_PLAN = plan_mod_blocks()


def segments(pairs, mods):
    out = [(0, 1, mods > 0)]
    if mods >= pairs - 1:
        out.append((1, pairs - 1, True))
    elif mods > 1:
        out += [(1, mods, True), (mods, pairs - 1, False)]
    else:
        out.append((1, pairs - 1, False))
    return out + [(pairs - 1, pairs, mods >= pairs)]


def attention_steps(with_ctx):
    out = []
    for h in range(HEADS):
        tiles = [(t, False) for t in range(LAT // P)] + [(t, True) for t in range(CTX // P)] * with_ctx
        out += [("diff", h, (t,), c, n == len(tiles) - 1) for n, (t, c) in enumerate(tiles)]
    for h in range(HEADS):
        tiles = [((0, 1), False), ((2, 3), False)] + [((0, 1), True)] * with_ctx
        out += [("na", h, t, c, n == len(tiles) - 1) for n, (t, c) in enumerate(tiles)]
    return out


SEMAPHORES = [
    "inputs", "mixer_consts", "const_rows",
    "raw_loaded0", "raw_loaded1", "split_hi", "split_lo", "unit_done", "slot_free0", "slot_free1",
    "mod_raw", "mod_sum", "mod_vec", "cond_silu", "mod_step",
    "hidden_hi", "hidden_lo", "square", "sum_squares", "norm_sum", "norm_sqrt", "rstd",
    "normed", "affine", "y_hi", "y_lo", "scale_ready", "gates_ready",
    "rope_tables", "rope_step", "rope_done", "lam_in", "lam_exp", "lam_step", "lam_ready",
    "zeros", "conv_u", "conv_acc", "conv_mean", "conv_cent", "conv_sq", "conv_var", "conv_sqrt",
    "conv_rstd", "conv_norm", "conv_act", "conv_pw", "conv_out",
    "pool_step", "pool_tables", "pool_d", "pool_mm", "pool_out", "mixer_weights", "blocks_zero",
    "v_turned", "v_ready", "band_raw", "band_step", "band_ready",
    "scores", "neg_max", "exp", "stat", "probs", "turned", "probs_t", "pv", "head_out",
    "head_sq", "head_sum", "head_sqrt", "head_rstd", "head_norm", "final", "out_stored",
]


class Tally:

    def __init__(self, engine, sems):
        self.engine, self.sems, self.n = engine, sems, {}

    def wait(self, name, more=1):
        self.n[name] = self.n.get(name, 0) + more
        self.engine.wait_ge(self.sems[name], self.n[name])

    def skip(self, name, more=1):
        self.n[name] = self.n.get(name, 0) + more

    def again(self, name):
        if self.n.get(name, 0):
            self.engine.wait_ge(self.sems[name], self.n[name])


def trunk(nc, xT, cond, w_mod, b_mod, gains, g_final, w_up, w_down, w_in, w_out, pool_w, conv_pw,
          conv_vec, conv_taps, lam_in, subln, rpb, consts, rope, pool_inv, masks, out):
    sems = {name: nc.alloc_semaphore(name) for name in SEMAPHORES}

    cursor = [((nc.sbuf_base + 31) // 32) * 32]

    def place(name, shape, dtype=F32, at=None):
        size = 4 * int(np.prod(shape[1:]))
        at = (at + 31) // 32 * 32 if at is not None else None
        if at is None:
            at = cursor[0]
            cursor[0] = at + (size + 31) // 32 * 32
        return nc.alloc_sbuf_tensor_at(name, shape, dtype, offset=at)

    x = place("x", [P, DC, TOK])
    raw = [place(f"w_raw{s}", [P, FG, P]) for s in range(2)]
    w_hi = [place(f"w_hi{s}", [P, FG, P], F32R) for s in range(2)]
    w_lo = [place(f"w_lo{s}", [P, FG, P], F32R) for s in range(2)]
    at_mod = cursor[0]
    mod_raw = place("mod_raw", [P, DC, MOD_COLS])
    rope_t = place("rope_t", [P, 4, LAT], at=at_mod)
    mod_acc = place("mod_acc", [P, 2, MOD_COLS])
    mod_vec = place("mod_vec", [P, 2, LAYERS * N_MOD * DC])
    mod_bias = place("mod_bias", [P, 2, LAYERS * N_MOD * DC])
    gain = place("gain", [P, LAYERS * 3, DC])
    gain_f = place("gain_f", [P, DC])
    cvec = place("cvec", [P, 2, DC])
    cact = place("cact", [P, 2, DC])
    scale1 = place("scale1", [P, 2, DC])
    gates = place("gates", [P, 2, DC])
    eps_t = place("eps_t", [P, 2])
    ones = place("ones", [P, P])
    ident = place("ident", [P, P])
    pairsum = place("pairsum", [P, P])
    backward = place("backward", [P, P])
    mask = place("mask", [P, 2, GRID_W])
    cvecs = place("cvecs", [P, LAYERS, 5, WC])
    ctaps = place("ctaps", [P, LAYERS, WC, CONV_K])
    sub_g = place("sub_g", [P, LAYERS])
    lam_rows = place("lam_rows", [P, LAYERS, 4, DIFF_DH])
    lam = place("lam", [P, 8])
    nmax = place("nmax", [P, 4])
    esum = place("esum", [P, 4])
    rsum = place("rsum", [P, 4])
    nrsum = place("nrsum", [P, 4])
    act_buf = place("act_buf", [P, TOK])
    hid_buf = place("hid_buf", [P, TOK])
    sq = [place(f"sq{s}", [P, TOK]) for s in range(2)]
    rstd = place("rstd", [P, POOL_LEN])
    at_ssq = cursor[0]
    ssq = place("ssq", [P, TOK])
    pw_sb = place("pw_sb", [P, WC, W], at=at_ssq)
    pool_sb = place("pool_sb", [P, WC, P], at=at_ssq + 4 * WC * W)
    at_y = cursor[0]
    y_hi = place("y_hi", [P, DC, TOK], F32R)
    y_lo = place("y_lo", [P, DC, TOK], F32R)
    at_h = cursor[0]
    h_hi = place("h_hi", [P, FG, TOK], F32R)
    h_lo = place("h_lo", [P, FG, TOK], F32R)
    assert cursor[0] <= nc.sbuf_usable_end, cursor[0]
    v_sb = place("v_sb", [P, TOK // P, 2 * W], at=at_y)
    e_sb = place("e_sb", [P, 4, TOK], at=at_y + 4 * 3072)
    probs_t = place("probs_t", [P, 2, TOK // P, LAT], at=at_y + 8 * 3072)
    o_final = place("o_final", [P, DC, LAT], at=at_y)
    z = place("z", [P, Z_UNITS, TOK], at=at_h)
    conv_acc = [place(f"conv_acc{c}", [P, CONV_OUT], at=at_h + 4 * 2 * c * TOK) for c in range(WC)]
    ctx_probs = [place(f"ctx_probs{b}", [P, CTX // P, CTX], at=at_h + 4 * (1 + 2 * b) * TOK) for b in range(2)]
    at_free = at_h + 4 * Z_UNITS * TOK
    conv_u = place("conv_u", [P, WC, CONV_LEN], at=at_free)
    pool_a = place("pool_a", [P, POOL_LEN], at=at_free + 4 * WC * CONV_LEN)
    pool_b = rstd
    bands = [place(f"band{h}", [P, RPB_R - 1, GRID_W], at=at_free + h * 4 * (RPB_R - 1) * GRID_W) for h in range(3)]
    bands.append(place("band3", [P, RPB_R - 1, GRID_W], at=at_h + 4 * DIFF_Q * TOK))
    mixed = [z[:, POOL_U, :], z[:, POOL_U + 1, :], z[:, 0, :], z[:, 2, :],
             z[:, DIFF_V, :], z[:, DIFF_V + 1, :], z[:, NA_V, :], z[:, NA_V + 1, :]]

    ps = nc.alloc_psum_tensor("ps", [P, 8 * 512], F32)
    slot = [ps[:, 0:1024], ps[:, 1024:2048]]
    turn = ps[:, 2048:3072]
    outs = ps[:, 3072:4096]
    mod_ps = ps[:, 3072:3076].rearrange("p (t c) -> p t c", t=2)
    slot_free = ["slot_free0", "slot_free1"]
    raw_loaded = ["raw_loaded0", "raw_loaded1"]

    def spans(tokens):
        return ((0, LAT), (LAT, TOK)) if tokens == TOK else ((0, LAT),)

    def kinds(tokens):
        return tuple(enumerate(spans(tokens)))

    def mod_chunk(layer, i):
        return (layer * N_MOD + i) * DC

    def loop(engine, a, b):
        return engine.Fori(a, b)

    def lam_init(layer):
        return 0.8 - 0.6 * math.exp(-0.3 * layer)

    def y_count(layer, norm):
        return DC * (4 * layer + norm + 1)

    def unit_pairs(layer, name):
        return next(p.first // 2 for p in PHASES if p.layer == layer and p.name == name)

    def scores_before(layer):
        return sum(2 * len(attention_steps(n < LAYERS - 1)) for n in range(layer))

    def diff_scores(layer):
        return 2 * sum(s[0] == "diff" for s in attention_steps(layer < LAYERS - 1))

    def turned_before(layer):
        return sum(sum(len(s[2]) for s in attention_steps(n < LAYERS - 1)) for n in range(layer))

    with nc.Block() as block:

        @block.sync
        def _(sp):
            def load(dst, src, name="inputs"):
                sp.dma_start(dst, src).then_inc(sems[name], 16)

            load(cvec[:, :, :], cond)
            load(mod_bias[:, :, :], b_mod)
            load(x[:, :, :], xT)
            load(gain[:, :, :], gains)
            load(gain_f[:, :], g_final)
            load(ident[:, :], consts[0])
            load(pairsum[:, :], consts[1])
            load(backward[:, :], consts[2])
            load(mask[:, :, :], masks)
            load(cvecs[:, :, :, :], conv_vec)
            load(ctaps[:, :, :, :], conv_taps)
            load(sub_g[:, :], subln)
            load(lam_rows[:, :, :, :], lam_in.partition_broadcast(P))

            def source(p, i, s):
                if p.name == "up":
                    return w_up[p.layer, p.half, p.group * FG + i, s]
                if p.name == "down":
                    return w_down[p.layer, p.half, p.group, 2 * i + s]
                return (w_in if p.name == "mix_in" else w_out)[p.layer, 2 * i + s]

            def fetch(p, i, s, wait=True):
                if wait:
                    sp.wait_ge(sems["split_lo"], 2 * i + (p.first + s - 1))
                sp.dma_start(raw[s][:, 0:p.kc, :], source(p, i, s)).then_inc(sems[raw_loaded[s]], 16)

            for p in PHASES:
                if p is PHASES[0]:
                    for s in range(2):
                        fetch(p, 0, s, wait=False)
                start = 1 if p is PHASES[0] else 0
                with loop(sp, start, p.pairs) as i:
                    for s in range(2):
                        fetch(p, i, s)
            sp.wait_ge(sems["final"], DC)
            sp.dma_start(out, o_final[:, :, :]).then_inc(sems["out_stored"], 16)
            sp.wait_ge(sems["out_stored"], 16)

        @block.gpsimd
        def _(pool):
            t = Tally(pool, sems)
            pool.memset(ones[:, :], 1.0).then_inc(sems["const_rows"], 1)
            pool.memset(eps_t[:, 0:1], EPS).then_inc(sems["const_rows"], 1)
            pool.memset(eps_t[:, 1:2], LN_EPS).then_inc(sems["const_rows"], 1)

            def fetch_mod(b, wait=True):
                if wait:
                    pool.wait_ge(sems["mod_step"], MOD_STEPS * b)
                pool.dma_start(mod_raw[:, :, :], w_mod[b]).then_inc(sems["mod_raw"], 16)

            fetch_mod(0, wait=False)
            with loop(pool, 1, MOD_FIRST) as b:
                fetch_mod(b)

            def mixer(layer, mods_before):
                pool.wait_ge(sems["mod_step"], MOD_STEPS * mods_before)
                pool.dma_start(rope_t[:, :, :], rope).then_inc(sems["rope_tables"], 16)
                t.n["norm_sum"] = 1 + 3 * layer
                t.wait("norm_sum")
                pool.memset(pool_sb[:, :, :], 0.0).then_inc(sems["blocks_zero"], 1)
                t.wait("blocks_zero")
                for g in range(4):
                    a = DH * (g % 2)
                    pool.dma_start(pool_sb[a:a + DH, g // 2, a:a + DH], pool_w[layer, g]).then_inc(sems["mixer_weights"], 16)
                pool.dma_start(pw_sb[:, :, :], conv_pw[layer]).then_inc(sems["mixer_weights"], 16)
                pool.wait_ge(sems["y_lo"], y_count(layer, 1))
                for c, buf in enumerate((act_buf, hid_buf)):
                    pool.dma_start(buf[:, :], pool_inv[:, c, :]).then_inc(sems["pool_tables"], 16)
                t.wait("pool_tables", 32)

                def step(instruction):
                    instruction.then_inc(sems["pool_step"], 1)
                    t.wait("pool_step")

                for c, inv in enumerate((act_buf, hid_buf)):
                    pool.wait_ge(sems[slot_free[c]], unit_pairs(layer, "mix_in") + POOL_U // 2 + 1)
                    u = z[:, POOL_U + c, :]
                    step(pool.memset(pool_a[:, :], 0.0))
                    step(pool.memset(pool_b[:, :], 0.0))
                    step(pool.tensor_copy(pool_a[:, POOL_LAT0:POOL_LAT0 + LAT], u[:, 0:LAT]))
                    step(pool.tensor_copy(pool_a[:, POOL_CTX0:POOL_CTX0 + CTX], u[:, LAT:TOK]))
                    n = POOL_LEN
                    step(pool.tensor_tensor(pool_b[:, 1:n], pool_a[:, 0:n - 1], pool_a[:, 1:n], ALU.add))
                    if c == 0:
                        step(pool.tensor_tensor(pool_a[DH:P, 1:n - 1], pool_b[DH:P, 0:n - 2], pool_b[DH:P, 2:n], ALU.add))
                        halves = (pool_b, pool_a)
                    else:
                        step(pool.tensor_tensor(pool_a[:, 1:n - 1], pool_b[:, 0:n - 2], pool_b[:, 2:n], ALU.add))
                        step(pool.tensor_tensor(pool_b[:, 2:n - 2], pool_a[:, 0:n - 4], pool_a[:, 4:n], ALU.add))
                        step(pool.tensor_tensor(pool_a[DH:P, 4:n - 4], pool_b[DH:P, 0:n - 8], pool_b[DH:P, 8:n], ALU.add))
                        halves = (pool_b, pool_a)
                    for g, buf in enumerate(halves):
                        rows = slice(DH * g, DH * g + DH)
                        for a, b, at in ((0, LAT, POOL_LAT0), (LAT, TOK, POOL_CTX0)):
                            step(pool.tensor_tensor(inv[rows, a:b], buf[rows, at:at + b - a], inv[rows, a:b], ALU.mult))
                    pool.tensor_tensor(u, inv[:, :], u, ALU.subtract).then_inc(sems["pool_d"], 1)

                pool.wait_ge(sems["conv_acc"], (layer + 1) * WC * CONV_K)
                t.n["pool_d"] = WC * layer
                t.wait("pool_d", WC)
                for heads in (range(HEADS - 1), (HEADS - 1,)):
                    if HEADS - 1 in heads:
                        pool.wait_ge(sems["scores"], scores_before(layer) + diff_scores(layer))
                    for h in heads:
                        for s in range(2):
                            first = RPB_PAD + ((layer * HEADS + h) * RPB_R + 1 - s) * RPB_C + RPB_C // 2 - (GRID_W - 1)
                            src = bass.AP(rpb.tensor, first, [[1, GRID_W], [RPB_C, RPB_R - 1], [1, GRID_W]])
                            pool.dma_start(bands[h][GRID_W * s:GRID_W * s + GRID_W, :, :], src).then_inc(sems["band_raw"], 16)
                    t.wait("band_raw", 16 * 2 * len(heads))
                    for h in heads:
                        for row, op, name in ((0, ALU.mult, "band_step"), (1, ALU.add, "band_ready")):
                            m = mask[:, row:row + 1, :].to_broadcast([P, RPB_R - 1, GRID_W])
                            pool.tensor_tensor(bands[h][:, :, :], bands[h][:, :, :], m, op).then_inc(sems[name], 1)
                            if row == 0:
                                t.wait("band_step")

            for p, (b0, n) in zip(PHASES, MOD_PLAN):
                if p.name == "mix_in":
                    mixer(p.layer, b0)
                    pool.wait_ge(sems["rope_done"], p.layer + 1)
                if n:
                    with loop(pool, b0, b0 + n) as b:
                        fetch_mod(b)

        @block.scalar
        def _(act):
            t = Tally(act, sems)

            def split_hi(p, i, s, ahead):
                kc = ahead
                if not kc:
                    return
                act.wait_ge(sems["unit_done"], 2 * i + (p.first + s + 1))
                act.wait_ge(sems[raw_loaded[s]], 16 * i + 16 * (p.first // 2 + 2))
                act.activation(w_hi[s][:, 0:kc, :], raw[s][:, 0:kc, :], ACT.Copy).then_inc(sems["split_hi"], 1)

            def square(src, s, tokens, wait_buffer):
                if wait_buffer is not None:
                    act.wait_ge(sems["sum_squares"], wait_buffer)
                act.activation(sq[s][:, 0:tokens], src, ACT.Square).then_inc(sems["square"], 1)

            def norm_tail(tokens):
                t.wait("norm_sum")
                act.activation(rstd[:, 0:tokens], turn[:, 0:tokens], ACT.Sqrt, bias=eps_t[:, 0:1], scale=1.0 / D).then_inc(sems["norm_sqrt"], 1)

            def make_y(layer, norm, tokens):
                t.wait("scale_ready")
                shift = mod_chunk(layer, 3 * norm)
                for m in range(DC):
                    buf = (act_buf, hid_buf)[m % 2]
                    t.wait("normed")
                    if m >= 2:
                        act.wait_ge(sems["y_lo"], y_made[0] + m - 1)
                    for k, (a, b) in kinds(tokens):
                        act.activation(buf[:, a:b], sq[m % 2][:, a:b], ACT.Identity,
                                       bias=mod_vec[:, k, shift + m:shift + m + 1],
                                       scale=scale1[:, k, m:m + 1]).then_inc(sems["affine"], 1)
                    t.wait("affine", len(kinds(tokens)))
                    act.activation(y_hi[:, m, 0:tokens], buf[:, 0:tokens], ACT.Copy).then_inc(sems["y_hi"], 1)
                y_made[0] += DC

            y_made = [0]
            ssq_made = [0]
            hidden = [0]

            t.wait("inputs", 16 * 13)
            t.wait("const_rows", 3)
            act.activation(cact[:, :, :], cvec[:, :, :], ACT.Silu).then_inc(sems["cond_silu"], 1)
            for s in range(2):
                act.wait_ge(sems[raw_loaded[s]], 16)
                act.activation(w_hi[s][:, 0:DC, :], raw[s][:, 0:DC, :], ACT.Copy).then_inc(sems["split_hi"], 1)
            for m in range(DC):
                square(x[:, m, :], m % 2, TOK, m - 1 if m >= 2 else None)
            ssq_made[0] += DC
            norm_tail(TOK)
            make_y(0, 0, TOK)

            def up(p, mods):
                n = p.tokens
                h0 = hidden[0]
                pair0 = p.first // 2

                def body(i, ahead):
                    act.wait_ge(sems["unit_done"], 2 * i + (p.first + 1))
                    act.activation(act_buf[:, 0:n], slot[0][:, 0:n], ACT.Silu).then_inc(sems["slot_free0"], 1)
                    split_hi(p, i, 0, ahead)
                    split_hi(p, i, 1, ahead)
                    act.wait_ge(sems["slot_free1"], i + (pair0 + 1))
                    act.activation(h_hi[:, i, 0:n], hid_buf[:, 0:n], ACT.Copy).then_inc(sems["hidden_hi"], 1)

                act.wait_ge(sems["y_lo"], y_made[0])
                for a, b, _ in segments(p.pairs, mods):
                    if b - a == 1:
                        body(a, p.kc if b < p.pairs else p.next_kc)
                    else:
                        with loop(act, a, b) as i:
                            body(i, p.kc)
                hidden[0] += p.pairs

            def down(p, mods, squares):
                n = p.tokens
                pair0 = p.first // 2
                s0 = ssq_made[0]

                def body(i, ahead):
                    for s in range(2):
                        split_hi(p, i, s, ahead)
                        if squares:
                            act.wait_ge(sems[slot_free[s]], i + (pair0 + 1))
                            start = isinstance(i, int) and i == 0
                            square(x[:, 2 * i + s, 0:n], s, n, None if start else 2 * i + (s0 + s - 1))

                for a, b, _ in segments(p.pairs, mods):
                    if b - a == 1:
                        body(a, p.kc if b < p.pairs else p.next_kc)
                    else:
                        with loop(act, a, b) as i:
                            body(i, p.kc)
                if squares:
                    ssq_made[0] += DC

            def mix_in(p):
                def body(i, func, ahead):
                    for s in range(2):
                        act.wait_ge(sems["unit_done"], 2 * i + (p.first + s + 1))
                        act.activation(z[:, 2 * i + s, :], slot[s][:, 0:TOK], func).then_inc(sems[slot_free[s]], 1)
                        split_hi(p, i, s, ahead)

                body(0, ACT.Copy, p.kc)
                body(1, ACT.Sigmoid, p.kc)
                with loop(act, 2, p.pairs - 1) as i:
                    body(i, ACT.Copy, p.kc)
                body(p.pairs - 1, ACT.Copy, p.next_kc)

            def mixer(layer):
                with_ctx = layer < LAYERS - 1
                n = TOK if with_ctx else LAT
                t.wait("lam_in")
                act.activation(lam[:, 2:4], lam[:, 0:2], ACT.Exp).then_inc(sems["lam_exp"], 1)
                for k in range(TOK // P):
                    t.wait("v_turned")
                    act.activation(v_sb[:, k, :], turn[:, 512 * (k % 2):512 * (k % 2) + 512], ACT.Copy).then_inc(sems["v_ready"], 1)
                for c in range(WC):
                    t.wait("pool_mm")
                    act.activation(z[:, POOL_U + c, :], slot[c][:, 0:TOK], ACT.Identity,
                                   scale=cvecs[:, layer, 4, c:c + 1]).then_inc(sems["pool_out"], 1)
                for c in range(WC):
                    t.wait("conv_cent")
                    act.activation((act_buf, hid_buf)[c][:, :], sq[c][:, :], ACT.Square).then_inc(sems["conv_sq"], 1)
                t.wait("conv_var")
                act.activation(rstd[:, 0:TOK], outs[:, 0:TOK], ACT.Sqrt, bias=eps_t[:, 1:2], scale=1.0 / W).then_inc(sems["conv_sqrt"], 1)
                for c in range(WC):
                    t.wait("conv_norm")
                    act.activation(sq[c][:, :], sq[c][:, :], ACT.Silu, bias=cvecs[:, layer, 2, c:c + 1],
                                   scale=cvecs[:, layer, 1, c:c + 1]).then_inc(sems["conv_act"], 1)
                for c in range(WC):
                    t.wait("conv_pw")
                    act.activation(z[:, 2 * c, :], slot[c][:, 0:TOK], ACT.Identity,
                                   bias=cvecs[:, layer, 3, c:c + 1]).then_inc(sems["conv_out"], 1)

                steps = attention_steps(with_ctx)
                tiles0 = turned_before(layer)
                turned = [tiles0]
                step_tiles = []
                head = [0]
                out_due = norm_at = None

                def copy_out(c):
                    t.wait("pv", 2)
                    act.activation(mixed[c][:, 0:n], outs[:, 0:n], ACT.Copy).then_inc(sems["head_out"], 1)

                for k in range(len(steps) + 1):
                    if k < len(steps):
                        kind, h, tiles, ctx, _ = steps[k]
                        keys = slice(LAT, TOK) if ctx else slice(0, TOK)
                        for s in range(2):
                            t.wait("neg_max")
                            if k >= 2:
                                act.wait_ge(sems["turned"], step_tiles[k - 2])
                            e = (k % 2) * 2 + s
                            act.activation(e_sb[:, e, keys], slot[s][:, keys], ACT.Exp, bias=nmax[:, e:e + 1],
                                           accum_out=esum[:, e:e + 1]).then_inc(sems["exp"], 1)
                        step_tiles.append((step_tiles[-1] if step_tiles else tiles0) + len(tiles))
                    if k:
                        kind, h, tiles, ctx, last = steps[k - 1]
                        hn = head[0] % 2
                        for q in tiles:
                            t.wait("turned")
                            if head[0] >= 2 or layer:
                                act.wait_ge(sems["pv"], layer * 2 * HEADS + head[0] - 1)
                            if ctx:
                                act.activation(ctx_probs[hn][:, :, P * q:P * q + P],
                                               turn[:, 0:2 * P].rearrange("p (k q) -> p k q", q=P), ACT.Copy).then_inc(sems["probs_t"], 1)
                            else:
                                act.activation(probs_t[:, hn, :, P * q:P * q + P],
                                               turn[:, 0:TOK].rearrange("p (k q) -> p k q", q=P), ACT.Copy).then_inc(sems["probs_t"], 1)
                        if k == norm_at:
                            t.wait("head_sum")
                            act.activation(hid_buf[:, 0:n], turn[:, 0:n], ACT.Sqrt, bias=eps_t[:, 0:1], scale=1.0 / DH).then_inc(sems["head_sqrt"], 1)
                        if out_due is not None:
                            copy_out(out_due)
                            if out_due < 6:
                                t.wait("head_out")
                                act.activation(act_buf[:, 0:n], mixed[out_due][:, 0:n], ACT.Square).then_inc(sems["head_sq"], 1)
                                norm_at = k + 1
                            else:
                                t.skip("head_out")
                            out_due = None
                        if last:
                            head[0] += 1
                            if h % 2:
                                out_due = (4 if kind == "diff" else 6) + h // 2
                copy_out(out_due)
                t.wait("head_out")
                t.wait("head_norm", 2)
                t.wait("pool_out", WC)
                t.wait("conv_out", WC)
                for m in range(DC):
                    act.activation(y_hi[:, m, 0:n], mixed[m][:, 0:n], ACT.Copy).then_inc(sems["y_hi"], 1)
                y_made[0] += DC

            for p, (b0, mods) in zip(PHASES, MOD_PLAN):
                if p.name == "up":
                    up(p, mods)
                elif p.name == "down":
                    down(p, mods, squares=p.group == 1)
                    if p.group == 1:
                        norm_tail(p.tokens)
                        if p.half == 0:
                            make_y(p.layer, 1, TOK)
                        elif p.layer + 1 < LAYERS:
                            make_y(p.layer + 1, 0, TOK)
                elif p.name == "mix_in":
                    mix_in(p)
                    mixer(p.layer)
                else:
                    down(p, 0, squares=True)
                    norm_tail(p.tokens)
                    make_y(p.layer, 2, p.tokens)

        @block.vector
        def _(dve):
            t = Tally(dve, sems)
            y_made, ssq_made, hidden = [0], [0], [0]

            def split_lo(p, i, s, ahead):
                kc = ahead
                if not kc:
                    return
                dve.wait_ge(sems["split_hi"], 2 * i + (p.first + s + 3))
                dve.tensor_tensor(w_lo[s][:, 0:kc, :], raw[s][:, 0:kc, :], w_hi[s][:, 0:kc, :].bitcast(F32),
                                  ALU.subtract).then_inc(sems["split_lo"], 1)

            def mod_block(b, first=False):
                dve.wait_ge(sems["mod_raw"], 16 * b + 16)
                if not first:
                    dve.wait_ge(sems["mod_sum"], b)
                for k in range(DC):
                    for tok in range(2):
                        c = cact[:, tok, k:k + 1]
                        if k:
                            dve.wait_ge(sems["mod_step"], MOD_STEPS * b + (2 * k + tok - 1))
                        if k == 0:
                            ins = dve.tensor_scalar(mod_acc[:, tok, :], mod_raw[:, k, :], c, None, ALU.mult)
                        else:
                            ins = dve.scalar_tensor_tensor(mod_acc[:, tok, :], mod_raw[:, k, :], c, mod_acc[:, tok, :],
                                                           ALU.mult, ALU.add)
                        ins.then_inc(sems["mod_step"], 1)

            def mod_finish(b):
                dve.wait_ge(sems["mod_sum"], b + 1)
                dve.tensor_tensor(mod_vec[:, :, bass.ds(2 * b, 2)], mod_ps, mod_bias[:, :, bass.ds(2 * b, 2)],
                                  ALU.add).then_inc(sems["mod_vec"], 1)

            def add_squares(m_first, s, tokens, made):
                if m_first:
                    dve.tensor_copy(ssq[:, 0:tokens], sq[s][:, 0:tokens]).then_inc(sems["sum_squares"], 1)
                else:
                    dve.wait_ge(sems["sum_squares"], made)
                    dve.tensor_tensor(ssq[:, 0:tokens], ssq[:, 0:tokens], sq[s][:, 0:tokens], ALU.add).then_inc(sems["sum_squares"], 1)

            def norm_tail(tokens):
                t.wait("norm_sqrt")
                dve.reciprocal(rstd[:, 0:tokens], rstd[:, 0:tokens]).then_inc(sems["rstd"], 1)
                t.wait("rstd")

            def mods_ready(layer, i):
                dve.wait_ge(sems["mod_vec"], (mod_chunk(layer, i) + DC) // 2)

            def make_y(layer, norm, tokens):
                mods_ready(layer, 3 * norm + 1)
                a = mod_chunk(layer, 3 * norm + 1)
                for tok in range(2):
                    ins = dve.scalar_tensor_tensor(scale1[:, tok, :], mod_vec[:, tok, a:a + DC], 1.0,
                                                   gain[:, 3 * layer + norm, :], ALU.add, ALU.mult)
                ins.then_inc(sems["scale_ready"], 1)
                parts = len(kinds(tokens))
                for m in range(DC + 1):
                    if m < DC:
                        if m >= 2:
                            t.wait("affine", parts)
                        dve.tensor_tensor(sq[m % 2][:, 0:tokens], x[:, m, 0:tokens], rstd[:, 0:tokens], ALU.mult).then_inc(sems["normed"], 1)
                    if m:
                        t.wait("y_hi")
                        buf = (act_buf, hid_buf)[(m - 1) % 2]
                        dve.tensor_tensor(y_lo[:, m - 1, 0:tokens], buf[:, 0:tokens], y_hi[:, m - 1, 0:tokens].bitcast(F32),
                                          ALU.subtract).then_inc(sems["y_lo"], 1)
                t.skip("affine", 2 * parts)
                y_made[0] += DC

            def up(p, b0, mods):
                n = p.tokens
                pair0 = p.first // 2
                h0 = hidden[0]

                def body(i, ahead, with_mod):
                    if with_mod:
                        mod_block(b0 + i)
                    split_lo(p, i, 0, ahead)
                    dve.wait_ge(sems["unit_done"], 2 * i + (p.first + 2))
                    dve.wait_ge(sems["slot_free0"], i + (pair0 + 1))
                    if h0 or not isinstance(i, int) or i:
                        dve.wait_ge(sems["hidden_lo"], i + h0)
                    else:
                        dve.wait_ge(sems["y_lo"], y_made[0])
                    dve.tensor_tensor(hid_buf[:, 0:n], act_buf[:, 0:n], slot[1][:, 0:n], ALU.mult).then_inc(sems["slot_free1"], 1)
                    split_lo(p, i, 1, ahead)
                    dve.wait_ge(sems["hidden_hi"], i + (h0 + 1))
                    dve.tensor_tensor(h_lo[:, i, 0:n], hid_buf[:, 0:n], h_hi[:, i, 0:n].bitcast(F32), ALU.subtract).then_inc(sems["hidden_lo"], 1)
                    if with_mod:
                        mod_finish(b0 + i)

                for a, b, with_mod in segments(p.pairs, mods):
                    if b - a == 1:
                        body(a, p.kc if b < p.pairs else p.next_kc, with_mod)
                    else:
                        with loop(dve, a, b) as i:
                            body(i, p.kc, with_mod)
                hidden[0] += p.pairs

            def down(p, b0, mods, squares, gate):
                n = p.tokens
                s0 = ssq_made[0]
                mods_ready(p.layer, gate)
                a = mod_chunk(p.layer, gate)
                if p.group == 0:
                    dve.tensor_scalar(gates[:, :, :], mod_vec[:, :, a:a + DC], 1.0 if p.name == "mix_out" else 0.5, None,
                                      ALU.mult).then_inc(sems["gates_ready"], 1)
                    t.wait("gates_ready")

                def body(i, ahead, with_mod, first):
                    if with_mod:
                        mod_block(b0 + i)
                    for s in range(2):
                        dve.wait_ge(sems["unit_done"], 2 * i + (p.first + s + 1))
                        for k, (lo, hi) in kinds(n):
                            ins = dve.scalar_tensor_tensor(x[:, 2 * i + s, lo:hi], slot[s][:, lo:hi],
                                                           gates[:, k, bass.ds(2 * i + s, 1)], x[:, 2 * i + s, lo:hi],
                                                           ALU.mult, ALU.add)
                        ins.then_inc(sems[slot_free[s]], 1)
                        split_lo(p, i, s, ahead)
                        if squares:
                            dve.wait_ge(sems["square"], 2 * i + (s0 + s + 1))
                            add_squares(first and s == 0, s, n, 2 * i + (s0 + s))
                    if with_mod:
                        mod_finish(b0 + i)

                for lo_i, hi_i, with_mod in segments(p.pairs, mods):
                    if hi_i - lo_i == 1:
                        body(lo_i, p.kc if hi_i < p.pairs else p.next_kc, with_mod, lo_i == 0)
                    else:
                        with loop(dve, lo_i, hi_i) as i:
                            body(i, p.kc, with_mod, False)
                if squares:
                    ssq_made[0] += DC

            def mix_in(p):
                layer = p.layer
                t.n["zeros"] = layer
                taps = [0]

                def convolve(n):
                    for _ in range(n):
                        if taps[0] == WC * CONV_K:
                            return
                        k, c = divmod(taps[0], WC)
                        src = conv_u[:, c, k:k + CONV_OUT]
                        w = ctaps[:, layer, c, k:k + 1]
                        if k == 0:
                            ins = dve.tensor_scalar(conv_acc[c][:, :], src, w, cvecs[:, layer, 0, c:c + 1], ALU.mult, ALU.add)
                        else:
                            dve.wait_ge(sems["conv_acc"], layer * WC * CONV_K + taps[0] - 1)
                            ins = dve.scalar_tensor_tensor(conv_acc[c][:, :], src, w, conv_acc[c][:, :], ALU.mult, ALU.add)
                        ins.then_inc(sems["conv_acc"], 1)
                        taps[0] += 1

                def rope(chunk, table):
                    half = DIFF_DH // 4
                    part = z[:, chunk, 0:LAT]
                    dve.stream_shuffle(sq[0][:, 0:LAT], part, [d ^ half for d in range(DIFF_DH)]).then_inc(sems["rope_step"], 1)
                    dve.tensor_tensor(sq[1][:, 0:LAT], part, rope_t[:, table, :], ALU.mult).then_inc(sems["rope_step"], 1)
                    t.wait("rope_step", 2)
                    dve.tensor_tensor(sq[0][:, 0:LAT], sq[0][:, 0:LAT], rope_t[:, table + 1, :], ALU.mult).then_inc(sems["rope_step"], 1)
                    t.wait("rope_step")
                    dve.tensor_tensor(part, sq[1][:, 0:LAT], sq[0][:, 0:LAT], ALU.add).then_inc(sems["rope_step"], 1)
                    t.wait("rope_step")

                def copied(u):
                    dve.wait_ge(sems[slot_free[u % 2]], p.first // 2 + u // 2 + 1)

                dve.memset(conv_u[:, :, :], 0.0).then_inc(sems["zeros"], 1)
                t.wait("zeros")
                for u in range(Z_UNITS):
                    split_lo(p, u // 2, u % 2, p.kc if u < Z_UNITS - 2 else p.next_kc)
                    if u == 3:
                        copied(2)
                        copied(3)
                        for c in range(WC):
                            dve.tensor_tensor(conv_u[:, c, HALO:HALO + LAT], z[:, CONV_A + c, 0:LAT],
                                              z[:, CONV_G + c, 0:LAT], ALU.mult).then_inc(sems["conv_u"], 1)
                            dve.tensor_tensor(conv_u[:, c, 2 * HALO + LAT:2 * HALO + TOK], z[:, CONV_A + c, LAT:TOK],
                                              z[:, CONV_G + c, LAT:TOK], ALU.mult).then_inc(sems["conv_u"], 1)
                        t.wait("conv_u", 2 * WC)
                    if u >= 3:
                        convolve(6)
                    if u == 15:
                        t.wait("rope_tables", 16)
                        copied(DIFF_K)
                        copied(DIFF_K + 1)
                        for c in range(WC):
                            rope(DIFF_Q + c, 0)
                            dve.tensor_scalar(z[:, DIFF_Q + c, LAT:TOK], z[:, DIFF_Q + c, LAT:TOK], DIFF_DH ** -0.5, None,
                                              ALU.mult).then_inc(sems["rope_step"], 1)
                            t.wait("rope_step")
                    if u == 16:
                        for c in range(WC):
                            rope(DIFF_K + c, 2)
                    if u == 17:
                        copied(NA_Q)
                        copied(NA_Q + 1)
                        for c in range(WC):
                            ins = dve.tensor_scalar(z[:, NA_Q + c, :], z[:, NA_Q + c, :], DH ** -0.5, None, ALU.mult)
                        ins.then_inc(sems["rope_done"], 1)

            def mixer(layer):
                with_ctx = layer < LAYERS - 1
                n = TOK if with_ctx else LAT
                for k in range(2):
                    dve.tensor_tensor(sq[0][:, DIFF_DH * k:DIFF_DH * k + DIFF_DH], lam_rows[:, layer, 2 * k, :],
                                      lam_rows[:, layer, 2 * k + 1, :], ALU.mult).then_inc(sems["lam_step"], 1)
                t.wait("lam_step", 2)
                dve.tensor_reduce(lam[:, 0:2], sq[0][:, 0:2 * DIFF_DH].rearrange("p (a b) -> p a b", a=2), AX_X,
                                  ALU.add).then_inc(sems["lam_in"], 1)
                t.wait("lam_exp")
                dve.tensor_tensor(lam[:, 4:5], lam[:, 3:4], lam[:, 2:3], ALU.subtract).then_inc(sems["lam_step"], 1)
                t.wait("lam_step")
                dve.tensor_scalar(lam[:, 5:6], lam[:, 4:5], -lam_init(layer), None, ALU.add).then_inc(sems["lam_step"], 1)
                dve.tensor_scalar(lam[:, 6:7], sub_g[:, layer:layer + 1], 1.0 - lam_init(layer), None, ALU.mult).then_inc(sems["lam_step"], 1)
                t.wait("lam_step", 2)

                t.wait("conv_mean")
                for c in range(WC):
                    for (a, b), at in (((0, LAT), CONV_LAT), ((LAT, TOK), CONV_CTX)):
                        ins = dve.scalar_tensor_tensor(sq[c][:, a:b], outs[:, a:b], -1.0 / W, conv_acc[c][:, at], ALU.mult, ALU.add)
                    ins.then_inc(sems["conv_cent"], 1)
                t.wait("conv_sqrt")
                dve.reciprocal(rstd[:, 0:TOK], rstd[:, 0:TOK]).then_inc(sems["conv_rstd"], 1)
                t.wait("conv_rstd")
                for c in range(WC):
                    dve.tensor_tensor(sq[c][:, :], sq[c][:, :], rstd[:, 0:TOK], ALU.mult).then_inc(sems["conv_norm"], 1)

                steps = attention_steps(with_ctx)
                norm_due = norm_at = None
                for k in range(len(steps) + 1):
                    if k < len(steps):
                        kind, h, tiles, ctx, _ = steps[k]
                        keys = slice(LAT, TOK) if ctx else slice(0, TOK)
                        e0 = (k % 2) * 2
                        for s in range(2):
                            t.wait("scores")
                            dve.tensor_reduce(nmax[:, e0 + s:e0 + s + 1], slot[s][:, keys], AX_X, ALU.max,
                                              negate=True).then_inc(sems["neg_max"], 1)
                        t.wait("exp", 2)
                        dve.reciprocal(rsum[:, e0:e0 + 2], esum[:, e0:e0 + 2]).then_inc(sems["stat"], 1)
                        t.wait("stat")
                        if kind == "diff":
                            dve.tensor_scalar(nrsum[:, e0:e0 + 1], rsum[:, e0 + 1:e0 + 2], lam[:, 5:6], None, ALU.mult).then_inc(sems["stat"], 1)
                            t.wait("stat")
                            dve.tensor_scalar(e_sb[:, e0 + 1, keys], e_sb[:, e0 + 1, keys], nrsum[:, e0:e0 + 1], None, ALU.mult).then_inc(sems["stat"], 1)
                            t.wait("stat")
                            dve.scalar_tensor_tensor(e_sb[:, e0, keys], e_sb[:, e0, keys], rsum[:, e0:e0 + 1],
                                                     e_sb[:, e0 + 1, keys], ALU.mult, ALU.add).then_inc(sems["probs"], 1)
                        else:
                            for s in range(2):
                                ins = dve.tensor_scalar(e_sb[:, e0 + s, keys], e_sb[:, e0 + s, keys], rsum[:, e0 + s:e0 + s + 1], None, ALU.mult)
                            ins.then_inc(sems["probs"], 1)
                    if k:
                        kind, h, tiles, ctx, last = steps[k - 1]
                        if k == norm_at:
                            t.wait("head_sqrt")
                            dve.reciprocal(hid_buf[:, 0:n], hid_buf[:, 0:n]).then_inc(sems["head_rstd"], 1)
                            t.wait("head_rstd")
                            dve.scalar_tensor_tensor(mixed[norm_due][:, 0:n], mixed[norm_due][:, 0:n], lam[:, 6:7], hid_buf[:, 0:n],
                                                     ALU.mult, ALU.mult).then_inc(sems["head_norm"], 1)
                        if last and kind == "diff" and h % 2:
                            norm_due, norm_at = 4 + h // 2, k + 2
                for m in range(DC):
                    t.wait("y_hi")
                    dve.tensor_tensor(y_lo[:, m, 0:n], mixed[m][:, 0:n], y_hi[:, m, 0:n].bitcast(F32), ALU.subtract).then_inc(sems["y_lo"], 1)
                y_made[0] += DC

            dve.wait_ge(sems["inputs"], 16 * 13)
            t.wait("cond_silu")
            for s in range(2):
                dve.wait_ge(sems["split_hi"], s + 1)
                dve.tensor_tensor(w_lo[s][:, 0:DC, :], raw[s][:, 0:DC, :], w_hi[s][:, 0:DC, :].bitcast(F32), ALU.subtract).then_inc(sems["split_lo"], 1)
            for m in range(DC):
                dve.wait_ge(sems["square"], m + 1)
                add_squares(m == 0, m % 2, TOK, m)
            ssq_made[0] += DC
            mod_block(0, first=True)
            mod_finish(0)
            with loop(dve, 1, MOD_FIRST) as b:
                mod_block(b)
                mod_finish(b)
            norm_tail(TOK)
            make_y(0, 0, TOK)

            for p, (b0, mods) in zip(PHASES, MOD_PLAN):
                if p.name == "up":
                    up(p, b0, mods)
                elif p.name == "down":
                    down(p, b0, mods, squares=p.group == 1, gate=2 if p.half == 0 else 8)
                    if p.group == 1:
                        norm_tail(p.tokens)
                        if p.half == 0:
                            make_y(p.layer, 1, TOK)
                        elif p.layer + 1 < LAYERS:
                            make_y(p.layer + 1, 0, TOK)
                elif p.name == "mix_in":
                    mix_in(p)
                    mixer(p.layer)
                else:
                    down(p, 0, 0, squares=True, gate=5)
                    norm_tail(p.tokens)
                    make_y(p.layer, 2, p.tokens)
            for m in range(DC):
                dve.scalar_tensor_tensor(o_final[:, m, :], x[:, m, 0:LAT], gain_f[:, m:m + 1], rstd[:, 0:LAT],
                                         ALU.mult, ALU.mult).then_inc(sems["final"], 1)

        @block.tensor
        def _(pe):
            t = Tally(pe, sems)
            y_made, hidden, ssq_made = [0], [0], [0]

            def product(s, kc, rhs_hi, rhs_lo, tokens, before_chunk):
                for k in range(kc):
                    before_chunk(k)
                    for n, (w, r) in enumerate(((w_hi, rhs_hi), (w_lo, rhs_hi), (w_hi, rhs_lo))):
                        for a, b in spans(tokens):
                            mm = pe.matmul(slot[s][:, a:b], w[s][:, k, :], r[:, k, a:b],
                                           start=(k == 0 and n == 0), stop=(k == kc - 1 and n == 2))
                return mm

            def mod_reduce(b):
                pe.wait_ge(sems["mod_step"], MOD_STEPS * b + MOD_STEPS)
                for tok in range(2):
                    for c in range(MOD_COLS // P):
                        mm = pe.matmul(mod_ps[:, tok, c:c + 1], mod_acc[:, tok, P * c:P * c + P], ones[:, 0:1],
                                       start=True, stop=True)
                mm.then_inc(sems["mod_sum"], 1)

            def norm_reduce(tokens):
                pe.wait_ge(sems["sum_squares"], ssq_made[0])
                for a, b in spans(tokens):
                    mm = pe.matmul(turn[:, a:b], ones[:, :], ssq[:, a:b], start=True, stop=True)
                mm.then_inc(sems["norm_sum"], 1)

            def run(p, b0, mods, rhs_hi, rhs_lo, ready, made):
                pair0 = p.first // 2

                def body(i, first, with_mod):
                    for s in range(2):
                        pe.wait_ge(sems["split_lo"], 2 * i + (p.first + s + 1))
                        if pair0 or not first:
                            pe.wait_ge(sems[slot_free[s]], i + pair0)

                        def before(k):
                            if first and s == 0:
                                pe.wait_ge(sems[ready], made + k + 1)

                        mm = product(s, p.kc, rhs_hi, rhs_lo, p.tokens, before)
                        mm.then_inc(sems["unit_done"], 1)
                    if with_mod:
                        mod_reduce(b0 + i)

                for a, b, with_mod in segments(p.pairs, mods):
                    if b - a == 1:
                        body(a, a == 0, with_mod)
                    else:
                        with loop(pe, a, b) as i:
                            body(i, False, with_mod)

            def mixer(layer):
                with_ctx = layer < LAYERS - 1
                n = TOK if with_ctx else LAT
                pairs_done = unit_pairs(layer, "mix_in") + Z_UNITS // 2
                for s in range(2):
                    pe.wait_ge(sems[slot_free[s]], pairs_done)
                for k in range(TOK // P):
                    if k >= 2:
                        t.wait("v_ready")
                    for c in range(2 * WC):
                        src = z[:, (DIFF_V, DIFF_V + 1, NA_V, NA_V + 1)[c], P * k:P * k + P]
                        mm = pe.transpose(turn[:, 512 * (k % 2) + P * c:512 * (k % 2) + P * c + P], src, ident[:, :])
                    mm.then_inc(sems["v_turned"], 1)
                t.wait("v_ready", 2)
                t.wait("mixer_weights", 16 * 5)
                for c in range(WC):
                    t.wait("pool_d")
                    for a, b in spans(TOK):
                        mm = pe.matmul(slot[c][:, a:b], pool_sb[:, c, :], z[:, POOL_U + c, a:b], start=True, stop=True)
                    mm.then_inc(sems["pool_mm"], 1)
                pe.wait_ge(sems["conv_acc"], (layer + 1) * WC * CONV_K)
                for (a, b), at in (((0, LAT), CONV_LAT), ((LAT, TOK), CONV_CTX)):
                    for c in range(WC):
                        mm = pe.matmul(outs[:, a:b], ones[:, :], conv_acc[c][:, at], start=(c == 0), stop=(c == WC - 1))
                mm.then_inc(sems["conv_mean"], 1)
                t.wait("conv_sq", WC)
                for a, b in spans(TOK):
                    for c in range(WC):
                        mm = pe.matmul(outs[:, a:b], ones[:, :], (act_buf, hid_buf)[c][:, a:b], start=(c == 0), stop=(c == WC - 1))
                mm.then_inc(sems["conv_var"], 1)
                t.wait("pool_out", WC)
                t.wait("conv_act", WC)
                for m in range(WC):
                    for a, b in spans(TOK):
                        for c in range(WC):
                            mm = pe.matmul(slot[m][:, a:b], pw_sb[:, c, P * m:P * m + P], sq[c][:, a:b], start=(c == 0), stop=(c == WC - 1))
                    mm.then_inc(sems["conv_pw"], 1)
                t.wait("conv_out", WC)

                def scores(k):
                    kind, h, tiles, ctx, _ = steps[k]
                    for s in range(2):
                        if k:
                            t.wait("exp")
                        if kind == "diff":
                            base = DIFF_DH * ((2 * h + s) % 4)
                            rows = slice(base, base + DIFF_DH)
                            q, key, tile = DIFF_Q + h // 2, DIFF_K + h // 2, tiles[0]
                        else:
                            rows = slice(DH * (h % 2), DH * (h % 2) + DH)
                            q, key, tile = NA_Q + h // 2, NA_K + h // 2, tiles[s]
                        at = (LAT if ctx else 0) + P * tile
                        band = kind == "na" and not ctx
                        for a, b in spans(TOK)[1 if ctx else 0:]:
                            mm = pe.matmul(slot[s][:, a:b], z[rows, q, at:at + P], z[rows, key, a:b],
                                           start=True, stop=not (band and a == 0))
                        if band:
                            if tile == 0:
                                t.wait("band_ready")
                            j = GRID_H - 2 - 2 * tile
                            mm = pe.matmul(slot[s][:, 0:LAT], backward[:, :], bands[h][:, j:j + GRID_H, :], start=False, stop=True)
                        mm.then_inc(sems["scores"], 1)

                steps = attention_steps(with_ctx)
                pe.wait_ge(sems["rope_done"], layer + 1)
                heads, norm_at, sqrt_at = 0, None, None
                for k in range(len(steps) + 1):
                    if k < len(steps):
                        scores(k)
                    if not k:
                        continue
                    kind, h, tiles, ctx, last = steps[k - 1]
                    t.wait("probs")
                    for s, q in enumerate(tiles):
                        if k == sqrt_at and s == 0:
                            t.wait("head_sqrt")
                        t.again("probs_t")
                        e = ((k - 1) % 2) * 2 + s
                        for n_key, key in enumerate(range(LAT // P if ctx else 0, TOK // P)):
                            mm = pe.transpose(turn[:, P * n_key:P * n_key + P], e_sb[:, e, P * key:P * key + P], ident[:, :])
                        mm.then_inc(sems["turned"], 1)
                        t.skip("probs_t")
                    if k == norm_at:
                        t.wait("head_sq")
                        t.again("probs_t")
                        for a, b in spans(n):
                            mm = pe.matmul(turn[:, a:b], pairsum[:, :], act_buf[:, a:b], start=True, stop=True)
                        mm.then_inc(sems["head_sum"], 1)
                        sqrt_at = k + 1
                    if last:
                        t.again("probs_t")
                        if h % 2 == 0 and heads:
                            t.wait("head_out")
                        rows = slice(DH * (h % 2), DH * (h % 2) + DH)
                        col = (0 if kind == "diff" else W) + DH * h
                        for key in range(TOK // P):
                            mm = pe.matmul(outs[rows, 0:LAT], v_sb[:, key, col:col + DH], probs_t[:, heads % 2, key, :],
                                           start=(key == 0), stop=(key == TOK // P - 1))
                        if with_ctx:
                            for n_key, key in enumerate(range(LAT // P, TOK // P)):
                                mm = pe.matmul(outs[rows, LAT:TOK], v_sb[:, key, col:col + DH], ctx_probs[heads % 2][:, n_key, :],
                                               start=(n_key == 0), stop=(n_key == CTX // P - 1))
                        mm.then_inc(sems["pv"], 1)
                        heads += 1
                        if kind == "diff" and h % 2:
                            norm_at = k + 2
                t.wait("head_out")
                t.skip("exp", 2)
                pe.wait_ge(sems["exp"], t.n["exp"])

            t.wait("inputs", 16 * 13)
            t.wait("const_rows", 3)
            ssq_made[0] += DC
            mod_reduce(0)
            with loop(pe, 1, MOD_FIRST) as b:
                pe.wait_ge(sems["mod_vec"], b)
                mod_reduce(b)
            norm_reduce(TOK)
            y_made[0] += DC

            for p, (b0, mods) in zip(PHASES, MOD_PLAN):
                if p.name in ("up", "mix_in", "mix_out"):
                    if p.name != "up" or p.group == 0:
                        made = y_made[0] - DC
                    run(p, b0, mods, y_hi, y_lo, "y_lo", made)
                    if p.name == "mix_in":
                        mixer(p.layer)
                        y_made[0] += DC
                    if p.name == "mix_out":
                        ssq_made[0] += DC
                        norm_reduce(p.tokens)
                        y_made[0] += DC
                    if p.name == "up":
                        hidden[0] += p.pairs
                else:
                    run(p, b0, mods, h_hi, h_lo, "hidden_lo", hidden[0] - FG)
                    if p.group == 1:
                        ssq_made[0] += DC
                        norm_reduce(p.tokens)
                        y_made[0] += DC



def _feature_major(a):
    a = a.reshape(a.shape[:-1] + (-1, P))
    return np.ascontiguousarray(np.moveaxis(a, -1, 0))


def _weight_units(w, groups=1):
    rows, cols = w.shape
    return w.reshape(groups, rows // groups // P, P, cols // P, P).transpose(0, 3, 2, 1, 4)


def _constants():
    pairsum = np.kron(np.eye(2), np.ones((DH, DH))).astype(np.float32)
    backward = np.kron(np.eye(2), np.eye(GRID_W)[::-1]).astype(np.float32)
    consts = np.stack([np.eye(P, dtype=np.float32), pairsum, backward])
    nf = DIFF_DH // 4
    inv = np.power(np.float32(10000.0), -np.arange(nf, dtype=np.float32) / np.float32(nf)).astype(np.float32)
    tok = np.arange(LAT)
    d = np.arange(P) % DIFF_DH
    pos = np.where((d // (2 * nf) == 0)[:, None], tok // GRID_W, tok % GRID_W).astype(np.float32)
    ang = (pos * inv[d % nf][:, None]).astype(np.float32)
    sign = np.where((d // nf) % 2 == 0, -1.0, 1.0)[:, None].astype(np.float32)
    cos, sin = np.cos(ang), np.sin(ang) * sign
    scale = np.float32(DIFF_DH ** -0.5)
    rope = np.stack([cos * scale, sin * scale, cos, sin], 1).astype(np.float32)
    inv_w = np.empty((P, WC, TOK), np.float32)
    for g, w in enumerate(POOL_WINDOWS):
        for a, n in ((0, LAT), (LAT, CTX)):
            q = np.arange(n)
            size = np.clip(q + w - w // 2, 0, n) - np.clip(q - w // 2, 0, n)
            inv_w[DH * (g % 2):DH * (g % 2) + DH, g // 2, a:a + n] = np.float32(1) / size.astype(np.float32)
    q = GRID_W - 1 - np.arange(P) % GRID_W
    c0 = np.clip(q - NA_COLS // 2, 0, GRID_W - NA_COLS)[:, None]
    k = np.arange(GRID_W)[None]
    valid = (k >= c0) & (k < c0 + NA_COLS)
    masks = np.stack([valid.astype(np.float32), np.where(valid, 0.0, -1e30).astype(np.float32)], 1)
    return consts, rope, inv_w, masks


def _layout(x, c, ctx, c_ctx, w_mod, b_mod, g_norm, ffn_in, ffn_out, w_in, w_out, pool_w, pool_scale,
            conv_dw, conv_dw_b, conv_ln_g, conv_ln_b, conv_pw, conv_pw_b, diff_lambda, diff_subln_g,
            na_rpb, g_final):
    tokens = np.concatenate([x[0], ctx[0]], 0)
    consts, rope, pool_inv, masks = _constants()
    z_cols = np.concatenate([np.arange(a, a + W) for a in Z_COLUMNS])
    up = [[_weight_units(ffn_in[l, f]).reshape(2, FC, P, DC, P).transpose(1, 0, 2, 3, 4) for f in range(2)]
          for l in range(LAYERS)]
    bias = _feature_major(b_mod.reshape(-1))
    arrays = {
        "xT": tokens.T.reshape(DC, P, TOK).transpose(1, 0, 2),
        "cond": _feature_major(np.stack([c[0], c_ctx])),
        "w_mod": w_mod.reshape(LAYERS, DC, P, MOD_BLOCKS, MOD_COLS).transpose(0, 3, 2, 1, 4).reshape(MOD_ALL, P, DC, MOD_COLS),
        "b_mod": np.stack([bias, bias], 1),
        "gains": _feature_major(g_norm.reshape(LAYERS * 3, D)),
        "g_final": _feature_major(g_final),
        "w_up": np.stack([np.stack(u) for u in up]),
        "w_down": np.stack([np.stack([_weight_units(ffn_out[l, f], 2) for f in range(2)]) for l in range(LAYERS)]),
        "w_in": np.stack([_weight_units(w_in[l][:, z_cols])[0] for l in range(LAYERS)]),
        "w_out": np.stack([_weight_units(w_out[l])[0] for l in range(LAYERS)]),
        "pool_w": pool_w,
        "conv_pw": conv_pw.reshape(LAYERS, WC, P, W).transpose(0, 2, 1, 3),
        "conv_vec": _feature_major(np.stack([conv_dw_b, conv_ln_g, conv_ln_b, conv_pw_b, pool_scale], 1)),
        "conv_taps": conv_dw.reshape(LAYERS, CONV_K, WC, P).transpose(3, 0, 2, 1),
        "lam_in": diff_lambda,
        "subln": np.concatenate([diff_subln_g, diff_subln_g], 1).T,
        "rpb": np.pad(na_rpb.reshape(-1), RPB_PAD),
        "consts": consts, "rope": rope, "pool_inv": pool_inv, "masks": masks,
    }
    return {k: np.ascontiguousarray(v) for k, v in arrays.items()}


def kernel(**inputs):
    import concourse.bacc as bacc
    from concourse.bass_utils import run_bass_kernel_spmd

    arrays = _layout(**{k: np.asarray(v) for k, v in inputs.items()})
    nc = bacc.Bacc("TRN2", target_bir_lowering=False, num_devices=1)
    args = {k: nc.dram_tensor(f"in_{k}", a.shape, F32, kind="ExternalInput").ap() for k, a in arrays.items()}
    args["out"] = nc.dram_tensor("out_x", (P, DC, LAT), F32, kind="ExternalOutput").ap()
    trunk(nc, **args)
    r = run_bass_kernel_spmd(nc, [{f"in_{k}": a for k, a in arrays.items()}], core_ids=[0])
    out = np.asarray(r.results[0]["out_x"])
    return np.ascontiguousarray(out.transpose(1, 0, 2).reshape(D, LAT).T)[None]
```

```python
import math

import numpy as np

import concourse.bass as bass
from concourse import mybir

F32 = mybir.dt.float32
F32R = mybir.dt.float32r
ALU = mybir.AluOpType
ACT = mybir.ActivationFunctionType
AX_X = mybir.AxisListType.X

P = 128
D = 1024
LAYERS = 2
LAT = 512
CTX = 256
TOK = LAT + CTX
DC = D // P
F = 2816
FC = F // P
FG = FC // 2
N_MOD = 9
GRID_W = 64
GRID_H = LAT // GRID_W
NA_COLS = 16
RPB_R = 15
RPB_C = 31
CONV_K = 31
HALO = CONV_K // 2
W = 256
WC = W // P
HEADS = 4
DH = 64
DIFF_DH = 32
EPS = 1e-6
LN_EPS = 1e-5
POOL_WINDOWS = (2, 4, 8, 16)
RPB_PAD = 64
LAG = 3

CONV_A, CONV_G, POOL_U, DIFF_Q, DIFF_K, DIFF_V, NA_Q, NA_K, NA_V = range(0, 18, 2)
Z_UNITS = 18
Z_COLUMNS = [W, 2 * W, 0, 3 * W, 4 * W, 5 * W, 6 * W, 7 * W, 8 * W]

MOD_COLS = 256
MOD_BLOCKS = N_MOD * D // MOD_COLS
MOD_ALL = LAYERS * MOD_BLOCKS
MOD_STEPS = 2 * DC
MOD_FIRST = 2 * D // MOD_COLS

CONV_LEN = HALO + LAT + HALO + CTX + HALO
CONV_OUT = LAT + HALO + CTX
CONV_LAT = slice(0, LAT)
CONV_CTX = slice(LAT + HALO, CONV_OUT)
PPAD = 8
POOL_LEN = PPAD + LAT + PPAD + CTX + PPAD
POOL_LAT0 = PPAD
POOL_CTX0 = PPAD + LAT + PPAD


class Phase:

    def __init__(self, name, layer, half, group, pairs, kc, tokens, first):
        self.name, self.layer, self.half, self.group = name, layer, half, group
        self.pairs, self.kc, self.tokens, self.first = pairs, kc, tokens, first
        self.next_kc = 0


def plan_phases():
    out, unit = [], 0

    def add(name, layer, half, group, pairs, kc, tokens):
        nonlocal unit
        p = Phase(name, layer, half, group, pairs, kc, tokens, unit)
        if out:
            out[-1].next_kc = kc
        out.append(p)
        unit += 2 * pairs

    for layer in range(LAYERS):
        last = layer == LAYERS - 1
        for half in range(2):
            tokens = LAT if last and half == 1 else TOK
            for group in range(2):
                add("up", layer, half, group, FG, DC, tokens)
                add("down", layer, half, group, DC // 2, FG, tokens)
            if half == 0:
                add("mix_in", layer, half, 0, Z_UNITS // 2, DC, TOK)
                add("mix_out", layer, half, 0, DC // 2, DC, LAT if last else TOK)
    return out


PHASES = plan_phases()


def plan_mod_blocks():
    out, block = [], MOD_FIRST
    for p in PHASES:
        n = min(p.pairs, MOD_ALL - block) if p.name in ("up", "down") else 0
        out.append((block, n))
        block += n
    return out


MOD_PLAN = plan_mod_blocks()


def segments(pairs, mods):
    out = [(0, 1, mods > 0)]
    if mods >= pairs - 1:
        out.append((1, pairs - 1, True))
    elif mods > 1:
        out += [(1, mods, True), (mods, pairs - 1, False)]
    else:
        out.append((1, pairs - 1, False))
    return out + [(pairs - 1, pairs, mods >= pairs)]


def attention_steps(with_ctx):
    out = []
    for h in range(HEADS):
        tiles = [(t, False) for t in range(LAT // P)] + [(t, True) for t in range(CTX // P)] * with_ctx
        out += [("diff", h, (t,), c, n == len(tiles) - 1) for n, (t, c) in enumerate(tiles)]
    for h in range(HEADS):
        tiles = [((0, 1), False), ((2, 3), False)] + [((0, 1), True)] * with_ctx
        out += [("na", h, t, c, n == len(tiles) - 1) for n, (t, c) in enumerate(tiles)]
    return out


def value_steps(with_ctx):
    lengths = [0] * (2 * HEADS)
    for kind, h, *_ in attention_steps(with_ctx):
        lengths[h + HEADS * (kind == "na")] += 1
    return [min(4, n) for n in lengths[1:]] + [1]


def z_segments(layer):
    if layer < LAYERS - 1:
        return [(0, 1, TOK), (1, 2, TOK), (2, Z_UNITS // 2 - 1, TOK), (Z_UNITS // 2 - 1, Z_UNITS // 2, TOK)]
    return [(0, 1, LAT), (1, 2, LAT), (2, DIFF_K // 2, LAT), (DIFF_K // 2, NA_Q // 2, TOK),
            (NA_Q // 2, NA_K // 2, LAT), (NA_K // 2, NA_V // 2, TOK), (NA_V // 2, Z_UNITS // 2, TOK)]


SEMAPHORES = [
    *(f"mod_first{b}" for b in range(MOD_FIRST)), "qk_hi", "qk_lo", "stacked0", "stacked1", "cond", "x_in", "first_step", "mod_rounded", "mod_parts",
    "inputs", "mixer_consts", "const_rows",
    "raw_loaded0", "raw_loaded1", "split_hi", "split_lo", "unit_done", "slot_free0", "slot_free1",
    "mod_raw", "mod_sum", "mod_vec", "cond_silu", "mod_step",
    "hidden_hi", "hidden_lo", "square", "sum_squares", "norm_sum", "norm_sqrt", "rstd",
    "normed", "affine", "y_hi", "y_lo", "scale_ready", "gates_ready",
    "rope_tables", "rope_step", "rope_done", "lam_in", "lam_exp", "lam_step", "lam_ready",
    "zeros", "conv_u", "conv_acc", "conv_mean", "conv_cent", "conv_sq", "conv_var", "conv_sqrt",
    "conv_rstd", "conv_norm", "conv_act", "conv_pw", "conv_out",
    "pool_step", "pool_tables", "pool_d", "pool_mm", "pool_out", "mixer_weights", "blocks_zero",
    "v_turned", "v_ready0", "v_ready1", "band_raw", "band_step", "band_ready",
    "scores", "neg_max", "exp", "stat", "sums_inverted", "probs", "half_scaled", "turned", "probs_t", "pv", "head_out",
    "head_sq", "head_sum", "head_sqrt", "head_rstd", "head_norm", "final", "out_stored",
]


class Tally:

    def __init__(self, engine, sems):
        self.engine, self.sems, self.n = engine, sems, {}

    def wait(self, name, more=1):
        self.n[name] = self.n.get(name, 0) + more
        self.engine.wait_ge(self.sems[name], self.n[name])

    def skip(self, name, more=1):
        self.n[name] = self.n.get(name, 0) + more

    def again(self, name):
        if self.n.get(name, 0):
            self.engine.wait_ge(self.sems[name], self.n[name])


def trunk(nc, xT, cond, w_mod, b_mod, gains, g_final, w_up, w_down, w_in, w_out, pool_w, conv_pw,
          conv_vec, conv_taps, lam_in, subln, rpb, consts, rope, pool_inv, masks, out):
    sems = {name: nc.alloc_semaphore(name) for name in SEMAPHORES}

    cursor = [((nc.sbuf_base + 31) // 32) * 32]

    def place(name, shape, dtype=F32, at=None):
        size = 4 * int(np.prod(shape[1:]))
        at = (at + 31) // 32 * 32 if at is not None else None
        if at is None:
            at = cursor[0]
            cursor[0] = at + (size + 31) // 32 * 32
        return nc.alloc_sbuf_tensor_at(name, shape, dtype, offset=at)

    x = place("x", [P, DC, TOK])
    raw = [place(f"w_raw{s}", [P, FG, P]) for s in range(2)]
    w_hi = [place(f"w_hi{s}", [P, FG, P], F32R) for s in range(2)]
    w_lo = [place(f"w_lo{s}", [P, FG, P], F32R) for s in range(2)]
    at_mod = cursor[0]
    mod_raw = place("mod_raw", [P, DC, MOD_COLS])
    rope_t = place("rope_t", [P, 4, LAT], at=at_mod)
    at_acc = cursor[0]
    mod_acc = place("mod_acc", [P, 2, MOD_COLS])
    mod_lo = place("mod_lo", [P, 2, MOD_COLS], F32R, at=at_acc)
    mod_hi = place("mod_hi", [P, 2, MOD_COLS], F32R)
    mod_vec = place("mod_vec", [P, 2, LAYERS * N_MOD * DC])
    mod_bias = place("mod_bias", [P, 1, LAYERS * N_MOD * DC])
    gain = place("gain", [P, LAYERS * 3, DC])
    gain_f = place("gain_f", [P, DC])
    cvec = place("cvec", [P, 2, DC])
    cact = place("cact", [P, 2, DC])
    scale1 = place("scale1", [P, 2, DC])
    gates = place("gates", [P, 2, DC])
    eps_t = place("eps_t", [P, 2])
    ones = place("ones", [P, P])
    one_r = place("one_r", [P, 2], F32R)
    ident = place("ident", [P, P])
    pairsum = place("pairsum", [P, P])
    backward = place("backward", [P, P])
    mask = place("mask", [P, 2, GRID_W])
    cvecs = place("cvecs", [P, LAYERS, 5, WC])
    ctaps = place("ctaps", [P, LAYERS, WC, CONV_K])
    sub_g = place("sub_g", [P, LAYERS])
    lam_rows = place("lam_rows", [P, LAYERS, 4, DIFF_DH])
    lam = place("lam", [P, 8])
    nmax = place("nmax", [P, 4])
    esum = place("esum", [P, 4])
    rsum = place("rsum", [P, 4])
    nrsum = place("nrsum", [P, 4])
    act_buf = place("act_buf", [P, TOK])
    hid_buf = place("hid_buf", [P, TOK])
    at_sq = cursor[0]
    sq = [place(f"sq{s}", [P, TOK]) for s in range(2)]
    at_rstd = cursor[0]
    rstd = place("rstd", [P, POOL_LEN])
    at_ssq = cursor[0]
    ssq = place("ssq", [P, TOK])
    pw_sb = place("pw_sb", [P, WC, W], at=at_ssq)
    pool_sb = place("pool_sb", [P, WC, P], at=at_ssq + 4 * WC * W)
    at_y = cursor[0]
    y_hi = place("y_hi", [P, DC, TOK], F32R)
    y_lo = place("y_lo", [P, DC, TOK], F32R)
    at_h = cursor[0]
    h_hi = place("h_hi", [P, FG, TOK], F32R)
    h_lo = place("h_lo", [P, FG, TOK], F32R)
    assert cursor[0] <= nc.sbuf_usable_end, cursor[0]
    mod_start = place("mod_start", [P, MOD_FIRST, DC, MOD_COLS], at=at_h)
    mod_start_acc = place("mod_start_acc", [P, MOD_FIRST // 2, 2, MOD_COLS], at=at_y)
    v_sb = place("v_sb", [P, TOK // P, 2 * W], at=at_y)
    e_sb = place("e_sb", [P, 4, TOK], at=at_y + 4 * 3072)
    probs_t = place("probs_t", [P, 2, TOK // P, LAT], at=at_y + 8 * 3072)
    o_final = place("o_final", [P, DC, LAT], at=at_y)
    z = place("z", [P, Z_UNITS, TOK], at=at_h)
    conv_acc = [place(f"conv_acc{c}", [P, CONV_OUT], at=at_h + 4 * 2 * c * TOK) for c in range(WC)]
    ctx_probs = [place(f"ctx_probs{b}", [P, CTX // P, CTX], at=at_h + 4 * (1 + 2 * b) * TOK) for b in range(2)]
    at_free = at_h + 4 * Z_UNITS * TOK
    conv_u = place("conv_u", [P, WC, CONV_LEN], at=at_free)
    pool_a = place("pool_a", [P, POOL_LEN], at=at_free + 4 * WC * CONV_LEN)
    pool_b = rstd
    bands = [place(f"band{h}", [P, RPB_R - 1, GRID_W], at=at_free + h * 4 * (RPB_R - 1) * GRID_W) for h in range(3)]
    bands.append(place("band3", [P, RPB_R - 1, GRID_W], at=at_h + 4 * DIFF_Q * TOK))
    chunk = 4 * TOK
    at_probs1 = at_y + 12 * chunk
    qk_lo = place("qk_lo", [P, 4, TOK], F32R, at=at_h + DIFF_Q * chunk)
    qk_hi = [place(f"qk_hi{i}", [P, TOK], F32R, at=at)
             for i, at in enumerate((at_probs1, at_h + NA_V * chunk, at_probs1 + chunk, at_h + (NA_V + 1) * chunk))]
    places = [(at_mod, at_mod + chunk, at_probs1 + 2 * chunk, at_probs1 + 3 * chunk),
              (at_sq, at_sq + chunk, at_rstd, at_ssq),
              (at_mod, at_mod + chunk, at_h + (DIFF_V + 1) * chunk, at_h + DIFF_K * chunk)]
    places.append(places[1])
    stacks = [[place(f"stack{h}{i}", [P, TOK], F32R, at=at) for i, at in enumerate(tiles)] for h, tiles in enumerate(places)]
    mixed = [z[:, POOL_U, :], z[:, POOL_U + 1, :], z[:, 0, :], z[:, 2, :],
             z[:, DIFF_V, :], z[:, DIFF_V + 1, :], z[:, NA_V, :], z[:, NA_V + 1, :]]

    ps = nc.alloc_psum_tensor("ps", [P, 8 * 512], F32)
    slot = [ps[:, 0:1024], ps[:, 1024:2048]]
    turn = ps[:, 2048:3072]
    outs = ps[:, 3072:4096]
    mod_ps = ps[:, 3072:3080].rearrange("p (t c n) -> p t c n", t=2, c=2)
    mod_start_ps = ps[:, 3072:3072 + 4 * DC].rearrange("p (c t) -> p c t", t=2)
    slot_free = ["slot_free0", "slot_free1"]
    raw_loaded = ["raw_loaded0", "raw_loaded1"]

    def spans(tokens):
        return ((0, LAT), (LAT, TOK)) if tokens == TOK else ((0, LAT),)

    def kinds(tokens):
        return tuple(enumerate(spans(tokens)))

    def mod_chunk(layer, i):
        return (layer * N_MOD + i) * DC

    def loop(engine, a, b):
        return engine.Fori(a, b)

    def lam_init(layer):
        return 0.8 - 0.6 * math.exp(-0.3 * layer)

    def y_count(layer, norm):
        return DC * (4 * layer + norm + 1)

    def unit_pairs(layer, name):
        return next(p.first // 2 for p in PHASES if p.layer == layer and p.name == name)

    def scores_before(layer):
        return sum(2 * len(attention_steps(n < LAYERS - 1)) for n in range(layer))

    def diff_scores(layer):
        return 2 * sum(s[0] == "diff" for s in attention_steps(layer < LAYERS - 1))

    def turned_before(layer):
        return sum(sum(len(s[2]) for s in attention_steps(n < LAYERS - 1)) for n in range(layer))

    with nc.Block() as block:

        @block.sync
        def _(sp):
            def load(dst, src, name="inputs"):
                sp.dma_start(dst, src).then_inc(sems[name], 16)

            load(cvec[:, :, :], cond, "cond")
            load(mod_bias[:, :, :], b_mod)
            load(x[:, :, :], xT, "x_in")
            load(gain[:, :, :], gains)
            load(gain_f[:, :], g_final)
            load(ident[:, :], consts[0])
            load(pairsum[:, :], consts[1])
            load(backward[:, :], consts[2])
            load(mask[:, :, :], masks)
            load(cvecs[:, :, :, :], conv_vec)
            load(ctaps[:, :, :, :], conv_taps)
            load(sub_g[:, :], subln)
            load(lam_rows[:, :, :, :], lam_in.partition_broadcast(P))

            def source(p, i, s):
                if p.name == "up":
                    return w_up[p.layer, p.half, p.group * FG + i, s]
                if p.name == "down":
                    return w_down[p.layer, p.half, p.group, 2 * i + s]
                return (w_in if p.name == "mix_in" else w_out)[p.layer, 2 * i + s]

            def fetch(p, i, s, wait=True):
                if wait:
                    sp.wait_ge(sems["split_lo"], 2 * i + (p.first + s - 1))
                sp.dma_start(raw[s][:, 0:p.kc, :], source(p, i, s)).then_inc(sems[raw_loaded[s]], 16)

            def stack_heads(layer):
                scored = scores_before(layer)
                per_head = diff_scores(layer) // HEADS
                for h in range(HEADS):
                    if h % 2 == 0:
                        sp.wait_ge(sems["qk_hi"], 4 * layer + h + 2)
                        sp.wait_ge(sems["qk_lo"], 4 * layer + h + 2)
                    if h == 1:
                        sp.wait_ge(sems["conv_pw"], WC * (layer + 1))
                    if h >= 2:
                        sp.wait_ge(sems["scores"], scored + (h - 1) * per_head)
                    if h == 2:
                        sp.wait_ge(sems["stacked1"], 16 * 12 * (2 * layer + 1))
                    for s in range(2):
                        c = h // 2
                        rows = slice(DIFF_DH * ((2 * h + s) % 4), DIFF_DH * ((2 * h + s) % 4) + DIFF_DH)
                        nq = TOK if layer < LAYERS - 1 else LAT
                        parts = {"q_hi": qk_hi[c][rows, 0:nq], "q_lo": qk_lo[rows, c, 0:nq],
                                 "k_hi": qk_hi[WC + c][rows, :], "k_lo": qk_lo[rows, WC + c, :]}
                        for tile, names in ((stacks[h][s], ("q_hi", "q_hi", "q_lo")), (stacks[h][2 + s], ("k_hi", "k_lo", "k_hi"))):
                            for r, name in enumerate(names):
                                src = parts[name]
                                n = nq if name[0] == "q" else TOK
                                sp.dma_start(tile[DIFF_DH * r:DIFF_DH * r + DIFF_DH, 0:n].bitcast(F32), src.bitcast(F32)).then_inc(sems[f"stacked{h % 2}"], 16)

            for p in PHASES:
                if p is PHASES[0]:
                    for s in range(2):
                        fetch(p, 0, s, wait=False)
                if p.name == "mix_out":
                    for s in range(2):
                        fetch(p, 0, s)
                    stack_heads(p.layer)
                start = 1 if p is PHASES[0] or p.name == "mix_out" else 0
                with loop(sp, start, p.pairs) as i:
                    for s in range(2):
                        fetch(p, i, s)
            sp.wait_ge(sems["final"], DC)
            sp.dma_start(out, o_final[:, :, :]).then_inc(sems["out_stored"], 16)
            sp.wait_ge(sems["out_stored"], 16)

        @block.gpsimd
        def _(pool):
            t = Tally(pool, sems)
            pool.memset(ones[:, :], 1.0).then_inc(sems["const_rows"], 1)
            pool.memset(eps_t[:, 0:1], EPS).then_inc(sems["const_rows"], 1)
            t.wait("const_rows", 2)
            pool.tensor_copy(one_r[:, :], ones[:, 0:2]).then_inc(sems["const_rows"], 1)
            pool.memset(eps_t[:, 1:2], LN_EPS).then_inc(sems["const_rows"], 1)

            def fetch_mod(b, wait=True):
                if wait:
                    pool.wait_ge(sems["mod_step"], MOD_STEPS * b - MOD_STEPS * MOD_FIRST)
                pool.dma_start(mod_raw[:, :, :], w_mod[b]).then_inc(sems["mod_raw"], 16)

            ones2 = ones[:, 0:1].rearrange("p (a b) -> p a b", a=1).to_broadcast([P, 2, MOD_COLS])

            def round_mod(b):
                pool.wait_ge(sems["mod_step"], MOD_STEPS * b - MOD_STEPS * (MOD_FIRST - 1))
                pool.tensor_tensor(mod_hi[:, :, :], mod_acc[:, :, :], ones2, ALU.mult).then_inc(sems["mod_rounded"], 1)
                pool.wait_ge(sems["mod_rounded"], b - (MOD_FIRST - 1))
                pool.tensor_tensor(mod_lo[:, :, :], mod_acc[:, :, :], mod_hi[:, :, :].bitcast(F32),
                                   ALU.subtract).then_inc(sems["mod_parts"], 1)

            def mixer(layer, mods_before):
                pool.wait_ge(sems["mod_step"], MOD_STEPS * (mods_before - MOD_FIRST))
                pool.dma_start(rope_t[:, :, :], rope).then_inc(sems["rope_tables"], 16)
                t.n["norm_sum"] = 1 + 3 * layer
                t.wait("norm_sum")
                pool.memset(pool_sb[:, :, :], 0.0).then_inc(sems["blocks_zero"], 1)
                t.wait("blocks_zero")
                for g in range(4):
                    a = DH * (g % 2)
                    pool.dma_start(pool_sb[a:a + DH, g // 2, a:a + DH], pool_w[layer, g]).then_inc(sems["mixer_weights"], 16)
                pool.dma_start(pw_sb[:, :, :], conv_pw[layer]).then_inc(sems["mixer_weights"], 16)
                pool.wait_ge(sems["y_lo"], y_count(layer, 1))
                for c, buf in enumerate((act_buf, hid_buf)):
                    pool.dma_start(buf[:, :], pool_inv[:, c, :]).then_inc(sems["pool_tables"], 16)
                t.wait("pool_tables", 32)

                def step(instruction):
                    instruction.then_inc(sems["pool_step"], 1)
                    t.wait("pool_step")

                parts = ((0, LAT, POOL_LAT0), (LAT, TOK, POOL_CTX0))[:1 if layer == LAYERS - 1 else 2]
                n_out = parts[-1][1]
                for c, inv in enumerate((act_buf, hid_buf)):
                    pool.wait_ge(sems[slot_free[c]], unit_pairs(layer, "mix_in") + POOL_U // 2 + 1)
                    u = z[:, POOL_U + c, :]
                    step(pool.memset(pool_a[:, :], 0.0))
                    step(pool.memset(pool_b[:, :], 0.0))
                    for a, b, at in parts:
                        step(pool.tensor_copy(pool_a[:, at:at + b - a], u[:, a:b]))
                    n = parts[-1][2] + parts[-1][1] - parts[-1][0] + PPAD
                    step(pool.tensor_tensor(pool_b[:, 1:n], pool_a[:, 0:n - 1], pool_a[:, 1:n], ALU.add))
                    if c == 0:
                        step(pool.tensor_tensor(pool_a[DH:P, 1:n - 1], pool_b[DH:P, 0:n - 2], pool_b[DH:P, 2:n], ALU.add))
                        halves = (pool_b, pool_a)
                    else:
                        step(pool.tensor_tensor(pool_a[:, 1:n - 1], pool_b[:, 0:n - 2], pool_b[:, 2:n], ALU.add))
                        step(pool.tensor_tensor(pool_b[:, 2:n - 2], pool_a[:, 0:n - 4], pool_a[:, 4:n], ALU.add))
                        step(pool.tensor_tensor(pool_a[DH:P, 4:n - 4], pool_b[DH:P, 0:n - 8], pool_b[DH:P, 8:n], ALU.add))
                        halves = (pool_b, pool_a)
                    for g, buf in enumerate(halves):
                        rows = slice(DH * g, DH * g + DH)
                        for a, b, at in parts:
                            step(pool.tensor_tensor(inv[rows, a:b], buf[rows, at:at + b - a], inv[rows, a:b], ALU.mult))
                    pool.tensor_tensor(u[:, 0:n_out], inv[:, 0:n_out], u[:, 0:n_out], ALU.subtract).then_inc(sems["pool_d"], 1)

                pool.wait_ge(sems["conv_acc"], (layer + 1) * WC * CONV_K)
                t.n["pool_d"] = WC * layer
                t.wait("pool_d", WC)

                def load_band(h):
                    for s in range(2):
                        first = RPB_PAD + ((layer * HEADS + h) * RPB_R + 1 - s) * RPB_C + RPB_C // 2 - (GRID_W - 1)
                        src = bass.AP(rpb.tensor, first, [[1, GRID_W], [RPB_C, RPB_R - 1], [1, GRID_W]])
                        pool.dma_start(bands[h][GRID_W * s:GRID_W * s + GRID_W, :, :], src).then_inc(sems["band_raw"], 16)

                def mask_band(h, row):
                    if row == 1:
                        t.wait("band_step")
                    m = mask[:, row:row + 1, :].to_broadcast([P, RPB_R - 1, GRID_W])
                    pool.tensor_tensor(bands[h][:, :, :], bands[h][:, :, :], m,
                                       (ALU.mult, ALU.add)[row]).then_inc(sems[("band_step", "band_ready")[row]], 1)

                for h in range(HEADS - 1):
                    load_band(h)
                t.wait("band_raw", 16 * 2 * (HEADS - 1))
                for h in range(HEADS - 1):
                    for row in range(2):
                        mask_band(h, row)
                for n_split, c in enumerate((0, 2, 1, 3)):
                    pool.wait_ge(sems["qk_hi"], 4 * layer + n_split + 1)
                    w = TOK if c >= WC or layer < LAYERS - 1 else LAT
                    pool.tensor_tensor(qk_lo[:, c, 0:w], z[:, DIFF_Q + c, 0:w], qk_hi[c][:, 0:w].bitcast(F32),
                                       ALU.subtract).then_inc(sems["qk_lo"], 1)
                na_step = 0
                for k, (kind, h, tiles, ctx, last) in enumerate(attention_steps(layer < LAYERS - 1)):
                    if kind == "na":
                        if na_step == 0:
                            pool.wait_ge(sems["scores"], scores_before(layer) + diff_scores(layer))
                            load_band(HEADS - 1)
                        elif na_step == 2:
                            t.wait("band_raw", 16 * 2)
                            mask_band(HEADS - 1, 0)
                        elif na_step == 3:
                            mask_band(HEADS - 1, 1)
                        na_step += 1
                    keys = slice(LAT, TOK) if ctx else slice(0, TOK)
                    e = (k % 2) * 2 + 1
                    t.wait("sums_inverted")
                    factor = nrsum[:, e - 1:e] if kind == "diff" else rsum[:, e:e + 1]
                    factor = factor.to_broadcast([P, keys.stop - keys.start])
                    pool.tensor_tensor(e_sb[:, e, keys], e_sb[:, e, keys], factor, ALU.mult).then_inc(sems["half_scaled"], 1)

            for p, (b0, n) in zip(PHASES, MOD_PLAN):
                if p.name == "mix_in":
                    mixer(p.layer, b0)
                    pool.wait_ge(sems["rope_done"], p.layer + 1)
                if b0 == MOD_FIRST:
                    fetch_mod(b0, wait=False)
                    round_mod(b0)
                    b0, n = b0 + 1, n - 1
                if n:
                    with loop(pool, b0, b0 + n) as b:
                        fetch_mod(b)
                        round_mod(b)

        @block.scalar
        def _(act):
            t = Tally(act, sems)

            def split_hi(p, i, s, ahead):
                kc = ahead
                if not kc:
                    return
                act.wait_ge(sems["unit_done"], 2 * i + (p.first + s + 1))
                act.wait_ge(sems[raw_loaded[s]], 16 * i + 16 * (p.first // 2 + 2))
                act.activation(w_hi[s][:, 0:kc, :], raw[s][:, 0:kc, :], ACT.Copy).then_inc(sems["split_hi"], 1)

            def square(src, s, tokens, wait_buffer):
                if wait_buffer is not None:
                    act.wait_ge(sems["sum_squares"], wait_buffer)
                act.activation(sq[s][:, 0:tokens], src, ACT.Square).then_inc(sems["square"], 1)

            def norm_tail(tokens):
                t.wait("norm_sum")
                act.activation(rstd[:, 0:tokens], turn[:, 0:tokens], ACT.Sqrt, bias=eps_t[:, 0:1], scale=1.0 / D).then_inc(sems["norm_sqrt"], 1)

            def make_y(layer, norm, tokens):
                t.wait("scale_ready")
                shift = mod_chunk(layer, 3 * norm)
                for m in range(DC):
                    buf = (act_buf, hid_buf)[m % 2]
                    t.wait("normed")
                    if m >= 2:
                        act.wait_ge(sems["y_lo"], y_made[0] + m - 1)
                    for k, (a, b) in kinds(tokens):
                        act.activation(buf[:, a:b], sq[m % 2][:, a:b], ACT.Identity,
                                       bias=mod_vec[:, k, shift + m:shift + m + 1],
                                       scale=scale1[:, k, m:m + 1]).then_inc(sems["affine"], 1)
                    t.wait("affine", len(kinds(tokens)))
                    act.activation(y_hi[:, m, 0:tokens], buf[:, 0:tokens], ACT.Copy).then_inc(sems["y_hi"], 1)
                y_made[0] += DC

            y_made = [0]
            ssq_made = [0]
            hidden = [0]

            for b in range(MOD_FIRST):
                act.dma_start(mod_start[:, b, :, :], w_mod[b]).then_inc(sems[f"mod_first{b}"], 16)
            t.wait("cond", 16)
            act.activation(cact[:, :, :], cvec[:, :, :], ACT.Silu).then_inc(sems["cond_silu"], 1)
            t.wait("x_in", 16)
            t.wait("const_rows", 4)
            for m in range(DC):
                square(x[:, m, :], m % 2, TOK, m - 1 if m >= 2 else None)
            ssq_made[0] += DC - 1
            norm_tail(TOK)
            t.wait("inputs", 16 * 11)
            for s in range(2):
                act.wait_ge(sems[raw_loaded[s]], 16)
                act.activation(w_hi[s][:, 0:DC, :], raw[s][:, 0:DC, :], ACT.Copy).then_inc(sems["split_hi"], 1)
            make_y(0, 0, TOK)

            def up(p, mods):
                n = p.tokens
                h0 = hidden[0]
                pair0 = p.first // 2

                def body(i, ahead):
                    act.wait_ge(sems["unit_done"], 2 * i + (p.first + 1))
                    act.activation(act_buf[:, 0:n], slot[0][:, 0:n], ACT.Silu).then_inc(sems["slot_free0"], 1)
                    split_hi(p, i, 0, ahead)
                    split_hi(p, i, 1, ahead)
                    act.wait_ge(sems["slot_free1"], i + (pair0 + 1))
                    act.activation(h_hi[:, i, 0:n], hid_buf[:, 0:n], ACT.Copy).then_inc(sems["hidden_hi"], 1)

                act.wait_ge(sems["y_lo"], y_made[0])
                for a, b, _ in segments(p.pairs, mods):
                    if b - a == 1:
                        body(a, p.kc if b < p.pairs else p.next_kc)
                    else:
                        with loop(act, a, b) as i:
                            body(i, p.kc)
                hidden[0] += p.pairs

            def down(p, mods, squares):
                n = p.tokens
                pair0 = p.first // 2
                s0 = ssq_made[0]

                def body(i, ahead):
                    for s in range(2):
                        split_hi(p, i, s, ahead)
                        if squares:
                            act.wait_ge(sems[slot_free[s]], i + (pair0 + 1))
                            start = isinstance(i, int) and i == 0
                            square(x[:, 2 * i + s, 0:n], s, n, None if start else 2 * i + (s0 + s - 1))

                for a, b, _ in segments(p.pairs, mods):
                    if b - a == 1:
                        body(a, p.kc if b < p.pairs else p.next_kc)
                    else:
                        with loop(act, a, b) as i:
                            body(i, p.kc)
                if squares:
                    ssq_made[0] += DC - 1

            def mix_in(p):
                def body(i, tokens, func, ahead):
                    for s in range(2):
                        act.wait_ge(sems["unit_done"], 2 * i + (p.first + s + 1))
                        act.activation(z[:, 2 * i + s, 0:tokens], slot[s][:, 0:tokens], func).then_inc(sems[slot_free[s]], 1)
                        split_hi(p, i, s, ahead)

                for a, b, tokens in z_segments(p.layer):
                    func = ACT.Sigmoid if a == CONV_G // 2 else ACT.Copy
                    if b - a == 1:
                        body(a, tokens, func, p.kc if b < p.pairs else p.next_kc)
                    else:
                        with loop(act, a, b) as i:
                            body(i, tokens, func, p.kc)

            def mixer(layer):
                with_ctx = layer < LAYERS - 1
                n = TOK if with_ctx else LAT
                t.wait("lam_in")
                act.activation(lam[:, 2:4], lam[:, 0:2], ACT.Exp).then_inc(sems["lam_exp"], 1)
                def copy_values(k):
                    act.wait_ge(sems["v_turned"], layer * (TOK // P) + k + 1)
                    act.activation(v_sb[:, k, :], turn[:, 0:512], ACT.Copy).then_inc(sems["v_ready0"], 1)

                def qk_hi_part(c):
                    w = TOK if c >= WC else n
                    act.activation(qk_hi[c][:, 0:w], z[:, DIFF_Q + c, 0:w], ACT.Copy).then_inc(sems["qk_hi"], 1)

                act.wait_ge(sems["rope_done"], layer + 1)
                qk_hi_part(0)
                qk_hi_part(2)
                copy_values(0)
                copy_values(2)
                act.wait_ge(sems["pool_d"], WC * (layer + 1))
                for c in range(WC):
                    t.wait("conv_cent")
                    act.activation((act_buf, hid_buf)[c][:, 0:n], sq[c][:, 0:n], ACT.Square).then_inc(sems["conv_sq"], 1)
                copy_values(4)
                act.wait_ge(sems["v_turned"], (layer + 1) * (TOK // P))
                qk_hi_part(1)
                qk_hi_part(3)
                t.wait("conv_var")
                act.activation(rstd[:, 0:n], outs[:, 0:n], ACT.Sqrt, bias=eps_t[:, 1:2], scale=1.0 / W).then_inc(sems["conv_sqrt"], 1)
                for c in range(WC):
                    t.wait("pool_mm")
                    act.activation(z[:, POOL_U + c, 0:n], slot[c][:, 0:n], ACT.Identity,
                                   scale=cvecs[:, layer, 4, c:c + 1]).then_inc(sems["pool_out"], 1)
                for c in range(WC):
                    t.wait("conv_norm")
                    act.activation(sq[c][:, 0:n], sq[c][:, 0:n], ACT.Silu, bias=cvecs[:, layer, 2, c:c + 1],
                                   scale=cvecs[:, layer, 1, c:c + 1]).then_inc(sems["conv_act"], 1)

                steps = attention_steps(with_ctx)
                tiles0 = turned_before(layer)
                step_tiles = []
                head = [0]
                copy_at, copy_chunk, norm_at = None, None, None
                spread = value_steps(with_ctx)

                def copy_out(c):
                    t.wait("pv", 2)
                    act.activation(mixed[c][:, 0:n], outs[:, 0:n], ACT.Copy).then_inc(sems["head_out"], 1)

                def exponentials(k, s):
                    kind, h, tiles, ctx, _ = steps[k]
                    keys = slice(LAT, TOK) if ctx else slice(0, TOK)
                    t.wait("neg_max")
                    if k >= 2:
                        before = step_tiles[k - 3] if k >= 3 else tiles0
                        act.wait_ge(sems["turned"], before + min(s + 1, len(steps[k - 2][2])))
                    e = (k % 2) * 2 + s
                    act.activation(e_sb[:, e, keys], slot[s][:, keys], ACT.Exp, bias=nmax[:, e:e + 1],
                                   accum_out=esum[:, e:e + 1]).then_inc(sems["exp"], 1)

                def copy_probs(step, q):
                    kind, h, tiles, ctx, last = step
                    hn = head[0] % 2
                    t.wait("turned")
                    if head[0] >= 2 or layer:
                        act.wait_ge(sems["pv"], layer * 2 * HEADS + head[0] - 1)
                    if ctx:
                        act.activation(ctx_probs[hn][:, :, P * q:P * q + P],
                                       turn[:, 0:2 * P].rearrange("p (k q) -> p k q", q=P), ACT.Copy).then_inc(sems["probs_t"], 1)
                    else:
                        act.activation(probs_t[:, hn, :, P * q:P * q + P],
                                       turn[:, 0:TOK].rearrange("p (k q) -> p k q", q=P), ACT.Copy).then_inc(sems["probs_t"], 1)

                for k in range(len(steps) + 3):
                    turned = steps[k - 2] if 2 <= k < len(steps) + 2 else None
                    for s in range(2):
                        if k < len(steps):
                            exponentials(k, s)
                        if turned and s < len(turned[2]):
                            copy_probs(turned, turned[2][s])
                    if k < len(steps):
                        step_tiles.append((step_tiles[-1] if step_tiles else tiles0) + len(steps[k][2]))
                    if k == 0:
                        for c in range(WC):
                            t.wait("conv_pw")
                            act.activation(z[:, 2 * c, 0:n], (turn, outs)[c][:, 0:n], ACT.Identity,
                                           bias=cvecs[:, layer, 3, c:c + 1]).then_inc(sems["conv_out"], 1)
                    if k == norm_at:
                        t.wait("head_sum")
                        act.activation(hid_buf[:, 0:n], turn[:, 0:n], ACT.Sqrt, bias=eps_t[:, 0:1], scale=1.0 / DH).then_inc(sems["head_sqrt"], 1)
                    if k == copy_at:
                        copy_out(copy_chunk)
                        if copy_chunk < 6:
                            t.wait("head_out")
                            act.activation(act_buf[:, 0:n], mixed[copy_chunk][:, 0:n], ACT.Square).then_inc(sems["head_sq"], 1)
                            norm_at = k + 1
                        else:
                            t.skip("head_out")
                    if turned and turned[4]:
                        head[0] += 1
                        if turned[1] % 2:
                            copy_at, copy_chunk = k + spread[head[0] - 1] + 1, (4 if turned[0] == "diff" else 6) + turned[1] // 2
                copy_out(copy_chunk)
                t.wait("head_out")
                t.wait("head_norm", 2 * n // CTX)
                t.wait("pool_out", WC)
                t.wait("conv_out", WC)
                for m in range(DC):
                    act.activation(y_hi[:, m, 0:n], mixed[m][:, 0:n], ACT.Copy).then_inc(sems["y_hi"], 1)
                y_made[0] += DC

            for p, (b0, mods) in zip(PHASES, MOD_PLAN):
                if p.name == "up":
                    up(p, mods)
                elif p.name == "down":
                    down(p, mods, squares=p.group == 1)
                    if p.group == 1:
                        norm_tail(p.tokens)
                        if p.half == 0:
                            make_y(p.layer, 1, TOK)
                        elif p.layer + 1 < LAYERS:
                            make_y(p.layer + 1, 0, TOK)
                elif p.name == "mix_in":
                    mix_in(p)
                    mixer(p.layer)
                else:
                    down(p, 0, squares=True)
                    norm_tail(p.tokens)
                    make_y(p.layer, 2, p.tokens)

        @block.vector
        def _(dve):
            t = Tally(dve, sems)
            y_made, ssq_made, squares_made, hidden = [0], [0], [0], [0]

            def split_lo(p, i, s, ahead):
                kc = ahead
                if not kc:
                    return
                dve.wait_ge(sems["split_hi"], 2 * i + (p.first + s + 3))
                dve.tensor_tensor(w_lo[s][:, 0:kc, :], raw[s][:, 0:kc, :], w_hi[s][:, 0:kc, :].bitcast(F32),
                                  ALU.subtract).then_inc(sems["split_lo"], 1)

            def mod_block(b):
                dve.wait_ge(sems["mod_raw"], 16 * b - 16 * (MOD_FIRST - 1))
                if not isinstance(b, int) or b > MOD_FIRST:
                    dve.wait_ge(sems["mod_sum"], b - (MOD_FIRST - 1))
                for k in range(DC):
                    for tok in range(2):
                        c = cact[:, tok, k:k + 1]
                        if k:
                            dve.wait_ge(sems["mod_step"], MOD_STEPS * b + (2 * k + tok - 1 - MOD_STEPS * MOD_FIRST))
                        if k == 0:
                            ins = dve.tensor_scalar(mod_acc[:, tok, :], mod_raw[:, k, :], c, None, ALU.mult)
                        else:
                            ins = dve.scalar_tensor_tensor(mod_acc[:, tok, :], mod_raw[:, k, :], c, mod_acc[:, tok, :],
                                                           ALU.mult, ALU.add)
                        ins.then_inc(sems["mod_step"], 1)

            def mod_finish(b):
                dve.wait_ge(sems["mod_sum"], b - (MOD_FIRST - 2))
                dve.tensor_tensor(mod_vec[:, :, bass.ds(2 * b, 2)], mod_ps[:, :, :, 0],
                                  mod_bias[:, :, bass.ds(2 * b, 2)].to_broadcast([P, 2, 2]),
                                  ALU.add).then_inc(sems["mod_vec"], 1)

            def add_squares(m_first, s, tokens, made):
                if m_first:
                    dve.tensor_copy(ssq[:, 0:tokens], sq[s][:, 0:tokens]).then_inc(sems["sum_squares"], 1)
                else:
                    dve.wait_ge(sems["sum_squares"], made)
                    dve.tensor_tensor(ssq[:, 0:tokens], ssq[:, 0:tokens], sq[s][:, 0:tokens], ALU.add).then_inc(sems["sum_squares"], 1)

            def norm_tail(tokens):
                t.wait("norm_sqrt")
                dve.reciprocal(rstd[:, 0:tokens], rstd[:, 0:tokens]).then_inc(sems["rstd"], 1)
                t.wait("rstd")

            def mods_ready(layer, i):
                dve.wait_ge(sems["mod_vec"], (mod_chunk(layer, i) + DC) // 2)

            def make_y(layer, norm, tokens):
                mods_ready(layer, 3 * norm + 1)
                a = mod_chunk(layer, 3 * norm + 1)
                for tok in range(2):
                    ins = dve.scalar_tensor_tensor(scale1[:, tok, :], mod_vec[:, tok, a:a + DC], 1.0,
                                                   gain[:, 3 * layer + norm, :], ALU.add, ALU.mult)
                ins.then_inc(sems["scale_ready"], 1)
                parts = len(kinds(tokens))
                for m in range(DC + 1):
                    if m < DC:
                        if m >= 2:
                            t.wait("affine", parts)
                        dve.tensor_tensor(sq[m % 2][:, 0:tokens], x[:, m, 0:tokens], rstd[:, 0:tokens], ALU.mult).then_inc(sems["normed"], 1)
                    if m:
                        t.wait("y_hi")
                        buf = (act_buf, hid_buf)[(m - 1) % 2]
                        dve.tensor_tensor(y_lo[:, m - 1, 0:tokens], buf[:, 0:tokens], y_hi[:, m - 1, 0:tokens].bitcast(F32),
                                          ALU.subtract).then_inc(sems["y_lo"], 1)
                t.skip("affine", 2 * parts)
                y_made[0] += DC

            def up(p, b0, mods):
                n = p.tokens
                pair0 = p.first // 2
                h0 = hidden[0]

                def body(i, ahead, with_mod):
                    if with_mod:
                        mod_block(b0 + i)
                    split_lo(p, i, 0, ahead)
                    dve.wait_ge(sems["unit_done"], 2 * i + (p.first + 2))
                    dve.wait_ge(sems["slot_free0"], i + (pair0 + 1))
                    if h0 or not isinstance(i, int) or i:
                        dve.wait_ge(sems["hidden_lo"], i + h0)
                    else:
                        dve.wait_ge(sems["y_lo"], y_made[0])
                    dve.tensor_tensor(hid_buf[:, 0:n], act_buf[:, 0:n], slot[1][:, 0:n], ALU.mult).then_inc(sems["slot_free1"], 1)
                    split_lo(p, i, 1, ahead)
                    dve.wait_ge(sems["hidden_hi"], i + (h0 + 1))
                    dve.tensor_tensor(h_lo[:, i, 0:n], hid_buf[:, 0:n], h_hi[:, i, 0:n].bitcast(F32), ALU.subtract).then_inc(sems["hidden_lo"], 1)
                    if with_mod:
                        mod_finish(b0 + i)

                for a, b, with_mod in segments(p.pairs, mods):
                    if b - a == 1:
                        body(a, p.kc if b < p.pairs else p.next_kc, with_mod)
                    else:
                        with loop(dve, a, b) as i:
                            body(i, p.kc, with_mod)
                hidden[0] += p.pairs

            def down(p, b0, mods, squares, gate):
                n = p.tokens
                s0, q0 = ssq_made[0], squares_made[0]
                mods_ready(p.layer, gate)
                a = mod_chunk(p.layer, gate)
                if p.group == 0:
                    dve.tensor_scalar(gates[:, :, :], mod_vec[:, :, a:a + DC], 1.0 if p.name == "mix_out" else 0.5, None,
                                      ALU.mult).then_inc(sems["gates_ready"], 1)
                    t.wait("gates_ready")

                def body(i, ahead, with_mod, first, last):
                    if with_mod:
                        mod_block(b0 + i)
                    for s in range(2):
                        dve.wait_ge(sems["unit_done"], 2 * i + (p.first + s + 1))
                        for k, (lo, hi) in kinds(n):
                            ins = dve.scalar_tensor_tensor(x[:, 2 * i + s, lo:hi], slot[s][:, lo:hi],
                                                           gates[:, k, bass.ds(2 * i + s, 1)], x[:, 2 * i + s, lo:hi],
                                                           ALU.mult, ALU.add)
                        ins.then_inc(sems[slot_free[s]], 1)
                        split_lo(p, i, s, ahead)
                        if squares and not (last and s == 1):
                            dve.wait_ge(sems["square"], 2 * i + (q0 + s + 1))
                            add_squares(first and s == 0, s, n, 2 * i + (s0 + s))
                    if with_mod:
                        mod_finish(b0 + i)

                for lo_i, hi_i, with_mod in segments(p.pairs, mods):
                    if hi_i - lo_i == 1:
                        body(lo_i, p.kc if hi_i < p.pairs else p.next_kc, with_mod, lo_i == 0, hi_i == p.pairs)
                    else:
                        with loop(dve, lo_i, hi_i) as i:
                            body(i, p.kc, with_mod, False, False)
                if squares:
                    ssq_made[0] += DC - 1
                    squares_made[0] += DC

            def mix_in(p):
                layer = p.layer
                t.n["zeros"] = layer
                taps = [0]
                with_ctx = layer < LAYERS - 1
                conv_out = CONV_OUT if with_ctx else LAT

                def convolve(n):
                    for _ in range(n):
                        if taps[0] == WC * CONV_K:
                            return
                        k, c = divmod(taps[0], WC)
                        src = conv_u[:, c, k:k + conv_out]
                        w = ctaps[:, layer, c, k:k + 1]
                        if k == 0:
                            ins = dve.tensor_scalar(conv_acc[c][:, 0:conv_out], src, w, cvecs[:, layer, 0, c:c + 1], ALU.mult, ALU.add)
                        else:
                            dve.wait_ge(sems["conv_acc"], layer * WC * CONV_K + taps[0] - 1)
                            ins = dve.scalar_tensor_tensor(conv_acc[c][:, 0:conv_out], src, w, conv_acc[c][:, 0:conv_out], ALU.mult, ALU.add)
                        ins.then_inc(sems["conv_acc"], 1)
                        taps[0] += 1

                def rope(chunk, table):
                    half = DIFF_DH // 4
                    part = z[:, chunk, 0:LAT]
                    dve.stream_shuffle(sq[0][:, 0:LAT], part, [d ^ half for d in range(DIFF_DH)]).then_inc(sems["rope_step"], 1)
                    dve.tensor_tensor(sq[1][:, 0:LAT], part, rope_t[:, table, :], ALU.mult).then_inc(sems["rope_step"], 1)
                    t.wait("rope_step", 2)
                    dve.tensor_tensor(sq[0][:, 0:LAT], sq[0][:, 0:LAT], rope_t[:, table + 1, :], ALU.mult).then_inc(sems["rope_step"], 1)
                    t.wait("rope_step")
                    dve.tensor_tensor(part, sq[1][:, 0:LAT], sq[0][:, 0:LAT], ALU.add).then_inc(sems["rope_step"], 1)
                    t.wait("rope_step")

                def copied(u):
                    dve.wait_ge(sems[slot_free[u % 2]], p.first // 2 + u // 2 + 1)

                dve.memset(conv_u[:, :, :], 0.0).then_inc(sems["zeros"], 1)
                t.wait("zeros")
                for u in range(Z_UNITS):
                    split_lo(p, u // 2, u % 2, p.kc if u < Z_UNITS - 2 else p.next_kc)
                    if u == 3:
                        copied(2)
                        copied(3)
                        for c in range(WC):
                            for kind, (a, b) in kinds(TOK if with_ctx else LAT):
                                at = a + HALO * (kind + 1)
                                dve.tensor_tensor(conv_u[:, c, at:at + b - a], z[:, CONV_A + c, a:b],
                                                  z[:, CONV_G + c, a:b], ALU.mult).then_inc(sems["conv_u"], 1)
                        t.wait("conv_u", WC * (1 + with_ctx))
                    if u >= 3:
                        convolve(6)
                    if u == 15:
                        t.wait("rope_tables", 16)
                        copied(DIFF_K)
                        copied(DIFF_K + 1)
                        for c in range(WC):
                            rope(DIFF_Q + c, 0)
                            if with_ctx:
                                dve.tensor_scalar(z[:, DIFF_Q + c, LAT:TOK], z[:, DIFF_Q + c, LAT:TOK], DIFF_DH ** -0.5, None,
                                                  ALU.mult).then_inc(sems["rope_step"], 1)
                                t.wait("rope_step")
                    if u == 16:
                        for c in range(WC):
                            rope(DIFF_K + c, 2)
                    if u == 17:
                        copied(NA_Q)
                        copied(NA_Q + 1)
                        for c in range(WC):
                            nq = TOK if with_ctx else LAT
                            ins = dve.tensor_scalar(z[:, NA_Q + c, 0:nq], z[:, NA_Q + c, 0:nq], DH ** -0.5, None, ALU.mult)
                        ins.then_inc(sems["rope_done"], 1)

            def mixer(layer):
                with_ctx = layer < LAYERS - 1
                n = TOK if with_ctx else LAT
                for k in range(2):
                    dve.tensor_tensor(sq[0][:, DIFF_DH * k:DIFF_DH * k + DIFF_DH], lam_rows[:, layer, 2 * k, :],
                                      lam_rows[:, layer, 2 * k + 1, :], ALU.mult).then_inc(sems["lam_step"], 1)
                t.wait("lam_step", 2)
                dve.tensor_reduce(lam[:, 0:2], sq[0][:, 0:2 * DIFF_DH].rearrange("p (a b) -> p a b", a=2), AX_X,
                                  ALU.add).then_inc(sems["lam_in"], 1)
                t.wait("lam_exp")
                dve.tensor_tensor(lam[:, 4:5], lam[:, 3:4], lam[:, 2:3], ALU.subtract).then_inc(sems["lam_step"], 1)
                t.wait("lam_step")
                dve.tensor_scalar(lam[:, 5:6], lam[:, 4:5], -lam_init(layer), None, ALU.add).then_inc(sems["lam_step"], 1)
                dve.tensor_scalar(lam[:, 6:7], sub_g[:, layer:layer + 1], 1.0 - lam_init(layer), None, ALU.mult).then_inc(sems["lam_step"], 1)
                t.wait("lam_step", 2)

                def copy_values(k):
                    dve.wait_ge(sems["v_turned"], layer * (TOK // P) + k + 1)
                    dve.tensor_copy(v_sb[:, k, :], turn[:, 512:1024]).then_inc(sems["v_ready1"], 1)

                copy_values(1)
                t.wait("conv_mean")
                for c in range(WC):
                    for (a, b), at in zip(spans(n), (CONV_LAT, CONV_CTX)):
                        ins = dve.scalar_tensor_tensor(sq[c][:, a:b], outs[:, a:b], -1.0 / W, conv_acc[c][:, at], ALU.mult, ALU.add)
                    ins.then_inc(sems["conv_cent"], 1)
                copy_values(3)
                copy_values(5)
                t.wait("conv_sqrt")
                dve.reciprocal(rstd[:, 0:n], rstd[:, 0:n]).then_inc(sems["conv_rstd"], 1)
                t.wait("conv_rstd")
                for c in range(WC):
                    dve.tensor_tensor(sq[c][:, 0:n], sq[c][:, 0:n], rstd[:, 0:n], ALU.mult).then_inc(sems["conv_norm"], 1)

                steps = attention_steps(with_ctx)
                norm_due = norm_at = None
                spread = value_steps(with_ctx)

                def maxima(k, s):
                    kind, h, tiles, ctx, _ = steps[k]
                    keys = slice(LAT, TOK) if ctx else slice(0, TOK)
                    e = (k % 2) * 2 + s
                    t.wait("scores")
                    dve.tensor_reduce(nmax[:, e:e + 1], slot[s][:, keys], AX_X, ALU.max,
                                      negate=True).then_inc(sems["neg_max"], 1)

                def invert_sums(k):
                    e0 = (k % 2) * 2
                    t.wait("exp", 2)
                    if k >= 2 or layer:
                        dve.wait_ge(sems["half_scaled"], scores_before(layer) // 2 + k - 1)
                    if steps[k][0] == "diff":
                        dve.reciprocal(rsum[:, e0:e0 + 2], esum[:, e0:e0 + 2]).then_inc(sems["stat"], 1)
                        t.wait("stat")
                        dve.tensor_scalar(nrsum[:, e0:e0 + 1], rsum[:, e0 + 1:e0 + 2], lam[:, 5:6], None,
                                          ALU.mult).then_inc(sems["sums_inverted"], 1)
                        t.skip("sums_inverted")
                    else:
                        dve.reciprocal(rsum[:, e0:e0 + 2], esum[:, e0:e0 + 2]).then_inc(sems["sums_inverted"], 1)
                        t.wait("sums_inverted")

                def scale_probs(k):
                    kind, h, tiles, ctx, _ = steps[k]
                    keys = slice(LAT, TOK) if ctx else slice(0, TOK)
                    e0 = (k % 2) * 2
                    if kind == "diff":
                        dve.wait_ge(sems["half_scaled"], scores_before(layer) // 2 + k + 1)
                        ins = dve.scalar_tensor_tensor(e_sb[:, e0, keys], e_sb[:, e0, keys], rsum[:, e0:e0 + 1],
                                                       e_sb[:, e0 + 1, keys], ALU.mult, ALU.add)
                    else:
                        ins = dve.tensor_scalar(e_sb[:, e0, keys], e_sb[:, e0, keys], rsum[:, e0:e0 + 1], None, ALU.mult)
                    ins.then_inc(sems["probs"], 1)

                for k in range(len(steps) + 3):
                    if k < len(steps):
                        maxima(k, 0)
                    if 1 <= k <= len(steps):
                        invert_sums(k - 1)
                    if k < len(steps):
                        maxima(k, 1)
                    if 1 <= k <= len(steps):
                        scale_probs(k - 1)
                    if norm_at is not None and norm_at <= k < norm_at + n // CTX:
                        if k == norm_at:
                            t.wait("head_sqrt")
                        part = slice(CTX * (k - norm_at), CTX * (k - norm_at) + CTX)
                        dve.reciprocal(hid_buf[:, part], hid_buf[:, part]).then_inc(sems["head_rstd"], 1)
                        t.wait("head_rstd")
                        dve.scalar_tensor_tensor(mixed[norm_due][:, part], mixed[norm_due][:, part], lam[:, 6:7], hid_buf[:, part],
                                                 ALU.mult, ALU.mult).then_inc(sems["head_norm"], 1)
                    if 2 <= k < len(steps) + 2:
                        kind, h, tiles, ctx, last = steps[k - 2]
                        if last and kind == "diff" and h % 2:
                            norm_due, norm_at = 4 + h // 2, k + spread[h] + 3
                for m in range(DC):
                    t.wait("y_hi")
                    dve.tensor_tensor(y_lo[:, m, 0:n], mixed[m][:, 0:n], y_hi[:, m, 0:n].bitcast(F32), ALU.subtract).then_inc(sems["y_lo"], 1)
                y_made[0] += DC

            t.wait("cond_silu")

            def first_sums(blocks):
                for j in blocks:
                    dve.wait_ge(sems[f"mod_first{2 * j + 1}"], 16)
                    for k in range(DC):
                        for tok in range(2):
                            src, c = mod_start[:, 2 * j + 1, k, :], cact[:, tok, k:k + 1]
                            acc = mod_start_acc[:, j, tok, :]
                            if k == 0:
                                ins = dve.tensor_scalar(acc, src, c, None, ALU.mult)
                            else:
                                dve.wait_ge(sems["first_step"], MOD_STEPS * j + 2 * k + tok - 1)
                                ins = dve.scalar_tensor_tensor(acc, src, c, acc, ALU.mult, ALU.add)
                            ins.then_inc(sems["first_step"], 1)

            first_sums(range(1))
            dve.wait_ge(sems["x_in"], 16)
            for m in range(DC - 1):
                dve.wait_ge(sems["square"], m + 1)
                add_squares(m == 0, m % 2, TOK, m)
            ssq_made[0] += DC - 1
            squares_made[0] += DC
            first_sums(range(1, 2))
            norm_tail(TOK)
            first_sums(range(2, MOD_FIRST // 2))
            dve.wait_ge(sems["inputs"], 16 * 11)
            for s in range(2):
                dve.wait_ge(sems["split_hi"], s + 1)
                dve.tensor_tensor(w_lo[s][:, 0:DC, :], raw[s][:, 0:DC, :], w_hi[s][:, 0:DC, :].bitcast(F32), ALU.subtract).then_inc(sems["split_lo"], 1)
            dve.wait_ge(sems["mod_sum"], 1)
            for tok in range(2):
                dve.tensor_tensor(mod_vec[:, tok, 0:2 * DC], mod_start_ps[:, :, tok], mod_bias[:, 0, 0:2 * DC],
                                  ALU.add).then_inc(sems["mod_vec"], MOD_FIRST // 2)
            make_y(0, 0, TOK)

            for p, (b0, mods) in zip(PHASES, MOD_PLAN):
                if p.name == "up":
                    up(p, b0, mods)
                elif p.name == "down":
                    down(p, b0, mods, squares=p.group == 1, gate=2 if p.half == 0 else 8)
                    if p.group == 1:
                        norm_tail(p.tokens)
                        if p.half == 0:
                            make_y(p.layer, 1, TOK)
                        elif p.layer + 1 < LAYERS:
                            make_y(p.layer + 1, 0, TOK)
                elif p.name == "mix_in":
                    mix_in(p)
                    mixer(p.layer)
                else:
                    down(p, 0, 0, squares=True, gate=5)
                    norm_tail(p.tokens)
                    make_y(p.layer, 2, p.tokens)
            for m in range(DC):
                dve.scalar_tensor_tensor(o_final[:, m, :], x[:, m, 0:LAT], gain_f[:, m:m + 1], rstd[:, 0:LAT],
                                         ALU.mult, ALU.mult).then_inc(sems["final"], 1)

        @block.tensor
        def _(pe):
            t = Tally(pe, sems)
            y_made, hidden, ssq_made, squares_made = [0], [0], [0], [0]

            def product(s, k, kc, rhs_hi, rhs_lo, tokens):
                for n, (w, r) in enumerate(((w_hi, rhs_hi), (w_lo, rhs_hi), (w_hi, rhs_lo))):
                    for a, b in spans(tokens):
                        mm = pe.matmul(slot[s][:, a:b], w[s][:, k, :], r[:, k, a:b],
                                       start=(k == 0 and n == 0), stop=(k == kc - 1 and n == 2))
                if k == kc - 1:
                    mm.then_inc(sems["unit_done"], 1)

            def mod_reduce(b):
                pe.wait_ge(sems["mod_parts"], b - (MOD_FIRST - 1))
                for tok in range(2):
                    for c in range(MOD_COLS // P):
                        for part in (mod_hi, mod_lo):
                            mm = pe.matmul(mod_ps[:, tok, c, :], part[:, tok, P * c:P * c + P], one_r[:, :],
                                           start=(part is mod_hi), stop=(part is mod_lo))
                mm.then_inc(sems["mod_sum"], 1)

            def norm_reduce(tokens):
                ssq_made[0] += DC - 1
                squares_made[0] += DC
                for src, last in ((ssq, False), (sq[1], True)):
                    pe.wait_ge(sems["square" if last else "sum_squares"], (squares_made if last else ssq_made)[0])
                    for a, b in spans(tokens):
                        mm = pe.matmul(turn[:, a:b], ones[:, :], src[:, a:b], start=not last, stop=last)
                mm.then_inc(sems["norm_sum"], 1)

            def run(p, b0, mods, rhs_hi, rhs_lo, ready, made):
                pair0 = p.first // 2
                follows_norm = p.name == "mix_in" or p.name == "up" and p.group == 0

                def body(i, first, with_mod, tokens):
                    def unit_ready(s):
                        pe.wait_ge(sems["split_lo"], 2 * i + (p.first + s + 1))
                        if pair0 or not first:
                            pe.wait_ge(sems[slot_free[s]], i + pair0)

                    lag = LAG if first and follows_norm else p.kc
                    for step in range(lag + p.kc):
                        for s, k in ((0, step), (1, step - lag)):
                            if 0 <= k < p.kc:
                                if k == 0:
                                    unit_ready(s)
                                if first and s == 0:
                                    pe.wait_ge(sems[ready], made + k + 1)
                                product(s, k, p.kc, rhs_hi, rhs_lo, tokens)
                    if with_mod:
                        mod_reduce(b0 + i)

                if p.name == "mix_in":
                    parts = [(a, b, False, tokens) for a, b, tokens in z_segments(p.layer)]
                else:
                    parts = [(a, b, with_mod, p.tokens) for a, b, with_mod in segments(p.pairs, mods)]
                for a, b, with_mod, tokens in parts:
                    if b - a == 1:
                        body(a, a == 0, with_mod, tokens)
                    else:
                        with loop(pe, a, b) as i:
                            body(i, False, with_mod, tokens)

            def mixer(layer):
                with_ctx = layer < LAYERS - 1
                n = TOK if with_ctx else LAT
                pairs_done = unit_pairs(layer, "mix_in") + Z_UNITS // 2
                for s in range(2):
                    pe.wait_ge(sems[slot_free[s]], pairs_done)
                for k in range(TOK // P):
                    if k >= 2:
                        t.wait(("v_ready0", "v_ready1")[k % 2])
                    for c in range(2 * WC):
                        src = z[:, (DIFF_V, DIFF_V + 1, NA_V, NA_V + 1)[c], P * k:P * k + P]
                        mm = pe.transpose(turn[:, 512 * (k % 2) + P * c:512 * (k % 2) + P * c + P], src, ident[:, :])
                    mm.then_inc(sems["v_turned"], 1)
                    if k == 1:
                        pe.wait_ge(sems["conv_acc"], (layer + 1) * WC * CONV_K)
                        for (a, b), at in zip(spans(n), (CONV_LAT, CONV_CTX)):
                            for c in range(WC):
                                mm = pe.matmul(outs[:, a:b], ones[:, :], conv_acc[c][:, at], start=(c == 0), stop=(c == WC - 1))
                        mm.then_inc(sems["conv_mean"], 1)
                t.wait("conv_sq", WC)
                for a, b in spans(n):
                    for c in range(WC):
                        mm = pe.matmul(outs[:, a:b], ones[:, :], (act_buf, hid_buf)[c][:, a:b], start=(c == 0), stop=(c == WC - 1))
                mm.then_inc(sems["conv_var"], 1)
                t.wait("mixer_weights", 16 * 5)
                for c in range(WC):
                    t.wait("pool_d")
                    for a, b in spans(n):
                        mm = pe.matmul(slot[c][:, a:b], pool_sb[:, c, :], z[:, POOL_U + c, a:b], start=True, stop=True)
                    mm.then_inc(sems["pool_mm"], 1)

                def conv_pointwise():
                    t.wait("v_ready0")
                    t.wait("v_ready1")
                    t.wait("conv_act", WC)
                    for m in range(WC):
                        for a, b in spans(n):
                            for c in range(WC):
                                mm = pe.matmul((turn, outs)[m][:, a:b], pw_sb[:, c, P * m:P * m + P], sq[c][:, a:b],
                                               start=(c == 0), stop=(c == WC - 1))
                        mm.then_inc(sems["conv_pw"], 1)

                def scores(k, s):
                    kind, h, tiles, ctx, _ = steps[k]
                    if k:
                        t.wait("exp")
                    else:
                        t.wait("pool_out")
                    if kind == "diff":
                        tile = tiles[0]
                        if tile == 0 and not ctx and s == 0:
                            pe.wait_ge(sems[f"stacked{h % 2}"], 16 * 12 * (2 * layer + h // 2 + 1))
                    else:
                        rows = slice(DH * (h % 2), DH * (h % 2) + DH)
                        q, key, tile = NA_Q + h // 2, NA_K + h // 2, tiles[s]
                    at = (LAT if ctx else 0) + P * tile
                    band = kind == "na" and not ctx
                    for a, b in spans(TOK)[1 if ctx else 0:]:
                        if kind == "diff":
                            mm = pe.matmul(slot[s][:, a:b], stacks[h][s][0:3 * DIFF_DH, at:at + P],
                                           stacks[h][2 + s][0:3 * DIFF_DH, a:b], start=True, stop=True)
                        else:
                            mm = pe.matmul(slot[s][:, a:b], z[rows, q, at:at + P], z[rows, key, a:b],
                                           start=True, stop=not (band and a == 0))
                    if band:
                        if tile == 0:
                            t.wait("band_ready")
                        j = GRID_H - 2 - 2 * tile
                        mm = pe.matmul(slot[s][:, 0:LAT], backward[:, :], bands[h][:, j:j + GRID_H, :], start=False, stop=True)
                    mm.then_inc(sems["scores"], 1)

                steps = attention_steps(with_ctx)
                pe.wait_ge(sems["rope_done"], layer + 1)
                heads, norm_at, sqrt_at, pv_from = 0, None, None, None
                spread = value_steps(with_ctx)
                tiles_turned = turned_before(layer)

                def transpose_probs(k, s):
                    kind, h, tiles, ctx, _ = steps[k]
                    if s == 0:
                        t.wait("probs")
                    else:
                        pe.wait_ge(sems["half_scaled"], scores_before(layer) // 2 + k + 1)
                    if tiles_turned:
                        pe.wait_ge(sems["probs_t"], tiles_turned)
                    e = (k % 2) * 2 + s
                    for n_key, key in enumerate(range(LAT // P if ctx else 0, TOK // P)):
                        mm = pe.transpose(turn[:, P * n_key:P * n_key + P], e_sb[:, e, P * key:P * key + P], ident[:, :])
                    mm.then_inc(sems["turned"], 1)

                for k in range(len(steps) + 3):
                    turned = steps[k - 2] if 2 <= k < len(steps) + 2 else None
                    for s in range(2):
                        if k < len(steps):
                            scores(k, s)
                        if turned and s < len(turned[2]):
                            if k == 2 and s == 0:
                                t.wait("conv_out", WC)
                            if k == sqrt_at and s == 0:
                                t.wait("head_sqrt")
                            transpose_probs(k - 2, s)
                            tiles_turned += 1
                    if k == 0:
                        conv_pointwise()
                    if k == norm_at:
                        t.wait("head_sq")
                        pe.wait_ge(sems["probs_t"], tiles_turned)
                        for a, b in spans(n):
                            mm = pe.matmul(turn[:, a:b], pairsum[:, :], act_buf[:, a:b], start=True, stop=True)
                        mm.then_inc(sems["head_sum"], 1)
                        sqrt_at = k + 1
                    if pv_from is not None and pv_from <= k < pv_from + spread[heads]:
                        kind, h = pv_head
                        if k == pv_from:
                            pe.wait_ge(sems["probs_t"], pv_tiles)
                            if h % 2 == 0 and heads:
                                t.wait("head_out")
                        rows = slice(DH * (h % 2), DH * (h % 2) + DH)
                        col = (0 if kind == "diff" else W) + DH * h
                        products = [(key, False) for key in range(TOK // P)]
                        products += [(key, True) for key in range(LAT // P, TOK // P)] * with_ctx
                        share = -(-len(products) // spread[heads])
                        for key, of_ctx in products[share * (k - pv_from):share * (k - pv_from + 1)]:
                            if of_ctx:
                                n_key = key - LAT // P
                                mm = pe.matmul(outs[rows, LAT:TOK], v_sb[:, key, col:col + DH], ctx_probs[heads % 2][:, n_key, :],
                                               start=(n_key == 0), stop=(key == TOK // P - 1))
                            else:
                                mm = pe.matmul(outs[rows, 0:LAT], v_sb[:, key, col:col + DH], probs_t[:, heads % 2, key, :],
                                               start=(key == 0), stop=(key == TOK // P - 1))
                        if k == pv_from + spread[heads] - 1:
                            mm.then_inc(sems["pv"], 1)
                            heads += 1
                            pv_from = None
                            if kind == "diff" and h % 2:
                                norm_at = k + 2
                    if turned and turned[4]:
                        pv_head, pv_tiles, pv_from = turned[0:2], tiles_turned, k + 1
                t.wait("head_out")
                t.skip("exp", 2)
                pe.wait_ge(sems["exp"], t.n["exp"])

            t.wait("cond_silu")
            for b in range(0, MOD_FIRST, 2):
                if b == MOD_FIRST // 2:
                    t.wait("const_rows", 4)
                    norm_reduce(TOK)
                pe.wait_ge(sems[f"mod_first{b}"], 16)
                for c in range(MOD_COLS // P):
                    for k in range(DC):
                        mm = pe.matmul(mod_start_ps[:, MOD_COLS // P * b + c, :], mod_start[:, b, k, P * c:P * c + P],
                                       cact[:, :, k], start=(k == 0), stop=(k == DC - 1))
            t.wait("inputs", 16 * 11)
            for j in range(MOD_FIRST // 2):
                pe.wait_ge(sems["first_step"], MOD_STEPS * (j + 1))
                for tok in range(2):
                    for c in range(MOD_COLS // P):
                        mm = pe.matmul(mod_start_ps[:, MOD_COLS // P * (2 * j + 1) + c, tok:tok + 1],
                                       mod_start_acc[:, j, tok, P * c:P * c + P], ones[:, 0:1], start=True, stop=True)
            mm.then_inc(sems["mod_sum"], 1)
            y_made[0] += DC

            for p, (b0, mods) in zip(PHASES, MOD_PLAN):
                if p.name in ("up", "mix_in", "mix_out"):
                    if p.name != "up" or p.group == 0:
                        made = y_made[0] - DC
                    run(p, b0, mods, y_hi, y_lo, "y_lo", made)
                    if p.name == "mix_in":
                        mixer(p.layer)
                        y_made[0] += DC
                    if p.name == "mix_out":
                        norm_reduce(p.tokens)
                        y_made[0] += DC
                    if p.name == "up":
                        hidden[0] += p.pairs
                else:
                    run(p, b0, mods, h_hi, h_lo, "hidden_lo", hidden[0] - FG)
                    if p.group == 1:
                        norm_reduce(p.tokens)
                        y_made[0] += DC



def _feature_major(a):
    a = a.reshape(a.shape[:-1] + (-1, P))
    return np.ascontiguousarray(np.moveaxis(a, -1, 0))


def _weight_units(w, groups=1):
    rows, cols = w.shape
    return w.reshape(groups, rows // groups // P, P, cols // P, P).transpose(0, 3, 2, 1, 4)


def _constants():
    pairsum = np.kron(np.eye(2), np.ones((DH, DH))).astype(np.float32)
    backward = np.kron(np.eye(2), np.eye(GRID_W)[::-1]).astype(np.float32)
    consts = np.stack([np.eye(P, dtype=np.float32), pairsum, backward])
    nf = DIFF_DH // 4
    inv = np.power(np.float32(10000.0), -np.arange(nf, dtype=np.float32) / np.float32(nf)).astype(np.float32)
    tok = np.arange(LAT)
    d = np.arange(P) % DIFF_DH
    pos = np.where((d // (2 * nf) == 0)[:, None], tok // GRID_W, tok % GRID_W).astype(np.float32)
    ang = (pos * inv[d % nf][:, None]).astype(np.float32)
    sign = np.where((d // nf) % 2 == 0, -1.0, 1.0)[:, None].astype(np.float32)
    cos, sin = np.cos(ang), np.sin(ang) * sign
    scale = np.float32(DIFF_DH ** -0.5)
    rope = np.stack([cos * scale, sin * scale, cos, sin], 1).astype(np.float32)
    inv_w = np.empty((P, WC, TOK), np.float32)
    for g, w in enumerate(POOL_WINDOWS):
        for a, n in ((0, LAT), (LAT, CTX)):
            q = np.arange(n)
            size = np.clip(q + w - w // 2, 0, n) - np.clip(q - w // 2, 0, n)
            inv_w[DH * (g % 2):DH * (g % 2) + DH, g // 2, a:a + n] = np.float32(1) / size.astype(np.float32)
    q = GRID_W - 1 - np.arange(P) % GRID_W
    c0 = np.clip(q - NA_COLS // 2, 0, GRID_W - NA_COLS)[:, None]
    k = np.arange(GRID_W)[None]
    valid = (k >= c0) & (k < c0 + NA_COLS)
    masks = np.stack([valid.astype(np.float32), np.where(valid, 0.0, -1e30).astype(np.float32)], 1)
    return consts, rope, inv_w, masks


def _layout(x, c, ctx, c_ctx, w_mod, b_mod, g_norm, ffn_in, ffn_out, w_in, w_out, pool_w, pool_scale,
            conv_dw, conv_dw_b, conv_ln_g, conv_ln_b, conv_pw, conv_pw_b, diff_lambda, diff_subln_g,
            na_rpb, g_final):
    tokens = np.concatenate([x[0], ctx[0]], 0)
    consts, rope, pool_inv, masks = _constants()
    z_cols = np.concatenate([np.arange(a, a + W) for a in Z_COLUMNS])
    up = [[_weight_units(ffn_in[l, f]).reshape(2, FC, P, DC, P).transpose(1, 0, 2, 3, 4) for f in range(2)]
          for l in range(LAYERS)]
    bias = _feature_major(b_mod.reshape(-1))
    arrays = {
        "xT": tokens.T.reshape(DC, P, TOK).transpose(1, 0, 2),
        "cond": _feature_major(np.stack([c[0], c_ctx])),
        "w_mod": w_mod.reshape(LAYERS, DC, P, MOD_BLOCKS, MOD_COLS).transpose(0, 3, 2, 1, 4).reshape(MOD_ALL, P, DC, MOD_COLS),
        "b_mod": bias[:, None],
        "gains": _feature_major(g_norm.reshape(LAYERS * 3, D)),
        "g_final": _feature_major(g_final),
        "w_up": np.stack([np.stack(u) for u in up]),
        "w_down": np.stack([np.stack([_weight_units(ffn_out[l, f], 2) for f in range(2)]) for l in range(LAYERS)]),
        "w_in": np.stack([_weight_units(w_in[l][:, z_cols])[0] for l in range(LAYERS)]),
        "w_out": np.stack([_weight_units(w_out[l])[0] for l in range(LAYERS)]),
        "pool_w": pool_w,
        "conv_pw": conv_pw.reshape(LAYERS, WC, P, W).transpose(0, 2, 1, 3),
        "conv_vec": _feature_major(np.stack([conv_dw_b, conv_ln_g, conv_ln_b, conv_pw_b, pool_scale], 1)),
        "conv_taps": conv_dw.reshape(LAYERS, CONV_K, WC, P).transpose(3, 0, 2, 1),
        "lam_in": diff_lambda,
        "subln": np.concatenate([diff_subln_g, diff_subln_g], 1).T,
        "rpb": np.pad(na_rpb.reshape(-1), RPB_PAD),
        "consts": consts, "rope": rope, "pool_inv": pool_inv, "masks": masks,
    }
    return {k: np.ascontiguousarray(v) for k, v in arrays.items()}


def kernel(**inputs):
    import concourse.bacc as bacc
    from concourse.bass_utils import run_bass_kernel_spmd

    arrays = _layout(**{k: np.asarray(v) for k, v in inputs.items()})
    nc = bacc.Bacc("TRN2", target_bir_lowering=False, num_devices=1)
    args = {k: nc.dram_tensor(f"in_{k}", a.shape, F32, kind="ExternalInput").ap() for k, a in arrays.items()}
    args["out"] = nc.dram_tensor("out_x", (P, DC, LAT), F32, kind="ExternalOutput").ap()
    trunk(nc, **args)
    r = run_bass_kernel_spmd(nc, [{f"in_{k}": a for k, a in arrays.items()}], core_ids=[0])
    out = np.asarray(r.results[0]["out_x"])
    return np.ascontiguousarray(out.transpose(1, 0, 2).reshape(D, LAT).T)[None]
```

```python
import math

import numpy as np

import concourse.bass as bass
from concourse import mybir

F32 = mybir.dt.float32
F32R = mybir.dt.float32r
ALU = mybir.AluOpType
ACT = mybir.ActivationFunctionType
AX_X = mybir.AxisListType.X

P = 128
D = 1024
LAYERS = 2
LAT = 512
CTX = 256
TOK = LAT + CTX
DC = D // P
F = 2816
FC = F // P
FG = FC // 2
N_MOD = 9
GRID_W = 64
GRID_H = LAT // GRID_W
NA_COLS = 16
RPB_R = 15
RPB_C = 31
CONV_K = 31
HALO = CONV_K // 2
W = 256
WC = W // P
HEADS = 4
DH = 64
DIFF_DH = 32
EPS = 1e-6
LN_EPS = 1e-5
POOL_WINDOWS = (2, 4, 8, 16)
RPB_PAD = 64
LAG = (4, 5)

CONV_A, CONV_G, POOL_U, DIFF_Q, DIFF_K, DIFF_V, NA_Q, NA_K, NA_V = range(0, 18, 2)
Z_UNITS = 18
Z_COLUMNS = [W, 2 * W, 0, 3 * W, 4 * W, 5 * W, 6 * W, 7 * W, 8 * W]

MOD_COLS = 256
MOD_BLOCKS = N_MOD * D // MOD_COLS
MOD_ALL = LAYERS * MOD_BLOCKS
MOD_STEPS = 2 * DC
MOD_FIRST = 2 * D // MOD_COLS

CONV_LEN = HALO + LAT + HALO + CTX + HALO
CONV_OUT = LAT + HALO + CTX
CONV_LAT = slice(0, LAT)
CONV_CTX = slice(LAT + HALO, CONV_OUT)
PPAD = 8
POOL_LEN = PPAD + LAT + PPAD + CTX + PPAD
POOL_LAT0 = PPAD
POOL_CTX0 = PPAD + LAT + PPAD


class Phase:

    def __init__(self, name, layer, half, group, pairs, kc, tokens, first):
        self.name, self.layer, self.half, self.group = name, layer, half, group
        self.pairs, self.kc, self.tokens, self.first = pairs, kc, tokens, first
        self.next_kc = 0
        self.after_norm = name == "mix_in" or name == "up" and group == 0


def plan_phases():
    out, unit = [], 0

    def add(name, layer, half, group, pairs, kc, tokens):
        nonlocal unit
        p = Phase(name, layer, half, group, pairs, kc, tokens, unit)
        if out:
            out[-1].next_kc = kc
        out.append(p)
        unit += 2 * pairs

    for layer in range(LAYERS):
        last = layer == LAYERS - 1
        for half in range(2):
            tokens = LAT if last and half == 1 else TOK
            for group in range(2):
                add("up", layer, half, group, FG, DC, tokens)
                add("down", layer, half, group, DC // 2, FG, tokens)
            if half == 0:
                add("mix_in", layer, half, 0, Z_UNITS // 2, DC, TOK)
                add("mix_out", layer, half, 0, DC // 2, DC, LAT if last else TOK)
    return out


PHASES = plan_phases()


def plan_mod_blocks():
    out, block = [], MOD_FIRST
    for p in PHASES:
        n = min(p.pairs - p.after_norm, MOD_ALL - block) if p.name in ("up", "down") else 0
        out.append((block, n))
        block += n
    return out


MOD_PLAN = plan_mod_blocks()


def segments(p, mods):
    end = mods + p.after_norm
    out = [(0, 1, mods > 0 and not p.after_norm)]
    if end >= p.pairs - 1:
        out.append((1, p.pairs - 1, True))
    elif end > 1:
        out += [(1, end, True), (end, p.pairs - 1, False)]
    else:
        out.append((1, p.pairs - 1, False))
    return out + [(p.pairs - 1, p.pairs, end >= p.pairs)]


def attention_steps(with_ctx):
    out = []
    for h in range(HEADS):
        tiles = [(t, False) for t in range(LAT // P)] + [(t, True) for t in range(CTX // P)] * with_ctx
        out += [("diff", h, (t,), c, n == len(tiles) - 1) for n, (t, c) in enumerate(tiles)]
    for h in range(HEADS):
        tiles = [((0, 1), False), ((2, 3), False)] + [((0, 1), True)] * with_ctx
        out += [("na", h, t, c, n == len(tiles) - 1) for n, (t, c) in enumerate(tiles)]
    return out


def value_steps(with_ctx):
    lengths = [0] * (2 * HEADS)
    for kind, h, *_ in attention_steps(with_ctx):
        lengths[h + HEADS * (kind == "na")] += 1
    return [min(4, n) for n in lengths[1:]] + [1]


def z_segments(layer):
    if layer < LAYERS - 1:
        return [(0, 1, TOK), (1, 2, TOK), (2, Z_UNITS // 2 - 1, TOK), (Z_UNITS // 2 - 1, Z_UNITS // 2, TOK)]
    return [(0, 1, LAT), (1, 2, LAT), (2, DIFF_K // 2, LAT), (DIFF_K // 2, NA_Q // 2, TOK),
            (NA_Q // 2, NA_K // 2, LAT), (NA_K // 2, NA_V // 2, TOK), (NA_V // 2, Z_UNITS // 2, TOK)]


SEMAPHORES = [
    *(f"mod_first{b}" for b in range(MOD_FIRST)), "qk_hi", "qk_lo", "stacked0", "stacked1", "cond", "x_in", "first_step", "mod_rounded", "mod_parts", "mod_diagonal",
    "inputs", "mixer_consts", "const_rows",
    "raw_loaded0", "raw_loaded1", "split_hi", "split_lo", "unit_done", "slot_free0", "slot_free1",
    "mod_raw", "mod_sum", "mod_vec", "cond_silu", "mod_step",
    "hidden_hi", "hidden_lo", "square", "sum_squares", "norm_sum", "norm_sqrt", "rstd",
    "early_done", "updated", "normed0", "normed1", "affine", "y_hi", "y_lo", "scale_ready", "gates_ready",
    "rope_tables", "rope_step", "rope_done", "lam_in", "lam_exp", "lam_step", "lam_ready",
    "zeros", "conv_u", "conv_acc", "conv_mean", "conv_cent", "conv_sq", "conv_var", "conv_sqrt",
    "conv_rstd", "conv_norm", "conv_act", "conv_pw", "conv_out",
    "pool_step", "pool_tables", "pool_d", "pool_mm", "pool_out", "mixer_weights", "blocks_zero",
    "v_turned", "v_ready0", "v_ready1", "band_raw", "band_step", "band_ready",
    "scores", "neg_max", "exp", "stat", "sums_inverted", "probs", "half_scaled", "turned", "probs_t", "pv", "head_out",
    "head_sq", "head_sum", "head_sqrt", "head_rstd", "head_norm", "final", "out_stored",
]


class Tally:

    def __init__(self, engine, sems):
        self.engine, self.sems, self.n = engine, sems, {}

    def wait(self, name, more=1):
        self.n[name] = self.n.get(name, 0) + more
        self.engine.wait_ge(self.sems[name], self.n[name])

    def skip(self, name, more=1):
        self.n[name] = self.n.get(name, 0) + more

    def again(self, name):
        if self.n.get(name, 0):
            self.engine.wait_ge(self.sems[name], self.n[name])


def trunk(nc, xT, cond, w_mod, b_mod, gains, g_final, w_up, w_down, w_in, w_out, pool_w, conv_pw,
          conv_vec, conv_taps, lam_in, subln, rpb, consts, rope, pool_inv, masks, out):
    sems = {name: nc.alloc_semaphore(name) for name in SEMAPHORES}

    cursor = [((nc.sbuf_base + 31) // 32) * 32]

    def place(name, shape, dtype=F32, at=None):
        size = 4 * int(np.prod(shape[1:]))
        at = (at + 31) // 32 * 32 if at is not None else None
        if at is None:
            at = cursor[0]
            cursor[0] = at + (size + 31) // 32 * 32
        return nc.alloc_sbuf_tensor_at(name, shape, dtype, offset=at)

    x = place("x", [P, DC, TOK])
    raw = [place(f"w_raw{s}", [P, FG, P]) for s in range(2)]
    w_hi = [place(f"w_hi{s}", [P, FG, P], F32R) for s in range(2)]
    w_lo = [place(f"w_lo{s}", [P, FG, P], F32R) for s in range(2)]
    at_mod = cursor[0]
    mod_raw = place("mod_raw", [P, DC, MOD_COLS])
    rope_t = place("rope_t", [P, 4, LAT], at=at_mod)
    at_acc = cursor[0]
    mod_acc = place("mod_acc", [P, 2, MOD_COLS])
    mod_lo = place("mod_lo", [P, 2, MOD_COLS], F32R, at=at_acc)
    at_mod_hi = cursor[0]
    mod_hi = place("mod_hi", [P, 2, MOD_COLS], F32R)
    mod_diag = place("mod_diag", [P, 4, P], at=at_mod_hi)
    mod_out = place("mod_out", [P, 4])
    mod_vec = place("mod_vec", [P, 2, LAYERS * N_MOD * DC])
    mod_bias = place("mod_bias", [P, 1, LAYERS * N_MOD * DC])
    gain = place("gain", [P, LAYERS * 3, DC])
    gain_f = place("gain_f", [P, DC])
    cvec = place("cvec", [P, 2, DC])
    cact = place("cact", [P, 2, DC])
    scale1 = place("scale1", [P, 2, DC])
    gates = place("gates", [P, 2, DC])
    eps_t = place("eps_t", [P, 2])
    ones_r = place("ones_r", [P, P], F32R)
    ones = ones_r[:, :].bitcast(F32)
    ident = place("ident", [P, P])
    pairsum = place("pairsum", [P, P])
    backward = place("backward", [P, P])
    mask = place("mask", [P, 2, GRID_W])
    cvecs = place("cvecs", [P, LAYERS, 5, WC])
    ctaps = place("ctaps", [P, LAYERS, WC, CONV_K])
    sub_g = place("sub_g", [P, LAYERS])
    lam_rows = place("lam_rows", [P, LAYERS, 4, DIFF_DH])
    lam = place("lam", [P, 8])
    nmax = place("nmax", [P, 4])
    esum = place("esum", [P, 4])
    rsum = place("rsum", [P, 4])
    nrsum = place("nrsum", [P, 4])
    act_buf = place("act_buf", [P, TOK])
    hid_buf = place("hid_buf", [P, TOK])
    at_sq = cursor[0]
    sq = [place(f"sq{s}", [P, TOK]) for s in range(2)]
    at_rstd = cursor[0]
    rstd = place("rstd", [P, POOL_LEN])
    at_ssq = cursor[0]
    ssq = place("ssq", [P, TOK])
    pw_sb = place("pw_sb", [P, WC, W], at=at_ssq)
    pool_sb = place("pool_sb", [P, WC, P], at=at_ssq + 4 * WC * W)
    at_y = cursor[0]
    y_hi = place("y_hi", [P, DC, TOK], F32R)
    y_lo = place("y_lo", [P, DC, TOK], F32R)
    at_h = cursor[0]
    h_hi = place("h_hi", [P, FG, TOK], F32R)
    h_lo = place("h_lo", [P, FG, TOK], F32R)
    assert cursor[0] <= nc.sbuf_usable_end, cursor[0]
    mod_start = place("mod_start", [P, MOD_FIRST, DC, MOD_COLS], at=at_h)
    mod_start_acc = place("mod_start_acc", [P, MOD_FIRST // 2, 2, MOD_COLS], at=at_y)
    chunk = 4 * TOK
    at_probs1 = at_y + 12 * chunk
    v_sb = place("v_sb", [P, TOK // P, 2 * W], at=at_y + 4 * chunk)
    e_sb = place("e_sb", [P, 4, TOK], at=at_y + 8 * chunk)
    probs_t = [place(f"probs_t{b}", [P, TOK // P, LAT], at=at) for b, at in enumerate((at_y, at_probs1))]
    o_final = place("o_final", [P, DC, LAT], at=at_y)
    z = place("z", [P, Z_UNITS, TOK], at=at_h)
    conv_acc = [place(f"conv_acc{c}", [P, CONV_OUT], at=at_h + 4 * 2 * c * TOK) for c in range(WC)]
    ctx_probs = [place(f"ctx_probs{b}", [P, CTX // P, CTX], at=at_h + 4 * (1 + 2 * b) * TOK) for b in range(2)]
    at_free = at_h + 4 * Z_UNITS * TOK
    conv_u = place("conv_u", [P, WC, CONV_LEN], at=at_free)
    pool_a = place("pool_a", [P, POOL_LEN], at=at_free + 4 * WC * CONV_LEN)
    pool_b = rstd
    bands = [place(f"band{h}", [P, RPB_R - 1, GRID_W], at=at_free + h * 4 * (RPB_R - 1) * GRID_W) for h in range(3)]
    bands.append(place("band3", [P, RPB_R - 1, GRID_W], at=at_h + 4 * DIFF_Q * TOK))
    qk_lo = place("qk_lo", [P, 4, TOK], F32R, at=at_h + DIFF_Q * chunk)
    qk_hi = [place(f"qk_hi{i}", [P, TOK], F32R, at=at)
             for i, at in enumerate((at_probs1, at_h + NA_V * chunk, at_probs1 + chunk, at_h + (NA_V + 1) * chunk))]
    places = [(at_mod, at_mod + chunk, at_probs1 + 2 * chunk, at_probs1 + 3 * chunk),
              (at_sq, at_sq + chunk, at_rstd, at_ssq),
              (at_mod, at_mod + chunk, at_h + (DIFF_V + 1) * chunk, at_h + DIFF_K * chunk)]
    places.append(places[1])
    stacks = [[place(f"stack{h}{i}", [P, TOK], F32R, at=at) for i, at in enumerate(tiles)] for h, tiles in enumerate(places)]
    mixed = [z[:, POOL_U, :], z[:, POOL_U + 1, :], z[:, 0, :], z[:, 2, :],
             z[:, DIFF_V, :], z[:, DIFF_V + 1, :], z[:, NA_V, :], z[:, NA_V + 1, :]]

    ps = nc.alloc_psum_tensor("ps", [P, 8 * 512], F32)
    slot = [ps[:, 0:1024], ps[:, 1024:2048]]
    turn = ps[:, 2048:3072]
    outs = ps[:, 3072:4096]
    mod_ps = outs[:, 0:2 * MOD_COLS]
    mod_start_ps = ps[:, 3072:3072 + 4 * DC].rearrange("p (c t) -> p c t", t=2)
    slot_free = ["slot_free0", "slot_free1"]
    raw_loaded = ["raw_loaded0", "raw_loaded1"]

    def spans(tokens):
        return ((0, LAT), (LAT, TOK)) if tokens == TOK else ((0, LAT),)

    def halves(tokens):
        return ((0, LAT, 0), (LAT, TOK, 1)) if tokens == TOK else ((0, LAT // 2, 0), (LAT // 2, LAT, 0))

    def kinds(tokens):
        return tuple(enumerate(spans(tokens)))

    def next_norm(p):
        if p.name == "mix_out":
            return p.layer, 2
        if p.half == 0:
            return p.layer, 1
        return (p.layer + 1, 0) if p.layer + 1 < LAYERS else None

    def mod_chunk(layer, i):
        return (layer * N_MOD + i) * DC

    def loop(engine, a, b):
        return engine.Fori(a, b)

    def lam_init(layer):
        return 0.8 - 0.6 * math.exp(-0.3 * layer)

    def y_count(layer, norm):
        return 7 * DC * layer + 2 * DC * (norm + 1)

    def unit_pairs(layer, name):
        return next(p.first // 2 for p in PHASES if p.layer == layer and p.name == name)

    def scores_before(layer):
        return sum(2 * len(attention_steps(n < LAYERS - 1)) for n in range(layer))

    def diff_scores(layer):
        return 2 * sum(s[0] == "diff" for s in attention_steps(layer < LAYERS - 1))

    def turned_before(layer):
        return sum(sum(len(s[2]) for s in attention_steps(n < LAYERS - 1)) for n in range(layer))

    with nc.Block() as block:

        @block.sync
        def _(sp):
            def load(dst, src, name="inputs"):
                sp.dma_start(dst, src).then_inc(sems[name], 16)

            load(cvec[:, :, :], cond, "cond")
            load(mod_bias[:, :, :], b_mod)
            load(x[:, :, :], xT, "x_in")
            load(gain[:, :, :], gains)
            load(gain_f[:, :], g_final)
            load(ident[:, :], consts[0])
            load(pairsum[:, :], consts[1])
            load(backward[:, :], consts[2])
            load(mask[:, :, :], masks)
            load(cvecs[:, :, :, :], conv_vec)
            load(ctaps[:, :, :, :], conv_taps)
            load(sub_g[:, :], subln)
            load(lam_rows[:, :, :, :], lam_in.partition_broadcast(P))

            def source(p, i, s):
                if p.name == "up":
                    return w_up[p.layer, p.half, p.group * FG + i, s]
                if p.name == "down":
                    return w_down[p.layer, p.half, p.group, 2 * i + s]
                return (w_in if p.name == "mix_in" else w_out)[p.layer, 2 * i + s]

            def fetch(p, i, s, wait=True):
                if wait:
                    sp.wait_ge(sems["split_lo"], 2 * i + (p.first + s - 1))
                sp.dma_start(raw[s][:, 0:p.kc, :], source(p, i, s)).then_inc(sems[raw_loaded[s]], 16)

            def stack_heads(layer):
                scored = scores_before(layer)
                per_head = diff_scores(layer) // HEADS
                for h in range(HEADS):
                    if h % 2 == 0:
                        sp.wait_ge(sems["qk_hi"], 4 * layer + h + 2)
                        sp.wait_ge(sems["qk_lo"], 4 * layer + h + 2)
                    if h == 1:
                        sp.wait_ge(sems["conv_pw"], WC * (layer + 1))
                    if h >= 2:
                        sp.wait_ge(sems["scores"], scored + (h - 1) * per_head)
                    if h == 2:
                        sp.wait_ge(sems["stacked1"], 16 * 12 * (2 * layer + 1))
                    for s in range(2):
                        c = h // 2
                        rows = slice(DIFF_DH * ((2 * h + s) % 4), DIFF_DH * ((2 * h + s) % 4) + DIFF_DH)
                        nq = TOK if layer < LAYERS - 1 else LAT
                        parts = {"q_hi": qk_hi[c][rows, 0:nq], "q_lo": qk_lo[rows, c, 0:nq],
                                 "k_hi": qk_hi[WC + c][rows, :], "k_lo": qk_lo[rows, WC + c, :]}
                        for tile, names in ((stacks[h][s], ("q_hi", "q_hi", "q_lo")), (stacks[h][2 + s], ("k_hi", "k_lo", "k_hi"))):
                            for r, name in enumerate(names):
                                src = parts[name]
                                n = nq if name[0] == "q" else TOK
                                sp.dma_start(tile[DIFF_DH * r:DIFF_DH * r + DIFF_DH, 0:n].bitcast(F32), src.bitcast(F32)).then_inc(sems[f"stacked{h % 2}"], 16)

            for p in PHASES:
                if p is PHASES[0]:
                    for s in range(2):
                        fetch(p, 0, s, wait=False)
                if p.name == "mix_out":
                    for s in range(2):
                        fetch(p, 0, s)
                    stack_heads(p.layer)
                start = 1 if p is PHASES[0] or p.name == "mix_out" else 0
                with loop(sp, start, p.pairs) as i:
                    for s in range(2):
                        fetch(p, i, s)
            for half, (a, b, _) in enumerate(halves(LAT)):
                sp.wait_ge(sems["final"], DC * (half + 1))
                sp.dma_start(out[:, :, a:b], o_final[:, :, a:b]).then_inc(sems["out_stored"], 16)
            sp.wait_ge(sems["out_stored"], 32)

        @block.gpsimd
        def _(pool):
            t = Tally(pool, sems)
            pool.memset(ones[:, :], 1.0).then_inc(sems["const_rows"], 1)
            pool.memset(eps_t[:, 0:1], EPS).then_inc(sems["const_rows"], 1)
            pool.memset(eps_t[:, 1:2], LN_EPS).then_inc(sems["const_rows"], 1)

            def fetch_mod(b, wait=True):
                if wait:
                    pool.wait_ge(sems["mod_step"], MOD_STEPS * b - MOD_STEPS * MOD_FIRST)
                pool.dma_start(mod_raw[:, :, :], w_mod[b]).then_inc(sems["mod_raw"], 16)

            ones2 = ones[:, 0:1].rearrange("p (a b) -> p a b", a=1).to_broadcast([P, 2, MOD_COLS])

            def round_mod(b):
                pool.wait_ge(sems["mod_step"], MOD_STEPS * b - MOD_STEPS * (MOD_FIRST - 1))
                pool.tensor_tensor(mod_hi[:, :, :], mod_acc[:, :, :], ones2, ALU.mult).then_inc(sems["mod_rounded"], 1)
                pool.wait_ge(sems["mod_rounded"], b - (MOD_FIRST - 1))
                pool.tensor_tensor(mod_lo[:, :, :], mod_acc[:, :, :], mod_hi[:, :, :].bitcast(F32),
                                   ALU.subtract).then_inc(sems["mod_parts"], 1)

            def mixer(layer, mods_before):
                pool.wait_ge(sems["mod_step"], MOD_STEPS * (mods_before - MOD_FIRST))
                pool.dma_start(rope_t[:, :, :], rope).then_inc(sems["rope_tables"], 16)
                pool.wait_ge(sems["norm_sum"], 2 * (2 + 3 * layer))
                pool.memset(pool_sb[:, :, :], 0.0).then_inc(sems["blocks_zero"], 1)
                t.wait("blocks_zero")
                for g in range(4):
                    a = DH * (g % 2)
                    pool.dma_start(pool_sb[a:a + DH, g // 2, a:a + DH], pool_w[layer, g]).then_inc(sems["mixer_weights"], 16)
                pool.dma_start(pw_sb[:, :, :], conv_pw[layer]).then_inc(sems["mixer_weights"], 16)
                pool.wait_ge(sems["y_lo"], y_count(layer, 1))
                for c, buf in enumerate((act_buf, hid_buf)):
                    pool.dma_start(buf[:, :], pool_inv[:, c, :]).then_inc(sems["pool_tables"], 16)
                t.wait("pool_tables", 32)

                def step(instruction):
                    instruction.then_inc(sems["pool_step"], 1)
                    t.wait("pool_step")

                parts = ((0, LAT, POOL_LAT0), (LAT, TOK, POOL_CTX0))[:1 if layer == LAYERS - 1 else 2]
                n_out = parts[-1][1]
                for c, inv in enumerate((act_buf, hid_buf)):
                    pool.wait_ge(sems[slot_free[c]], unit_pairs(layer, "mix_in") + POOL_U // 2 + 1)
                    u = z[:, POOL_U + c, :]
                    step(pool.memset(pool_a[:, :], 0.0))
                    step(pool.memset(pool_b[:, :], 0.0))
                    for a, b, at in parts:
                        step(pool.tensor_copy(pool_a[:, at:at + b - a], u[:, a:b]))
                    n = parts[-1][2] + parts[-1][1] - parts[-1][0] + PPAD
                    step(pool.tensor_tensor(pool_b[:, 1:n], pool_a[:, 0:n - 1], pool_a[:, 1:n], ALU.add))
                    if c == 0:
                        step(pool.tensor_tensor(pool_a[DH:P, 1:n - 1], pool_b[DH:P, 0:n - 2], pool_b[DH:P, 2:n], ALU.add))
                        halves = (pool_b, pool_a)
                    else:
                        step(pool.tensor_tensor(pool_a[:, 1:n - 1], pool_b[:, 0:n - 2], pool_b[:, 2:n], ALU.add))
                        step(pool.tensor_tensor(pool_b[:, 2:n - 2], pool_a[:, 0:n - 4], pool_a[:, 4:n], ALU.add))
                        step(pool.tensor_tensor(pool_a[DH:P, 4:n - 4], pool_b[DH:P, 0:n - 8], pool_b[DH:P, 8:n], ALU.add))
                        halves = (pool_b, pool_a)
                    for g, buf in enumerate(halves):
                        rows = slice(DH * g, DH * g + DH)
                        for a, b, at in parts:
                            step(pool.tensor_tensor(inv[rows, a:b], buf[rows, at:at + b - a], inv[rows, a:b], ALU.mult))
                    pool.tensor_tensor(u[:, 0:n_out], inv[:, 0:n_out], u[:, 0:n_out], ALU.subtract).then_inc(sems["pool_d"], 1)

                pool.wait_ge(sems["conv_acc"], (layer + 1) * WC * CONV_K)
                t.n["pool_d"] = WC * layer
                t.wait("pool_d", WC)

                def load_band(h):
                    for s in range(2):
                        first = RPB_PAD + ((layer * HEADS + h) * RPB_R + 1 - s) * RPB_C + RPB_C // 2 - (GRID_W - 1)
                        src = bass.AP(rpb.tensor, first, [[1, GRID_W], [RPB_C, RPB_R - 1], [1, GRID_W]])
                        pool.dma_start(bands[h][GRID_W * s:GRID_W * s + GRID_W, :, :], src).then_inc(sems["band_raw"], 16)

                def mask_band(h, row):
                    if row == 1:
                        t.wait("band_step")
                    m = mask[:, row:row + 1, :].to_broadcast([P, RPB_R - 1, GRID_W])
                    pool.tensor_tensor(bands[h][:, :, :], bands[h][:, :, :], m,
                                       (ALU.mult, ALU.add)[row]).then_inc(sems[("band_step", "band_ready")[row]], 1)

                for h in range(HEADS - 1):
                    load_band(h)
                t.wait("band_raw", 16 * 2 * (HEADS - 1))
                for h in range(HEADS - 1):
                    for row in range(2):
                        mask_band(h, row)
                for n_split, c in enumerate((0, 2, 1, 3)):
                    pool.wait_ge(sems["qk_hi"], 4 * layer + n_split + 1)
                    w = TOK if c >= WC or layer < LAYERS - 1 else LAT
                    pool.tensor_tensor(qk_lo[:, c, 0:w], z[:, DIFF_Q + c, 0:w], qk_hi[c][:, 0:w].bitcast(F32),
                                       ALU.subtract).then_inc(sems["qk_lo"], 1)
                na_step = 0
                for k, (kind, h, tiles, ctx, last) in enumerate(attention_steps(layer < LAYERS - 1)):
                    if kind == "na":
                        if na_step == 0:
                            pool.wait_ge(sems["scores"], scores_before(layer) + diff_scores(layer))
                            load_band(HEADS - 1)
                        elif na_step == 2:
                            t.wait("band_raw", 16 * 2)
                            mask_band(HEADS - 1, 0)
                        elif na_step == 3:
                            mask_band(HEADS - 1, 1)
                        na_step += 1
                    keys = slice(LAT, TOK) if ctx else slice(0, TOK)
                    e = (k % 2) * 2 + 1
                    t.wait("sums_inverted")
                    factor = nrsum[:, e - 1:e] if kind == "diff" else rsum[:, e:e + 1]
                    factor = factor.to_broadcast([P, keys.stop - keys.start])
                    pool.tensor_tensor(e_sb[:, e, keys], e_sb[:, e, keys], factor, ALU.mult).then_inc(sems["half_scaled"], 1)

            def normalize(tokens):
                a, b, _ = halves(tokens)[1]
                norms[0] += 1
                pool.wait_ge(sems["rstd"], 2 * norms[0])
                for m in range(DC):
                    if m >= 2:
                        pool.wait_ge(sems["affine"], 2 * DC * (norms[0] - 1) + DC + m - 1)
                    pool.tensor_tensor(sq[m % 2][:, a:b], x[:, m, a:b], rstd[:, a:b], ALU.mult).then_inc(sems["normed1"], 1)

            norms = [0]
            fetch_mod(MOD_FIRST, wait=False)
            normalize(TOK)
            fetched = MOD_FIRST + 1
            for n_phase, (p, (b0, n)) in enumerate(zip(PHASES, MOD_PLAN)):
                if p.name == "mix_in":
                    mixer(p.layer, b0)
                    pool.wait_ge(sems["rope_done"], p.layer + 1)
                if n and b0 < fetched:
                    round_mod(b0)
                    b0, n = b0 + 1, n - 1
                if n:
                    with loop(pool, b0, b0 + n) as b:
                        fetch_mod(b)
                        round_mod(b)
                if p.name == "mix_out" or p.name == "down" and p.group == 1:
                    if n_phase + 1 < len(PHASES) and MOD_PLAN[n_phase + 1][1]:
                        fetch_mod(MOD_PLAN[n_phase + 1][0])
                        fetched = MOD_PLAN[n_phase + 1][0] + 1
                    if n_phase + 1 < len(PHASES):
                        normalize(p.tokens)

        @block.scalar
        def _(act):
            t = Tally(act, sems)

            def split_hi(p, i, s, ahead):
                kc = ahead
                if not kc:
                    return
                act.wait_ge(sems["unit_done"], 2 * i + (p.first + s + 1))
                act.wait_ge(sems[raw_loaded[s]], 16 * i + 16 * (p.first // 2 + 2))
                act.activation(w_hi[s][:, 0:kc, :], raw[s][:, 0:kc, :], ACT.Copy).then_inc(sems["split_hi"], 1)

            def square(src, s, tokens, wait_buffer):
                if wait_buffer is not None:
                    act.wait_ge(sems["sum_squares"], wait_buffer)
                act.activation(sq[s][:, 0:tokens], src, ACT.Square).then_inc(sems["square"], 1)

            def root(tokens, half):
                a, b, _ = halves(tokens)[half]
                t.wait("norm_sum")
                act.activation(rstd[:, a:b], turn[:, LAT * half:LAT * half + b - a], ACT.Sqrt, bias=eps_t[:, 0:1], scale=1.0 / D).then_inc(sems["norm_sqrt"], 1)

            def make_y(layer, norm, tokens, after=None):
                t.wait("scale_ready")
                shift = mod_chunk(layer, 3 * norm)
                for half, (a, b, k) in enumerate(halves(tokens)):
                    for m in range(DC):
                        buf = (act_buf, hid_buf)[m % 2]
                        t.wait(f"normed{half}")
                        if m >= 2:
                            act.wait_ge(sems["y_lo"], y_made[0] + half * DC + m - 1)
                        act.activation(buf[:, a:b], sq[m % 2][:, a:b], ACT.Identity,
                                       bias=mod_vec[:, k, shift + m:shift + m + 1],
                                       scale=scale1[:, k, m:m + 1]).then_inc(sems["affine"], 1)
                        t.wait("affine")
                        if half == 0:
                            act.activation(y_hi[:, m, a:b], buf[:, a:b], ACT.Copy).then_inc(sems["y_hi"], 1)
                            if after:
                                after(m)
                y_made[0] += 2 * DC

            y_made = [0]
            ssq_made = [0]
            hidden = [0]

            for b in range(MOD_FIRST):
                act.dma_start(mod_start[:, b, :, :], w_mod[b]).then_inc(sems[f"mod_first{b}"], 16)
            t.wait("cond", 16)
            act.activation(cact[:, :, :], cvec[:, :, :], ACT.Silu).then_inc(sems["cond_silu"], 1)
            t.wait("x_in", 16)
            t.wait("const_rows", 3)
            for m in range(DC):
                square(x[:, m, :], m % 2, TOK, m - 1 if m >= 2 else None)
            ssq_made[0] += DC - 1
            root(TOK, 0)
            root(TOK, 1)
            t.wait("inputs", 16 * 11)
            for s in range(2):
                act.wait_ge(sems[raw_loaded[s]], 16)
                act.activation(w_hi[s][:, 0:DC, :], raw[s][:, 0:DC, :], ACT.Copy).then_inc(sems["split_hi"], 1)
            make_y(0, 0, TOK)

            def up(p, mods):
                n = p.tokens
                h0 = hidden[0]
                pair0 = p.first // 2

                def body(i, ahead):
                    act.wait_ge(sems["unit_done"], 2 * i + (p.first + 1))
                    act.activation(act_buf[:, 0:n], slot[0][:, 0:n], ACT.Silu).then_inc(sems["slot_free0"], 1)
                    split_hi(p, i, 0, ahead)
                    split_hi(p, i, 1, ahead)
                    act.wait_ge(sems["slot_free1"], i + (pair0 + 1))
                    act.activation(h_hi[:, i, 0:n], hid_buf[:, 0:n], ACT.Copy).then_inc(sems["hidden_hi"], 1)

                act.wait_ge(sems["y_lo"], y_made[0])
                for a, b, _ in segments(p, mods):
                    if b - a == 1:
                        body(a, p.kc if b < p.pairs else p.next_kc)
                    else:
                        with loop(act, a, b) as i:
                            body(i, p.kc)
                hidden[0] += p.pairs

            def down(p, mods, squares):
                n = p.tokens
                pair0 = p.first // 2
                s0 = ssq_made[0]

                def body(i, ahead):
                    for s in range(2):
                        split_hi(p, i, s, ahead)
                        if squares:
                            act.wait_ge(sems[slot_free[s]], i + (pair0 + 1))
                            start = isinstance(i, int) and i == 0
                            square(x[:, 2 * i + s, 0:n], s, n, None if start else 2 * i + (s0 + s - 1))

                for a, b, _ in segments(p, mods):
                    if squares and b == p.pairs:
                        continue
                    if b - a == 1:
                        body(a, p.kc if b < p.pairs else p.next_kc)
                    else:
                        with loop(act, a, b) as i:
                            body(i, p.kc)

            def down_last(p, norm):
                i, s0 = p.pairs - 1, ssq_made[0]
                (a0, b0, _), (a1, b1, _) = halves(p.tokens)
                for s in range(2):
                    t.wait("updated")
                    act.wait_ge(sems["sum_squares"], s0 + 2 * i + s - 1)
                    act.activation(sq[s][:, a0:b0], x[:, 2 * i + s, a0:b0], ACT.Square).then_inc(sems["square"], 1)
                root(p.tokens, 0)

                def second_square(s):
                    act.wait_ge(sems[slot_free[s]], p.first // 2 + i + 1)
                    act.activation(sq[s][:, a1:b1], x[:, 2 * i + s, a1:b1], ACT.Square).then_inc(sems["square"], 1)

                split_hi(p, i, 0, p.next_kc)
                if norm is None:
                    second_square(0)
                    second_square(1)
                    root(p.tokens, 1)
                    return

                def after(m):
                    if m < 2:
                        second_square(m)
                    if m == 2:
                        split_hi(p, i, 1, p.next_kc)
                    if m == 4:
                        root(p.tokens, 1)

                make_y(*norm, p.tokens, after)
                ssq_made[0] += DC

            def mix_in(p):
                def body(i, tokens, func, ahead):
                    for s in range(2):
                        act.wait_ge(sems["unit_done"], 2 * i + (p.first + s + 1))
                        act.activation(z[:, 2 * i + s, 0:tokens], slot[s][:, 0:tokens], func).then_inc(sems[slot_free[s]], 1)
                        split_hi(p, i, s, ahead)

                for a, b, tokens in z_segments(p.layer):
                    func = ACT.Sigmoid if a == CONV_G // 2 else ACT.Copy
                    if b - a == 1:
                        body(a, tokens, func, p.kc if b < p.pairs else p.next_kc)
                    else:
                        with loop(act, a, b) as i:
                            body(i, tokens, func, p.kc)

            def mixer(layer):
                with_ctx = layer < LAYERS - 1
                n = TOK if with_ctx else LAT
                t.wait("lam_in")
                act.activation(lam[:, 2:4], lam[:, 0:2], ACT.Exp).then_inc(sems["lam_exp"], 1)
                def copy_values(k):
                    act.wait_ge(sems["v_turned"], layer * (TOK // P) + k + 1)
                    act.activation(v_sb[:, k, :], turn[:, 0:512], ACT.Copy).then_inc(sems["v_ready0"], 1)

                def qk_hi_part(c):
                    w = TOK if c >= WC else n
                    act.activation(qk_hi[c][:, 0:w], z[:, DIFF_Q + c, 0:w], ACT.Copy).then_inc(sems["qk_hi"], 1)

                act.wait_ge(sems["rope_done"], layer + 1)
                qk_hi_part(0)
                qk_hi_part(2)
                copy_values(0)
                copy_values(2)
                act.wait_ge(sems["pool_d"], WC * (layer + 1))
                for c in range(WC):
                    t.wait("conv_cent")
                    act.activation((act_buf, hid_buf)[c][:, 0:n], sq[c][:, 0:n], ACT.Square).then_inc(sems["conv_sq"], 1)
                copy_values(4)
                act.wait_ge(sems["v_turned"], (layer + 1) * (TOK // P))
                qk_hi_part(1)
                qk_hi_part(3)
                t.wait("conv_var")
                act.activation(rstd[:, 0:n], outs[:, 0:n], ACT.Sqrt, bias=eps_t[:, 1:2], scale=1.0 / W).then_inc(sems["conv_sqrt"], 1)
                for c in range(WC):
                    t.wait("pool_mm")
                    act.activation(z[:, POOL_U + c, 0:n], slot[c][:, 0:n], ACT.Identity,
                                   scale=cvecs[:, layer, 4, c:c + 1]).then_inc(sems["pool_out"], 1)
                for c in range(WC):
                    t.wait("conv_norm")
                    act.activation(sq[c][:, 0:n], sq[c][:, 0:n], ACT.Silu, bias=cvecs[:, layer, 2, c:c + 1],
                                   scale=cvecs[:, layer, 1, c:c + 1]).then_inc(sems["conv_act"], 1)

                steps = attention_steps(with_ctx)
                tiles0 = turned_before(layer)
                step_tiles = []
                head = [0]
                copy_at, copy_chunk, norm_at = None, None, None
                spread = value_steps(with_ctx)

                def copy_out(c):
                    t.wait("pv", 2)
                    act.activation(mixed[c][:, 0:n], outs[:, 0:n], ACT.Copy).then_inc(sems["head_out"], 1)

                def exponentials(k, s):
                    kind, h, tiles, ctx, _ = steps[k]
                    keys = slice(LAT, TOK) if ctx else slice(0, TOK)
                    t.wait("neg_max")
                    if k >= 2:
                        before = step_tiles[k - 3] if k >= 3 else tiles0
                        act.wait_ge(sems["turned"], before + min(s + 1, len(steps[k - 2][2])))
                    e = (k % 2) * 2 + s
                    act.activation(e_sb[:, e, keys], slot[s][:, keys], ACT.Exp, bias=nmax[:, e:e + 1],
                                   accum_out=esum[:, e:e + 1]).then_inc(sems["exp"], 1)

                def copy_probs(step, q):
                    kind, h, tiles, ctx, last = step
                    hn = head[0] % 2
                    t.wait("turned")
                    if head[0] >= 2 or layer:
                        act.wait_ge(sems["pv"], layer * 2 * HEADS + head[0] - 1)
                    if ctx:
                        act.activation(ctx_probs[hn][:, :, P * q:P * q + P],
                                       turn[:, 0:2 * P].rearrange("p (k q) -> p k q", q=P), ACT.Copy).then_inc(sems["probs_t"], 1)
                    else:
                        act.activation(probs_t[hn][:, :, P * q:P * q + P],
                                       turn[:, 0:TOK].rearrange("p (k q) -> p k q", q=P), ACT.Copy).then_inc(sems["probs_t"], 1)

                for k in range(len(steps) + 3):
                    turned = steps[k - 2] if 2 <= k < len(steps) + 2 else None
                    for s in range(2):
                        if k < len(steps):
                            exponentials(k, s)
                        if turned and s < len(turned[2]):
                            copy_probs(turned, turned[2][s])
                    if k < len(steps):
                        step_tiles.append((step_tiles[-1] if step_tiles else tiles0) + len(steps[k][2]))
                    if k == 0:
                        for c in range(WC):
                            t.wait("conv_pw")
                            act.activation(z[:, 2 * c, 0:n], (turn, outs)[c][:, 0:n], ACT.Identity,
                                           bias=cvecs[:, layer, 3, c:c + 1]).then_inc(sems["conv_out"], 1)
                    if k == norm_at:
                        t.wait("head_sum")
                        act.activation(hid_buf[:, 0:n], turn[:, 0:n], ACT.Sqrt, bias=eps_t[:, 0:1], scale=1.0 / DH).then_inc(sems["head_sqrt"], 1)
                    if k == copy_at and copy_chunk < DC - 1:
                        copy_out(copy_chunk)
                        if copy_chunk < 6:
                            t.wait("head_out")
                            act.activation(act_buf[:, 0:n], mixed[copy_chunk][:, 0:n], ACT.Square).then_inc(sems["head_sq"], 1)
                            norm_at = k + 1
                        else:
                            t.skip("head_out")
                    if turned and turned[4]:
                        head[0] += 1
                        if turned[1] % 2:
                            copy_at, copy_chunk = k + spread[head[0] - 1], (4 if turned[0] == "diff" else 6) + turned[1] // 2
                t.wait("head_norm", 2 * n // CTX)
                t.wait("pool_out", WC)
                t.wait("conv_out", WC)
                act.wait_ge(sems["pv"], (layer + 1) * 2 * HEADS - 1)
                for m in range(DC):
                    if m == DC // 2:
                        copy_out(copy_chunk)
                        t.wait("head_out")
                    act.activation(y_hi[:, m, 0:n], mixed[m][:, 0:n], ACT.Copy).then_inc(sems["y_hi"], 1)
                y_made[0] += DC

            for p, (b0, mods) in zip(PHASES, MOD_PLAN):
                if p.name == "up":
                    up(p, mods)
                elif p.name == "down":
                    down(p, mods, squares=p.group == 1)
                    if p.group == 1:
                        down_last(p, next_norm(p))
                elif p.name == "mix_in":
                    mix_in(p)
                    mixer(p.layer)
                else:
                    down(p, 0, squares=True)
                    down_last(p, next_norm(p))

        @block.vector
        def _(dve):
            t = Tally(dve, sems)
            y_made, ssq_made, squares_made, hidden = [0], [0], [0], [0]

            def split_lo(p, i, s, ahead):
                kc = ahead
                if not kc:
                    return
                dve.wait_ge(sems["split_hi"], 2 * i + (p.first + s + 3))
                dve.tensor_tensor(w_lo[s][:, 0:kc, :], raw[s][:, 0:kc, :], w_hi[s][:, 0:kc, :].bitcast(F32),
                                  ALU.subtract).then_inc(sems["split_lo"], 1)

            def mod_block(b):
                dve.wait_ge(sems["mod_raw"], 16 * b - 16 * (MOD_FIRST - 1))
                if not isinstance(b, int) or b > MOD_FIRST:
                    dve.wait_ge(sems["mod_sum"], b - (MOD_FIRST - 1))
                for k in range(DC):
                    for tok in range(2):
                        c = cact[:, tok, k:k + 1]
                        if k:
                            dve.wait_ge(sems["mod_step"], MOD_STEPS * b + (2 * k + tok - 1 - MOD_STEPS * MOD_FIRST))
                        if k == 0:
                            ins = dve.tensor_scalar(mod_acc[:, tok, :], mod_raw[:, k, :], c, None, ALU.mult)
                        else:
                            ins = dve.scalar_tensor_tensor(mod_acc[:, tok, :], mod_raw[:, k, :], c, mod_acc[:, tok, :],
                                                           ALU.mult, ALU.add)
                        ins.then_inc(sems["mod_step"], 1)

            def mod_finish(b):
                dve.wait_ge(sems["mod_sum"], b - (MOD_FIRST - 2))
                dve.tensor_tensor(mod_diag[:, :, :], mod_ps.rearrange("p (n q) -> p n q", q=P),
                                  ident[:, :].rearrange("p (a q) -> p a q", a=1).to_broadcast([P, 4, P]),
                                  ALU.mult).then_inc(sems["mod_diagonal"], 1)
                dve.wait_ge(sems["mod_diagonal"], 2 * b - (2 * MOD_FIRST - 1))
                dve.tensor_reduce(mod_out[:, :], mod_diag[:, :, :], AX_X, ALU.add).then_inc(sems["mod_diagonal"], 1)
                dve.wait_ge(sems["mod_diagonal"], 2 * b - (2 * MOD_FIRST - 2))
                dve.tensor_tensor(mod_vec[:, :, bass.ds(2 * b, 2)], mod_out[:, :].rearrange("p (t c) -> p t c", t=2),
                                  mod_bias[:, :, bass.ds(2 * b, 2)].to_broadcast([P, 2, 2]),
                                  ALU.add).then_inc(sems["mod_vec"], 1)

            def add_squares(m_first, s, tokens, made):
                if m_first:
                    dve.tensor_copy(ssq[:, 0:tokens], sq[s][:, 0:tokens]).then_inc(sems["sum_squares"], 1)
                else:
                    dve.wait_ge(sems["sum_squares"], made)
                    dve.tensor_tensor(ssq[:, 0:tokens], ssq[:, 0:tokens], sq[s][:, 0:tokens], ALU.add).then_inc(sems["sum_squares"], 1)

            def invert_root(tokens, half):
                a, b, _ = halves(tokens)[half]
                t.wait("norm_sqrt")
                dve.reciprocal(rstd[:, a:b], rstd[:, a:b]).then_inc(sems["rstd"], 1)
                t.wait("rstd")

            def mods_ready(layer, i):
                dve.wait_ge(sems["mod_vec"], (mod_chunk(layer, i) + DC) // 2)

            def make_scale(layer, norm):
                mods_ready(layer, 3 * norm + 1)
                a = mod_chunk(layer, 3 * norm + 1)
                for tok in range(2):
                    ins = dve.scalar_tensor_tensor(scale1[:, tok, :], mod_vec[:, tok, a:a + DC], 1.0,
                                                   gain[:, 3 * layer + norm, :], ALU.add, ALU.mult)
                ins.then_inc(sems["scale_ready"], 1)

            def make_y(tokens, after=None):
                (a0, b0, _), (a1, b1, _) = halves(tokens)
                for m in range(DC + 1):
                    if m < DC:
                        if m >= 2:
                            t.wait("affine")
                        dve.tensor_tensor(sq[m % 2][:, a0:b0], x[:, m, a0:b0], rstd[:, a0:b0], ALU.mult).then_inc(sems["normed0"], 1)
                    if m:
                        t.wait("y_hi")
                        buf = (act_buf, hid_buf)[(m - 1) % 2]
                        dve.tensor_tensor(y_lo[:, m - 1, a0:b0], buf[:, a0:b0], y_hi[:, m - 1, a0:b0].bitcast(F32),
                                          ALU.subtract).then_inc(sems["y_lo"], 1)
                    if after:
                        after(m)
                t.skip("affine", 2)
                for m in range(DC):
                    t.wait("affine")
                    buf = (act_buf, hid_buf)[m % 2]
                    dve.tensor_copy(y_hi[:, m, a1:b1], buf[:, a1:b1]).then_inc(sems["y_hi"], 1)
                    t.wait("y_hi")
                    dve.tensor_tensor(y_lo[:, m, a1:b1], buf[:, a1:b1], y_hi[:, m, a1:b1].bitcast(F32),
                                      ALU.subtract).then_inc(sems["y_lo"], 1)
                y_made[0] += 2 * DC

            def up(p, b0, mods):
                n = p.tokens
                pair0 = p.first // 2
                h0 = hidden[0]

                def body(i, ahead, with_mod):
                    if with_mod:
                        mod_block(b0 + i)
                    split_lo(p, i, 0, ahead)
                    dve.wait_ge(sems["unit_done"], 2 * i + (p.first + 2))
                    dve.wait_ge(sems["slot_free0"], i + (pair0 + 1))
                    if h0 or not isinstance(i, int) or i:
                        dve.wait_ge(sems["hidden_lo"], i + h0)
                    else:
                        dve.wait_ge(sems["y_lo"], y_made[0])
                    dve.tensor_tensor(hid_buf[:, 0:n], act_buf[:, 0:n], slot[1][:, 0:n], ALU.mult).then_inc(sems["slot_free1"], 1)
                    split_lo(p, i, 1, ahead)
                    dve.wait_ge(sems["hidden_hi"], i + (h0 + 1))
                    dve.tensor_tensor(h_lo[:, i, 0:n], hid_buf[:, 0:n], h_hi[:, i, 0:n].bitcast(F32), ALU.subtract).then_inc(sems["hidden_lo"], 1)
                    if with_mod:
                        mod_finish(b0 + i)

                for a, b, with_mod in segments(p, mods):
                    if b - a == 1:
                        body(a, p.kc if b < p.pairs else p.next_kc, with_mod)
                    else:
                        with loop(dve, a, b) as i:
                            body(i, p.kc, with_mod)
                hidden[0] += p.pairs

            def down(p, b0, mods, squares, gate):
                n = p.tokens
                s0, q0 = ssq_made[0], squares_made[0]
                mods_ready(p.layer, gate)
                a = mod_chunk(p.layer, gate)
                if p.group == 0:
                    dve.tensor_scalar(gates[:, :, :], mod_vec[:, :, a:a + DC], 1.0 if p.name == "mix_out" else 0.5, None,
                                      ALU.mult).then_inc(sems["gates_ready"], 1)
                    t.wait("gates_ready")

                def body(i, ahead, with_mod, first):
                    if with_mod:
                        mod_block(b0 + i)
                    for s in range(2):
                        dve.wait_ge(sems["unit_done"], 2 * i + (p.first + s + 1))
                        for k, (lo, hi) in kinds(n):
                            ins = dve.scalar_tensor_tensor(x[:, 2 * i + s, lo:hi], slot[s][:, lo:hi],
                                                           gates[:, k, bass.ds(2 * i + s, 1)], x[:, 2 * i + s, lo:hi],
                                                           ALU.mult, ALU.add)
                        ins.then_inc(sems[slot_free[s]], 1)
                        split_lo(p, i, s, ahead)
                        if squares:
                            dve.wait_ge(sems["square"], 2 * i + (q0 + s + 1))
                            add_squares(first and s == 0, s, n, 2 * i + (s0 + s))
                    if with_mod:
                        mod_finish(b0 + i)

                for lo_i, hi_i, with_mod in segments(p, mods):
                    if squares and hi_i == p.pairs:
                        continue
                    if hi_i - lo_i == 1:
                        body(lo_i, p.kc if hi_i < p.pairs else p.next_kc, with_mod, lo_i == 0)
                    else:
                        with loop(dve, lo_i, hi_i) as i:
                            body(i, p.kc, with_mod, False)

            def down_last(p, b0, mods, norm):
                i, s0, q0 = p.pairs - 1, ssq_made[0], squares_made[0]
                parts = halves(p.tokens)
                with_mod = mods >= p.pairs
                if with_mod:
                    mod_block(b0 + i)

                def update(s, half):
                    lo, hi, k = parts[half]
                    m = 2 * i + s
                    at = LAT * half
                    return dve.scalar_tensor_tensor(x[:, m, lo:hi], slot[s][:, at:at + hi - lo], gates[:, k, m:m + 1], x[:, m, lo:hi],
                                                    ALU.mult, ALU.add)

                def add_square(half):
                    lo, hi, _ = parts[half]
                    dve.wait_ge(sems["square"], q0 + 2 * i + 1 + 2 * half)
                    dve.wait_ge(sems["sum_squares"], s0 + 2 * i + half)
                    dve.tensor_tensor(ssq[:, lo:hi], ssq[:, lo:hi], sq[0][:, lo:hi], ALU.add).then_inc(sems["sum_squares"], 1)

                def second_update(s):
                    dve.wait_ge(sems["unit_done"], 2 * i + p.first + s + 1)
                    update(s, 1).then_inc(sems[slot_free[s]], 1)

                for s in range(2):
                    t.wait("early_done")
                    update(s, 0).then_inc(sems["updated"], 1)
                add_square(0)
                if with_mod:
                    mod_finish(b0 + i)
                if norm:
                    make_scale(*norm)
                invert_root(p.tokens, 0)
                ssq_made[0] += DC
                squares_made[0] += DC + 2
                if norm is None:
                    second_update(0)
                    second_update(1)
                    add_square(1)
                    return

                def after(m):
                    if m == 0:
                        second_update(0)
                        split_lo(p, i, 0, p.next_kc)
                    if m == 1:
                        second_update(1)
                    if m == 2:
                        add_square(1)
                    if m == 3:
                        split_lo(p, i, 1, p.next_kc)
                    if m == 6:
                        invert_root(p.tokens, 1)

                make_y(p.tokens, after)

            def mix_in(p):
                layer = p.layer
                t.n["zeros"] = layer
                taps = [0]
                with_ctx = layer < LAYERS - 1
                conv_out = CONV_OUT if with_ctx else LAT

                def convolve(n):
                    for _ in range(n):
                        if taps[0] == WC * CONV_K:
                            return
                        k, c = divmod(taps[0], WC)
                        src = conv_u[:, c, k:k + conv_out]
                        w = ctaps[:, layer, c, k:k + 1]
                        if k == 0:
                            ins = dve.tensor_scalar(conv_acc[c][:, 0:conv_out], src, w, cvecs[:, layer, 0, c:c + 1], ALU.mult, ALU.add)
                        else:
                            dve.wait_ge(sems["conv_acc"], layer * WC * CONV_K + taps[0] - 1)
                            ins = dve.scalar_tensor_tensor(conv_acc[c][:, 0:conv_out], src, w, conv_acc[c][:, 0:conv_out], ALU.mult, ALU.add)
                        ins.then_inc(sems["conv_acc"], 1)
                        taps[0] += 1

                def rope(chunk, table):
                    half = DIFF_DH // 4
                    part = z[:, chunk, 0:LAT]
                    dve.stream_shuffle(sq[0][:, 0:LAT], part, [d ^ half for d in range(DIFF_DH)]).then_inc(sems["rope_step"], 1)
                    dve.tensor_tensor(sq[1][:, 0:LAT], part, rope_t[:, table, :], ALU.mult).then_inc(sems["rope_step"], 1)
                    t.wait("rope_step", 2)
                    dve.tensor_tensor(sq[0][:, 0:LAT], sq[0][:, 0:LAT], rope_t[:, table + 1, :], ALU.mult).then_inc(sems["rope_step"], 1)
                    t.wait("rope_step")
                    dve.tensor_tensor(part, sq[1][:, 0:LAT], sq[0][:, 0:LAT], ALU.add).then_inc(sems["rope_step"], 1)
                    t.wait("rope_step")

                def copied(u):
                    dve.wait_ge(sems[slot_free[u % 2]], p.first // 2 + u // 2 + 1)

                dve.memset(conv_u[:, :, :], 0.0).then_inc(sems["zeros"], 1)
                t.wait("zeros")
                for u in range(Z_UNITS):
                    split_lo(p, u // 2, u % 2, p.kc if u < Z_UNITS - 2 else p.next_kc)
                    if u == 3:
                        copied(2)
                        copied(3)
                        for c in range(WC):
                            for kind, (a, b) in kinds(TOK if with_ctx else LAT):
                                at = a + HALO * (kind + 1)
                                dve.tensor_tensor(conv_u[:, c, at:at + b - a], z[:, CONV_A + c, a:b],
                                                  z[:, CONV_G + c, a:b], ALU.mult).then_inc(sems["conv_u"], 1)
                        t.wait("conv_u", WC * (1 + with_ctx))
                    if u >= 3:
                        convolve(6)
                    if u == 15:
                        t.wait("rope_tables", 16)
                        copied(DIFF_K)
                        copied(DIFF_K + 1)
                        for c in range(WC):
                            rope(DIFF_Q + c, 0)
                            if with_ctx:
                                dve.tensor_scalar(z[:, DIFF_Q + c, LAT:TOK], z[:, DIFF_Q + c, LAT:TOK], DIFF_DH ** -0.5, None,
                                                  ALU.mult).then_inc(sems["rope_step"], 1)
                                t.wait("rope_step")
                    if u == 16:
                        for c in range(WC):
                            rope(DIFF_K + c, 2)
                    if u == 17:
                        copied(NA_Q)
                        copied(NA_Q + 1)
                        for c in range(WC):
                            nq = TOK if with_ctx else LAT
                            ins = dve.tensor_scalar(z[:, NA_Q + c, 0:nq], z[:, NA_Q + c, 0:nq], DH ** -0.5, None, ALU.mult)
                        ins.then_inc(sems["rope_done"], 1)

            def mixer(layer):
                with_ctx = layer < LAYERS - 1
                n = TOK if with_ctx else LAT
                for k in range(2):
                    dve.tensor_tensor(sq[0][:, DIFF_DH * k:DIFF_DH * k + DIFF_DH], lam_rows[:, layer, 2 * k, :],
                                      lam_rows[:, layer, 2 * k + 1, :], ALU.mult).then_inc(sems["lam_step"], 1)
                t.wait("lam_step", 2)
                dve.tensor_reduce(lam[:, 0:2], sq[0][:, 0:2 * DIFF_DH].rearrange("p (a b) -> p a b", a=2), AX_X,
                                  ALU.add).then_inc(sems["lam_in"], 1)
                t.wait("lam_exp")
                dve.tensor_tensor(lam[:, 4:5], lam[:, 3:4], lam[:, 2:3], ALU.subtract).then_inc(sems["lam_step"], 1)
                t.wait("lam_step")
                dve.tensor_scalar(lam[:, 5:6], lam[:, 4:5], -lam_init(layer), None, ALU.add).then_inc(sems["lam_step"], 1)
                dve.tensor_scalar(lam[:, 6:7], sub_g[:, layer:layer + 1], 1.0 - lam_init(layer), None, ALU.mult).then_inc(sems["lam_step"], 1)
                t.wait("lam_step", 2)

                def copy_values(k):
                    dve.wait_ge(sems["v_turned"], layer * (TOK // P) + k + 1)
                    dve.tensor_copy(v_sb[:, k, :], turn[:, 512:1024]).then_inc(sems["v_ready1"], 1)

                copy_values(1)
                t.wait("conv_mean")
                for c in range(WC):
                    for (a, b), at in zip(spans(n), (CONV_LAT, CONV_CTX)):
                        ins = dve.scalar_tensor_tensor(sq[c][:, a:b], outs[:, a:b], -1.0 / W, conv_acc[c][:, at], ALU.mult, ALU.add)
                    ins.then_inc(sems["conv_cent"], 1)
                copy_values(3)
                copy_values(5)
                t.wait("conv_sqrt")
                dve.reciprocal(rstd[:, 0:n], rstd[:, 0:n]).then_inc(sems["conv_rstd"], 1)
                t.wait("conv_rstd")
                for c in range(WC):
                    dve.tensor_tensor(sq[c][:, 0:n], sq[c][:, 0:n], rstd[:, 0:n], ALU.mult).then_inc(sems["conv_norm"], 1)

                steps = attention_steps(with_ctx)
                norm_due = norm_at = None
                spread = value_steps(with_ctx)

                def maxima(k, s):
                    kind, h, tiles, ctx, _ = steps[k]
                    keys = slice(LAT, TOK) if ctx else slice(0, TOK)
                    e = (k % 2) * 2 + s
                    t.wait("scores")
                    dve.tensor_reduce(nmax[:, e:e + 1], slot[s][:, keys], AX_X, ALU.max,
                                      negate=True).then_inc(sems["neg_max"], 1)

                def invert_sums(k):
                    e0 = (k % 2) * 2
                    t.wait("exp", 2)
                    if k >= 2 or layer:
                        dve.wait_ge(sems["half_scaled"], scores_before(layer) // 2 + k - 1)
                    if steps[k][0] == "diff":
                        dve.reciprocal(rsum[:, e0:e0 + 2], esum[:, e0:e0 + 2]).then_inc(sems["stat"], 1)
                        t.wait("stat")
                        dve.tensor_scalar(nrsum[:, e0:e0 + 1], rsum[:, e0 + 1:e0 + 2], lam[:, 5:6], None,
                                          ALU.mult).then_inc(sems["sums_inverted"], 1)
                        t.skip("sums_inverted")
                    else:
                        dve.reciprocal(rsum[:, e0:e0 + 2], esum[:, e0:e0 + 2]).then_inc(sems["sums_inverted"], 1)
                        t.wait("sums_inverted")

                def scale_probs(k):
                    kind, h, tiles, ctx, _ = steps[k]
                    keys = slice(LAT, TOK) if ctx else slice(0, TOK)
                    e0 = (k % 2) * 2
                    if kind == "diff":
                        dve.wait_ge(sems["half_scaled"], scores_before(layer) // 2 + k + 1)
                        ins = dve.scalar_tensor_tensor(e_sb[:, e0, keys], e_sb[:, e0, keys], rsum[:, e0:e0 + 1],
                                                       e_sb[:, e0 + 1, keys], ALU.mult, ALU.add)
                    else:
                        ins = dve.tensor_scalar(e_sb[:, e0, keys], e_sb[:, e0, keys], rsum[:, e0:e0 + 1], None, ALU.mult)
                    ins.then_inc(sems["probs"], 1)

                for k in range(len(steps) + 3):
                    if 1 <= k <= len(steps):
                        invert_sums(k - 1)
                    if k < len(steps):
                        maxima(k, 0)
                    if k < len(steps):
                        maxima(k, 1)
                    if 1 <= k <= len(steps):
                        scale_probs(k - 1)
                    if norm_at is not None and norm_at <= k < norm_at + n // CTX:
                        if k == norm_at:
                            t.wait("head_sqrt")
                        part = slice(CTX * (k - norm_at), CTX * (k - norm_at) + CTX)
                        dve.reciprocal(hid_buf[:, part], hid_buf[:, part]).then_inc(sems["head_rstd"], 1)
                        t.wait("head_rstd")
                        dve.scalar_tensor_tensor(mixed[norm_due][:, part], mixed[norm_due][:, part], lam[:, 6:7], hid_buf[:, part],
                                                 ALU.mult, ALU.mult).then_inc(sems["head_norm"], 1)
                    if 2 <= k < len(steps) + 2:
                        kind, h, tiles, ctx, last = steps[k - 2]
                        if last and kind == "diff" and h % 2:
                            norm_due, norm_at = 4 + h // 2, k + spread[h] + 2
                for m in range(DC):
                    t.wait("y_hi")
                    dve.tensor_tensor(y_lo[:, m, 0:n], mixed[m][:, 0:n], y_hi[:, m, 0:n].bitcast(F32), ALU.subtract).then_inc(sems["y_lo"], 1)
                y_made[0] += DC

            t.wait("cond_silu")

            def first_sums(blocks):
                for j in blocks:
                    dve.wait_ge(sems[f"mod_first{2 * j + 1}"], 16)
                    for k in range(DC):
                        for tok in range(2):
                            src, c = mod_start[:, 2 * j + 1, k, :], cact[:, tok, k:k + 1]
                            acc = mod_start_acc[:, j, tok, :]
                            if k == 0:
                                ins = dve.tensor_scalar(acc, src, c, None, ALU.mult)
                            else:
                                dve.wait_ge(sems["first_step"], MOD_STEPS * j + 2 * k + tok - 1)
                                ins = dve.scalar_tensor_tensor(acc, src, c, acc, ALU.mult, ALU.add)
                            ins.then_inc(sems["first_step"], 1)

            first_sums(range(1))
            dve.wait_ge(sems["x_in"], 16)
            for m in range(DC - 1):
                dve.wait_ge(sems["square"], m + 1)
                add_squares(m == 0, m % 2, TOK, m)
            ssq_made[0] += DC - 1
            squares_made[0] += DC
            first_sums(range(1, 2))
            invert_root(TOK, 0)
            invert_root(TOK, 1)
            first_sums(range(2, MOD_FIRST // 2))
            dve.wait_ge(sems["inputs"], 16 * 11)
            for s in range(2):
                dve.wait_ge(sems["split_hi"], s + 1)
                dve.tensor_tensor(w_lo[s][:, 0:DC, :], raw[s][:, 0:DC, :], w_hi[s][:, 0:DC, :].bitcast(F32), ALU.subtract).then_inc(sems["split_lo"], 1)
            dve.wait_ge(sems["mod_sum"], 1)
            for tok in range(2):
                dve.tensor_tensor(mod_vec[:, tok, 0:2 * DC], mod_start_ps[:, :, tok], mod_bias[:, 0, 0:2 * DC],
                                  ALU.add).then_inc(sems["mod_vec"], MOD_FIRST // 2)
            make_scale(0, 0)
            make_y(TOK)

            for p, (b0, mods) in zip(PHASES, MOD_PLAN):
                if p.name == "up":
                    up(p, b0 - p.after_norm, mods)
                elif p.name == "down":
                    down(p, b0, mods, squares=p.group == 1, gate=2 if p.half == 0 else 8)
                    if p.group == 1:
                        down_last(p, b0, mods, next_norm(p))
                elif p.name == "mix_in":
                    mix_in(p)
                    mixer(p.layer)
                else:
                    down(p, 0, 0, squares=True, gate=5)
                    down_last(p, 0, 0, next_norm(p))
            for half, (a, b, _) in enumerate(halves(LAT)):
                if half:
                    invert_root(LAT, 1)
                for m in range(DC):
                    dve.scalar_tensor_tensor(o_final[:, m, a:b], x[:, m, a:b], gain_f[:, m:m + 1], rstd[:, a:b],
                                             ALU.mult, ALU.mult).then_inc(sems["final"], 1)

        @block.tensor
        def _(pe):
            t = Tally(pe, sems)
            y_made, hidden, ssq_made, squares_made = [0], [0], [0], [0]

            def product(s, k, kc, rhs_hi, rhs_lo, ranges):
                for n, (w, r) in enumerate(((w_hi, rhs_hi), (w_lo, rhs_hi), (w_hi, rhs_lo))):
                    for a, b, at in ranges:
                        mm = pe.matmul(slot[s][:, at:at + b - a], w[s][:, k, :], r[:, k, a:b],
                                       start=(k == 0 and n == 0), stop=(k == kc - 1 and n == 2))
                return mm

            def mod_reduce(b):
                pe.wait_ge(sems["mod_parts"], b - (MOD_FIRST - 1))
                for part in (mod_hi, mod_lo):
                    mm = pe.matmul(mod_ps, ones_r[:, :], part[:, :, :], start=(part is mod_hi), stop=(part is mod_lo))
                mm.then_inc(sems["mod_sum"], 1)

            def norm_reduce(tokens, half):
                a, b, _ = halves(tokens)[half]
                for src, last in ((ssq, False), (sq[1], True)):
                    pe.wait_ge(sems["square" if last else "sum_squares"], (squares_made if last else ssq_made)[0])
                    mm = pe.matmul(turn[:, LAT * half:LAT * half + b - a], ones[:, :], src[:, a:b], start=not last, stop=last)
                mm.then_inc(sems["norm_sum"], 1)

            def run_last(p, b0, with_mod, rhs_hi, rhs_lo):
                i = p.pairs - 1
                (a0, c0, _), (a1, c1, _) = halves(p.tokens)
                for s in range(2):
                    pe.wait_ge(sems["split_lo"], 2 * i + p.first + s + 1)
                    pe.wait_ge(sems[slot_free[s]], p.first // 2 + i)
                    for k in range(p.kc):
                        mm = product(s, k, p.kc, rhs_hi, rhs_lo, [(a0, c0, 0)])
                    mm.then_inc(sems["early_done"], 1)
                if with_mod:
                    mod_reduce(b0 + i)
                for s in range(2):
                    for k in range(p.kc):
                        if s == 0 and k == p.kc // 3:
                            ssq_made[0] += DC - 1
                            squares_made[0] += DC
                            norm_reduce(p.tokens, 0)
                        mm = product(s, k, p.kc, rhs_hi, rhs_lo, [(a1, c1, LAT)])
                    mm.then_inc(sems["unit_done"], 1)
                ssq_made[0] += 1
                squares_made[0] += 2

            def run(p, b0, mods, rhs_hi, rhs_lo, ready, made):
                pair0 = p.first // 2

                def body(i, first, with_mod, tokens):
                    def unit_ready(s):
                        pe.wait_ge(sems["split_lo"], 2 * i + (p.first + s + 1))
                        if pair0 or not first:
                            pe.wait_ge(sems[slot_free[s]], i + pair0)

                    if first and p.after_norm:
                        parts = [h for h in halves(p.tokens) if h[1] <= tokens]
                        for half, (a, b, _) in enumerate(parts):
                            for step in range(LAG[half] + p.kc):
                                if half == 0 and step == 3 and pair0:
                                    norm_reduce(p.tokens, 1)
                                for s, k in ((0, step), (1, step - LAG[half])):
                                    if 0 <= k < p.kc:
                                        if k == 0 and half == 0:
                                            unit_ready(s)
                                        if s == 0:
                                            pe.wait_ge(sems[ready], made + half * DC + k + 1)
                                        mm = product(s, k, p.kc, rhs_hi, rhs_lo, [(a, b, a)])
                                        if k == p.kc - 1 and half == len(parts) - 1:
                                            mm.then_inc(sems["unit_done"], 1)
                        pe.wait_ge(sems[ready], made + 2 * DC)
                    else:
                        for s in range(2):
                            unit_ready(s)
                            for k in range(p.kc):
                                if first and s == 0:
                                    pe.wait_ge(sems[ready], made + k + 1)
                                mm = product(s, k, p.kc, rhs_hi, rhs_lo, [(a, b, a) for a, b in spans(tokens)])
                            mm.then_inc(sems["unit_done"], 1)
                    if with_mod:
                        mod_reduce(b0 + i)

                if p.name == "mix_in":
                    parts = [(a, b, False, tokens) for a, b, tokens in z_segments(p.layer)]
                else:
                    parts = [(a, b, with_mod, p.tokens) for a, b, with_mod in segments(p, mods)]
                for a, b, with_mod, tokens in parts:
                    if b == p.pairs and (p.name == "mix_out" or p.name == "down" and p.group == 1):
                        run_last(p, b0, with_mod, rhs_hi, rhs_lo)
                    elif b - a == 1:
                        body(a, a == 0, with_mod, tokens)
                    else:
                        with loop(pe, a, b) as i:
                            body(i, False, with_mod, tokens)

            def mixer(layer):
                with_ctx = layer < LAYERS - 1
                n = TOK if with_ctx else LAT
                pairs_done = unit_pairs(layer, "mix_in") + Z_UNITS // 2
                for s in range(2):
                    pe.wait_ge(sems[slot_free[s]], pairs_done)
                for k in range(TOK // P):
                    if k >= 2:
                        t.wait(("v_ready0", "v_ready1")[k % 2])
                    for c in range(2 * WC):
                        src = z[:, (DIFF_V, DIFF_V + 1, NA_V, NA_V + 1)[c], P * k:P * k + P]
                        mm = pe.transpose(turn[:, 512 * (k % 2) + P * c:512 * (k % 2) + P * c + P], src, ident[:, :])
                    mm.then_inc(sems["v_turned"], 1)
                    if k == 1:
                        pe.wait_ge(sems["conv_acc"], (layer + 1) * WC * CONV_K)
                        for (a, b), at in zip(spans(n), (CONV_LAT, CONV_CTX)):
                            for c in range(WC):
                                mm = pe.matmul(outs[:, a:b], ones[:, :], conv_acc[c][:, at], start=(c == 0), stop=(c == WC - 1))
                        mm.then_inc(sems["conv_mean"], 1)
                t.wait("conv_sq", WC)
                for a, b in spans(n):
                    for c in range(WC):
                        mm = pe.matmul(outs[:, a:b], ones[:, :], (act_buf, hid_buf)[c][:, a:b], start=(c == 0), stop=(c == WC - 1))
                mm.then_inc(sems["conv_var"], 1)
                t.wait("mixer_weights", 16 * 5)
                for c in range(WC):
                    t.wait("pool_d")
                    for a, b in spans(n):
                        mm = pe.matmul(slot[c][:, a:b], pool_sb[:, c, :], z[:, POOL_U + c, a:b], start=True, stop=True)
                    mm.then_inc(sems["pool_mm"], 1)

                def conv_pointwise():
                    t.wait("v_ready0")
                    t.wait("v_ready1")
                    t.wait("conv_act", WC)
                    for m in range(WC):
                        for a, b in spans(n):
                            for c in range(WC):
                                mm = pe.matmul((turn, outs)[m][:, a:b], pw_sb[:, c, P * m:P * m + P], sq[c][:, a:b],
                                               start=(c == 0), stop=(c == WC - 1))
                        mm.then_inc(sems["conv_pw"], 1)

                def scores(k, s):
                    kind, h, tiles, ctx, _ = steps[k]
                    if k:
                        t.wait("exp")
                    else:
                        t.wait("pool_out")
                    if kind == "diff":
                        tile = tiles[0]
                        if tile == 0 and not ctx and s == 0:
                            pe.wait_ge(sems[f"stacked{h % 2}"], 16 * 12 * (2 * layer + h // 2 + 1))
                    else:
                        rows = slice(DH * (h % 2), DH * (h % 2) + DH)
                        q, key, tile = NA_Q + h // 2, NA_K + h // 2, tiles[s]
                    at = (LAT if ctx else 0) + P * tile
                    band = kind == "na" and not ctx
                    for a, b in spans(TOK)[1 if ctx else 0:]:
                        if kind == "diff":
                            mm = pe.matmul(slot[s][:, a:b], stacks[h][s][0:3 * DIFF_DH, at:at + P],
                                           stacks[h][2 + s][0:3 * DIFF_DH, a:b], start=True, stop=True)
                        else:
                            mm = pe.matmul(slot[s][:, a:b], z[rows, q, at:at + P], z[rows, key, a:b],
                                           start=True, stop=not (band and a == 0))
                    if band:
                        if tile == 0:
                            t.wait("band_ready")
                        j = GRID_H - 2 - 2 * tile
                        mm = pe.matmul(slot[s][:, 0:LAT], backward[:, :], bands[h][:, j:j + GRID_H, :], start=False, stop=True)
                    mm.then_inc(sems["scores"], 1)

                steps = attention_steps(with_ctx)
                pe.wait_ge(sems["rope_done"], layer + 1)
                heads, norm_at, sqrt_at, pv_from = 0, None, None, None
                spread = value_steps(with_ctx)
                tiles_turned = turned_before(layer)

                def transpose_probs(k, s):
                    kind, h, tiles, ctx, _ = steps[k]
                    if s == 0:
                        t.wait("probs")
                    else:
                        pe.wait_ge(sems["half_scaled"], scores_before(layer) // 2 + k + 1)
                    if tiles_turned:
                        pe.wait_ge(sems["probs_t"], tiles_turned)
                    e = (k % 2) * 2 + s
                    for n_key, key in enumerate(range(LAT // P if ctx else 0, TOK // P)):
                        mm = pe.transpose(turn[:, P * n_key:P * n_key + P], e_sb[:, e, P * key:P * key + P], ident[:, :])
                    mm.then_inc(sems["turned"], 1)

                for k in range(len(steps) + 3):
                    turned = steps[k - 2] if 2 <= k < len(steps) + 2 else None
                    for s in range(2):
                        if k < len(steps):
                            scores(k, s)
                        if turned and s < len(turned[2]):
                            if k == 2 and s == 0:
                                t.wait("conv_out", WC)
                            if k == sqrt_at and s == 0:
                                t.wait("head_sqrt")
                            transpose_probs(k - 2, s)
                            tiles_turned += 1
                    if k == 0:
                        conv_pointwise()
                    if k == norm_at:
                        t.wait("head_sq")
                        pe.wait_ge(sems["probs_t"], tiles_turned)
                        for a, b in spans(n):
                            mm = pe.matmul(turn[:, a:b], pairsum[:, :], act_buf[:, a:b], start=True, stop=True)
                        mm.then_inc(sems["head_sum"], 1)
                        sqrt_at = k + 1
                    if pv_from is not None and pv_from <= k < pv_from + spread[heads]:
                        kind, h = pv_head
                        if k == pv_from:
                            pe.wait_ge(sems["probs_t"], pv_tiles)
                            if h % 2 == 0 and heads:
                                t.wait("head_out")
                        rows = slice(DH * (h % 2), DH * (h % 2) + DH)
                        col = (0 if kind == "diff" else W) + DH * h
                        products = [(key, False) for key in range(TOK // P)]
                        products += [(key, True) for key in range(LAT // P, TOK // P)] * with_ctx
                        share = -(-len(products) // spread[heads])
                        for key, of_ctx in products[share * (k - pv_from):share * (k - pv_from + 1)]:
                            if of_ctx:
                                n_key = key - LAT // P
                                mm = pe.matmul(outs[rows, LAT:TOK], v_sb[:, key, col:col + DH], ctx_probs[heads % 2][:, n_key, :],
                                               start=(n_key == 0), stop=(key == TOK // P - 1))
                            else:
                                mm = pe.matmul(outs[rows, 0:LAT], v_sb[:, key, col:col + DH], probs_t[heads % 2][:, key, :],
                                               start=(key == 0), stop=(key == TOK // P - 1))
                        if k == pv_from + spread[heads] - 1:
                            mm.then_inc(sems["pv"], 1)
                            heads += 1
                            pv_from = None
                            if kind == "diff" and h % 2:
                                norm_at = k + 1
                    if turned and turned[4]:
                        pv_head, pv_tiles, pv_from = turned[0:2], tiles_turned, k + 1
                t.skip("head_out")
                t.skip("exp", 2)
                pe.wait_ge(sems["exp"], t.n["exp"])

            t.wait("cond_silu")
            for b in range(0, MOD_FIRST, 2):
                if b == MOD_FIRST // 2:
                    t.wait("const_rows", 3)
                    ssq_made[0] += DC - 1
                    squares_made[0] += DC
                    norm_reduce(TOK, 0)
                    norm_reduce(TOK, 1)
                pe.wait_ge(sems[f"mod_first{b}"], 16)
                for c in range(MOD_COLS // P):
                    for k in range(DC):
                        mm = pe.matmul(mod_start_ps[:, MOD_COLS // P * b + c, :], mod_start[:, b, k, P * c:P * c + P],
                                       cact[:, :, k], start=(k == 0), stop=(k == DC - 1))
            t.wait("inputs", 16 * 11)
            for j in range(MOD_FIRST // 2):
                pe.wait_ge(sems["first_step"], MOD_STEPS * (j + 1))
                for tok in range(2):
                    for c in range(MOD_COLS // P):
                        mm = pe.matmul(mod_start_ps[:, MOD_COLS // P * (2 * j + 1) + c, tok:tok + 1],
                                       mod_start_acc[:, j, tok, P * c:P * c + P], ones[:, 0:1], start=True, stop=True)
            mm.then_inc(sems["mod_sum"], 1)
            y_made[0] += 2 * DC

            for p, (b0, mods) in zip(PHASES, MOD_PLAN):
                if p.name in ("up", "mix_in", "mix_out"):
                    if p.name != "up" or p.group == 0:
                        made = y_made[0] - (DC if p.name == "mix_out" else 2 * DC)
                    run(p, b0 - p.after_norm, mods, y_hi, y_lo, "y_lo", made)
                    if p.name == "mix_in":
                        mixer(p.layer)
                        y_made[0] += DC
                    if p.name == "mix_out":
                        y_made[0] += 2 * DC
                    if p.name == "up":
                        hidden[0] += p.pairs
                else:
                    run(p, b0, mods, h_hi, h_lo, "hidden_lo", hidden[0] - FG)
                    if p.group == 1:
                        y_made[0] += 2 * DC
            norm_reduce(LAT, 1)



def _feature_major(a):
    a = a.reshape(a.shape[:-1] + (-1, P))
    return np.ascontiguousarray(np.moveaxis(a, -1, 0))


def _weight_units(w, groups=1):
    rows, cols = w.shape
    return w.reshape(groups, rows // groups // P, P, cols // P, P).transpose(0, 3, 2, 1, 4)


def _constants():
    pairsum = np.kron(np.eye(2), np.ones((DH, DH))).astype(np.float32)
    backward = np.kron(np.eye(2), np.eye(GRID_W)[::-1]).astype(np.float32)
    consts = np.stack([np.eye(P, dtype=np.float32), pairsum, backward])
    nf = DIFF_DH // 4
    inv = np.power(np.float32(10000.0), -np.arange(nf, dtype=np.float32) / np.float32(nf)).astype(np.float32)
    tok = np.arange(LAT)
    d = np.arange(P) % DIFF_DH
    pos = np.where((d // (2 * nf) == 0)[:, None], tok // GRID_W, tok % GRID_W).astype(np.float32)
    ang = (pos * inv[d % nf][:, None]).astype(np.float32)
    sign = np.where((d // nf) % 2 == 0, -1.0, 1.0)[:, None].astype(np.float32)
    cos, sin = np.cos(ang), np.sin(ang) * sign
    scale = np.float32(DIFF_DH ** -0.5)
    rope = np.stack([cos * scale, sin * scale, cos, sin], 1).astype(np.float32)
    inv_w = np.empty((P, WC, TOK), np.float32)
    for g, w in enumerate(POOL_WINDOWS):
        for a, n in ((0, LAT), (LAT, CTX)):
            q = np.arange(n)
            size = np.clip(q + w - w // 2, 0, n) - np.clip(q - w // 2, 0, n)
            inv_w[DH * (g % 2):DH * (g % 2) + DH, g // 2, a:a + n] = np.float32(1) / size.astype(np.float32)
    q = GRID_W - 1 - np.arange(P) % GRID_W
    c0 = np.clip(q - NA_COLS // 2, 0, GRID_W - NA_COLS)[:, None]
    k = np.arange(GRID_W)[None]
    valid = (k >= c0) & (k < c0 + NA_COLS)
    masks = np.stack([valid.astype(np.float32), np.where(valid, 0.0, -1e30).astype(np.float32)], 1)
    return consts, rope, inv_w, masks


def _layout(x, c, ctx, c_ctx, w_mod, b_mod, g_norm, ffn_in, ffn_out, w_in, w_out, pool_w, pool_scale,
            conv_dw, conv_dw_b, conv_ln_g, conv_ln_b, conv_pw, conv_pw_b, diff_lambda, diff_subln_g,
            na_rpb, g_final):
    tokens = np.concatenate([x[0], ctx[0]], 0)
    consts, rope, pool_inv, masks = _constants()
    z_cols = np.concatenate([np.arange(a, a + W) for a in Z_COLUMNS])
    up = [[_weight_units(ffn_in[l, f]).reshape(2, FC, P, DC, P).transpose(1, 0, 2, 3, 4) for f in range(2)]
          for l in range(LAYERS)]
    bias = _feature_major(b_mod.reshape(-1))
    arrays = {
        "xT": tokens.T.reshape(DC, P, TOK).transpose(1, 0, 2),
        "cond": _feature_major(np.stack([c[0], c_ctx])),
        "w_mod": w_mod.reshape(LAYERS, DC, P, MOD_BLOCKS, MOD_COLS).transpose(0, 3, 2, 1, 4).reshape(MOD_ALL, P, DC, MOD_COLS),
        "b_mod": bias[:, None],
        "gains": _feature_major(g_norm.reshape(LAYERS * 3, D)),
        "g_final": _feature_major(g_final),
        "w_up": np.stack([np.stack(u) for u in up]),
        "w_down": np.stack([np.stack([_weight_units(ffn_out[l, f], 2) for f in range(2)]) for l in range(LAYERS)]),
        "w_in": np.stack([_weight_units(w_in[l][:, z_cols])[0] for l in range(LAYERS)]),
        "w_out": np.stack([_weight_units(w_out[l])[0] for l in range(LAYERS)]),
        "pool_w": pool_w,
        "conv_pw": conv_pw.reshape(LAYERS, WC, P, W).transpose(0, 2, 1, 3),
        "conv_vec": _feature_major(np.stack([conv_dw_b, conv_ln_g, conv_ln_b, conv_pw_b, pool_scale], 1)),
        "conv_taps": conv_dw.reshape(LAYERS, CONV_K, WC, P).transpose(3, 0, 2, 1),
        "lam_in": diff_lambda,
        "subln": np.concatenate([diff_subln_g, diff_subln_g], 1).T,
        "rpb": np.pad(na_rpb.reshape(-1), RPB_PAD),
        "consts": consts, "rope": rope, "pool_inv": pool_inv, "masks": masks,
    }
    return {k: np.ascontiguousarray(v) for k, v in arrays.items()}


def kernel(**inputs):
    import concourse.bacc as bacc
    from concourse.bass_utils import run_bass_kernel_spmd

    arrays = _layout(**{k: np.asarray(v) for k, v in inputs.items()})
    nc = bacc.Bacc("TRN2", target_bir_lowering=False, num_devices=1)
    args = {k: nc.dram_tensor(f"in_{k}", a.shape, F32, kind="ExternalInput").ap() for k, a in arrays.items()}
    args["out"] = nc.dram_tensor("out_x", (P, DC, LAT), F32, kind="ExternalOutput").ap()
    trunk(nc, **args)
    r = run_bass_kernel_spmd(nc, [{f"in_{k}": a for k, a in arrays.items()}], core_ids=[0])
    out = np.asarray(r.results[0]["out_x"])
    return np.ascontiguousarray(out.transpose(1, 0, 2).reshape(D, LAT).T)[None]
```
